# Optimizing a Trainium2 kernel written in Bass

```python
import math
import jax
import jax.numpy as jnp
from jax import lax
import numpy as np
import jax, jax.numpy as jnp

D_MODEL = 2048
BATCH = 1
SEQ = 256
DEPTH = 1

ATTN_HEAD_DIM = 64
D_ATTN = D_MODEL // 2
N_ATTN_HEADS = D_ATTN // ATTN_HEAD_DIM
ROT_DIM = ATTN_HEAD_DIM // 4
ROPE_THETA = 500000.0
DILATED_PATTERNS = ((128, 1), (512, 4), (2048, 16))
ATTN_BLOCK = 128
SSM_HEAD_DIM = 64
D_SSM = D_MODEL // 2
N_SSM_HEADS = D_SSM // SSM_HEAD_DIM
SSM_GROUPS = 4
SSM_STATE = 128
CONV_WIDTH = 4
SSD_CHUNK = 128
D_CONV = D_SSM + 2 * SSM_GROUPS * SSM_STATE
DT_MIN = 1e-3
DT_MAX = 1e-1
D_MIX = D_ATTN + D_SSM
D_IN = 3 * D_ATTN + D_SSM + D_CONV + N_SSM_HEADS
N_MEM = 256
N_CROSS_HEADS = 4
CROSS_HEAD_DIM = 128
D_CROSS = N_CROSS_HEADS * CROSS_HEAD_DIM
D_FF = 4 * D_MODEL
EPS = 1e-6


def rms_norm(x, g):
    xf = x.astype(jnp.float32)
    y = xf * lax.rsqrt(jnp.mean(xf * xf, axis=-1, keepdims=True) + EPS)
    return (y * g.astype(jnp.float32)).astype(x.dtype)

def partial_rope(x, positions):
    half = ROT_DIM // 2
    inv_freq = ROPE_THETA ** (-2.0 * jnp.arange(half, dtype=jnp.float32) / ROT_DIM)
    ang = positions.astype(jnp.float32)[..., None] * inv_freq
    cos = jnp.cos(ang)[:, :, None, :]
    sin = jnp.sin(ang)[:, :, None, :]
    xf = x.astype(jnp.float32)
    x1 = xf[..., :half]
    x2 = xf[..., half:ROT_DIM]
    out = jnp.concatenate([x1 * cos - x2 * sin, x2 * cos + x1 * sin, xf[..., ROT_DIM:]], axis=-1)
    return out.astype(x.dtype)

def dilated_window_branch(q, k, v, window, dilation):
    bsz, s_len, n_h, hd = q.shape
    steps = window // dilation
    span = dilation * ATTN_BLOCK
    s_pad = -(-s_len // span) * span
    nb = s_pad // span

    def to_blocks(t):
        t = jnp.pad(t, ((0, 0), (0, s_pad - s_len), (0, 0), (0, 0)))
        return t.reshape(bsz, nb, ATTN_BLOCK, dilation, n_h, hd)

    qb, kb, vb = to_blocks(q), to_blocks(k), to_blocks(v)

    def band(t):
        prev = jnp.concatenate([jnp.zeros_like(t[:, :1]), t[:, :-1]], axis=1)
        return jnp.concatenate([prev, t], axis=2)

    kband, vband = band(kb), band(vb)
    s = jnp.einsum('bnqrhd,bnkrhd->bnrhqk', qb, kband)
    qi = jnp.arange(ATTN_BLOCK)[:, None]
    kj = jnp.arange(2 * ATTN_BLOCK)[None, :]
    dist = qi + ATTN_BLOCK - kj
    in_window = (dist >= 0) & (dist <= steps)
    has_prev = (jnp.arange(nb)[:, None, None] > 0) | (kj[None] >= ATTN_BLOCK)
    mask = in_window[None] & has_prev
    s = jnp.where(mask[None, :, None, None], s, -jnp.inf)
    m = jnp.max(s, axis=-1, keepdims=True)
    p = jnp.exp(s - m)
    denom = jnp.sum(p, axis=-1)
    lse = m[..., 0] + jnp.log(denom)
    o = jnp.einsum('bnrhqk,bnkrhd->bnqrhd', p, vband)
    o = o / jnp.transpose(denom, (0, 1, 4, 2, 3))[..., None]
    o = o.reshape(bsz, s_pad, n_h, hd)[:, :s_len]
    lse = jnp.transpose(lse, (0, 1, 4, 2, 3)).reshape(bsz, s_pad, n_h)[:, :s_len]
    return o, lse

def dilated_attention(q, k, v, positions, g_q, g_k):
    q = partial_rope(rms_norm(q, g_q), positions).astype(jnp.float32) * (ATTN_HEAD_DIM ** -0.5)
    k = partial_rope(rms_norm(k, g_k), positions).astype(jnp.float32)
    v = v.astype(jnp.float32)
    outs, lses = [], []
    for window, dilation in DILATED_PATTERNS:
        o, l = dilated_window_branch(q, k, v, window, dilation)
        outs.append(o)
        lses.append(l)
    wts = jax.nn.softmax(jnp.stack(lses, axis=0), axis=0)
    return jnp.einsum('gbsh,gbshd->bshd', wts, jnp.stack(outs, axis=0))

def ssd_chunked(x, dt, a, b_mat, c_mat):
    bsz, l_len, n_h, p_dim = x.shape
    g, n = b_mat.shape[2], b_mat.shape[3]
    hg = n_h // g
    nc = l_len // SSD_CHUNK
    q = SSD_CHUNK
    xc = x.reshape(bsz, nc, q, g, hg, p_dim)
    dtc = dt.reshape(bsz, nc, q, g, hg)
    bc = b_mat.reshape(bsz, nc, q, g, n)
    cc = c_mat.reshape(bsz, nc, q, g, n)
    a_cs = jnp.cumsum(dtc * a.reshape(g, hg), axis=2)
    seg = a_cs[:, :, :, None] - a_cs[:, :, None, :]
    causal = jnp.tril(jnp.ones((q, q), dtype=bool))[:, :, None, None]
    l_mat = jnp.exp(jnp.where(causal, seg, -jnp.inf))
    cb = jnp.einsum('bclgn,bcsgn->bclsg', cc, bc)
    w = cb[..., None] * l_mat * dtc[:, :, None]
    y_diag = jnp.einsum('bclsgh,bcsghp->bclghp', w, xc)
    decay_states = jnp.exp(a_cs[:, :, -1:] - a_cs)
    states = jnp.einsum('bcsgn,bcsgh,bcsghp->bcghpn', bc, decay_states * dtc, xc)
    chunk_decay = jnp.exp(a_cs[:, :, -1])

    def step(h, inp):
        s_c, a_c = inp
        return h * a_c[..., None, None] + s_c, h

    h0 = jnp.zeros((bsz, g, hg, p_dim, n), jnp.float32)
    _, prev = lax.scan(step, h0, (jnp.moveaxis(states, 1, 0), jnp.moveaxis(chunk_decay, 1, 0)))
    prev = jnp.moveaxis(prev, 0, 1)
    y_off = jnp.einsum('bclgn,bcghpn->bclghp', cc, prev) * jnp.exp(a_cs)[..., None]
    return (y_diag + y_off).reshape(bsz, l_len, n_h, p_dim)

def ssd_mixer(z, xbc, dt_raw, conv_w, conv_b, dt_bias, a_log, d_skip, g_out):
    bsz, l_len, _ = xbc.shape
    xbc = lax.conv_general_dilated(
        xbc, conv_w.astype(xbc.dtype)[:, None, :], window_strides=(1,),
        padding=[(CONV_WIDTH - 1, 0)], dimension_numbers=('NWC', 'WIO', 'NWC'),
        feature_group_count=D_CONV) + conv_b.astype(xbc.dtype)
    xbc = jax.nn.silu(xbc)
    xs = xbc[..., :D_SSM].astype(jnp.float32).reshape(bsz, l_len, N_SSM_HEADS, SSM_HEAD_DIM)
    b_mat = xbc[..., D_SSM:D_SSM + SSM_GROUPS * SSM_STATE].astype(jnp.float32).reshape(bsz, l_len, SSM_GROUPS, SSM_STATE)
    c_mat = xbc[..., D_SSM + SSM_GROUPS * SSM_STATE:].astype(jnp.float32).reshape(bsz, l_len, SSM_GROUPS, SSM_STATE)
    dt = jax.nn.softplus(dt_raw.astype(jnp.float32) + dt_bias.astype(jnp.float32))
    a = -jnp.exp(a_log.astype(jnp.float32))
    y = ssd_chunked(xs, dt, a, b_mat, c_mat) + d_skip.astype(jnp.float32)[:, None] * xs
    y = y.reshape(bsz, l_len, D_SSM) * jax.nn.silu(z.astype(jnp.float32))
    y = rms_norm(y.reshape(bsz, l_len, SSM_GROUPS, D_SSM // SSM_GROUPS),
                 g_out.reshape(SSM_GROUPS, D_SSM // SSM_GROUPS))
    return y.reshape(bsz, l_len, D_SSM).astype(z.dtype)

def cross_attention(h, mem_h, w_q, w_kv, w_o, g_q, g_k):
    bsz, s_len, _ = h.shape
    q = (h @ w_q).reshape(bsz, s_len, N_CROSS_HEADS, CROSS_HEAD_DIM)
    kv = (mem_h @ w_kv).reshape(bsz, -1, 2, N_CROSS_HEADS, CROSS_HEAD_DIM)
    k, v = kv[:, :, 0], kv[:, :, 1]
    q = rms_norm(q, g_q).astype(jnp.float32) * (CROSS_HEAD_DIM ** -0.5)
    k = rms_norm(k, g_k).astype(jnp.float32)
    p = jax.nn.softmax(jnp.einsum('bshd,bmhd->bhsm', q, k), axis=-1)
    o = jnp.einsum('bhsm,bmhd->bshd', p, v.astype(jnp.float32)).astype(h.dtype)
    return o.reshape(bsz, s_len, D_CROSS) @ w_o

def first_inputs(seed: int = 0) -> dict:
    key = jax.random.key(seed)
    ks = jax.random.split(key, 26)
    f32 = jnp.float32

    def nrm(k, shape, scale):
        return jax.random.normal(k, shape, f32) * scale

    def gain(k, shape):
        return 1.0 + 0.02 * jax.random.normal(k, shape, f32)

    dt0 = jnp.exp(jax.random.uniform(ks[9], (DEPTH, N_SSM_HEADS), f32, math.log(DT_MIN), math.log(DT_MAX)))
    return {
        "x": nrm(ks[0], (BATCH, SEQ, D_MODEL), 1.0),
        "mem": nrm(ks[1], (BATCH, N_MEM, D_MODEL), 1.0),
        "positions": jnp.broadcast_to(jnp.arange(SEQ, dtype=jnp.int32), (BATCH, SEQ)),
        "g_mix": gain(ks[2], (DEPTH, D_MODEL)),
        "w_in": nrm(ks[3], (DEPTH, D_MODEL, D_IN), D_MODEL ** -0.5),
        "g_q": gain(ks[4], (DEPTH, ATTN_HEAD_DIM)),
        "g_k": gain(ks[5], (DEPTH, ATTN_HEAD_DIM)),
        "g_attn_out": gain(ks[6], (DEPTH, D_ATTN)),
        "conv_w": nrm(ks[7], (DEPTH, CONV_WIDTH, D_CONV), CONV_WIDTH ** -0.5),
        "conv_b": nrm(ks[8], (DEPTH, D_CONV), 0.02),
        "dt_bias": dt0 + jnp.log(-jnp.expm1(-dt0)),
        "a_log": jnp.log(jax.random.uniform(ks[10], (DEPTH, N_SSM_HEADS), f32, 1.0, 16.0)),
        "d_skip": 1.0 + 0.1 * jax.random.normal(ks[11], (DEPTH, N_SSM_HEADS), f32),
        "g_ssm_out": gain(ks[12], (DEPTH, D_SSM)),
        "w_out": nrm(ks[13], (DEPTH, D_MIX, D_MODEL), D_MIX ** -0.5),
        "g_cross": gain(ks[14], (DEPTH, D_MODEL)),
        "g_mem": gain(ks[15], (DEPTH, D_MODEL)),
        "w_cq": nrm(ks[16], (DEPTH, D_MODEL, D_CROSS), D_MODEL ** -0.5),
        "w_ckv": nrm(ks[17], (DEPTH, D_MODEL, 2 * D_CROSS), D_MODEL ** -0.5),
        "g_cq": gain(ks[18], (DEPTH, CROSS_HEAD_DIM)),
        "g_ck": gain(ks[19], (DEPTH, CROSS_HEAD_DIM)),
        "w_co": nrm(ks[20], (DEPTH, D_CROSS, D_MODEL), D_CROSS ** -0.5),
        "g_mlp": gain(ks[21], (DEPTH, D_MODEL)),
        "w_up": nrm(ks[22], (DEPTH, D_MODEL, D_FF), D_MODEL ** -0.5),
        "w_down": nrm(ks[23], (DEPTH, D_FF, D_MODEL), D_FF ** -0.5),
    }

def first_block(x, mem, positions, g_mix, w_in, g_q, g_k, g_attn_out, conv_w, conv_b, dt_bias,
              a_log, d_skip, g_ssm_out, w_out, g_cross, g_mem, w_cq, w_ckv, g_cq, g_ck, w_co,
              g_mlp, w_up, w_down):
    bsz, s_len, _ = x.shape
    splits = np.cumsum([D_ATTN, D_ATTN, D_ATTN, D_SSM, D_CONV]).tolist()
    for i in range(DEPTH):
        h = rms_norm(x, g_mix[i])
        q, k, v, z, xbc, dt_raw = jnp.split(h @ w_in[i], splits, axis=-1)
        shp = (bsz, s_len, N_ATTN_HEADS, ATTN_HEAD_DIM)
        attn = dilated_attention(q.reshape(shp), k.reshape(shp), v.reshape(shp), positions, g_q[i], g_k[i])
        attn = rms_norm(attn.reshape(bsz, s_len, D_ATTN), g_attn_out[i]).astype(x.dtype)
        ssm = ssd_mixer(z, xbc, dt_raw, conv_w[i], conv_b[i], dt_bias[i], a_log[i], d_skip[i], g_ssm_out[i])
        x = x + jnp.concatenate([attn, ssm], axis=-1) @ w_out[i]
        x = x + cross_attention(rms_norm(x, g_cross[i]), rms_norm(mem, g_mem[i]),
                                w_cq[i], w_ckv[i], w_co[i], g_cq[i], g_ck[i])
        hm = rms_norm(x, g_mlp[i])
        x = x + jnp.square(jax.nn.relu(hm @ w_up[i])) @ w_down[i]
    return x


PLE_DIM = 256
RMS_EPS = 1e-6
N_HEADS = 16
QK_NOPE_DIM = 128
QK_ROPE_DIM = 64
V_HEAD_DIM = 128
QK_HEAD_DIM = QK_NOPE_DIM + QK_ROPE_DIM
Q_LORA_RANK = 768
KV_LORA_RANK = 512
ROPE_THETA_2 = 10000.0
Q_BLOCK = 128
D_RNN = D_MODEL
RNN_BLOCKS = 16
RNN_BLOCK_DIM = D_RNN // RNN_BLOCKS
LRU_C = 8.0
PEER_HEADS = 8
N_KEYS = 128
N_EXPERTS = N_KEYS * N_KEYS
PEER_QUERY_DIM = 256
PEER_HALF = PEER_QUERY_DIM // 2
PEER_TOPK = 16
PEER_CHUNK = 128
IN_SPLITS = (Q_LORA_RANK, KV_LORA_RANK, QK_ROPE_DIM, D_RNN, D_RNN, D_MODEL, D_MODEL)
IN_WIDTH = Q_LORA_RANK + KV_LORA_RANK + QK_ROPE_DIM + 2 * D_RNN + 2 * D_MODEL


def rms_norm_2(x, g):
    xf = x.astype(jnp.float32)
    y = xf * lax.rsqrt(jnp.mean(xf * xf, axis=-1, keepdims=True) + RMS_EPS)
    return (y * g.astype(jnp.float32)).astype(x.dtype)

def rope(x, pos):
    half = QK_ROPE_DIM // 2
    inv_freq = 1.0 / (ROPE_THETA_2 ** (jnp.arange(half, dtype=jnp.float32) / half))
    ang = pos.astype(jnp.float32)[:, None] * inv_freq[None, :]
    cos = jnp.cos(ang)[:, None, :]
    sin = jnp.sin(ang)[:, None, :]
    xf = x.astype(jnp.float32)
    x1, x2 = xf[..., :half], xf[..., half:]
    return jnp.concatenate([x1 * cos - x2 * sin, x2 * cos + x1 * sin], axis=-1).astype(x.dtype)

def split_columns(z):
    offs, acc = [], 0
    for w in IN_SPLITS[:-1]:
        acc += w
        offs.append(acc)
    return jnp.split(z, offs, axis=-1)

def mla_branch(c_q, c_kv, k_r, q_norm, w_uq, kv_norm, w_ukv, w_attn_o):
    B, S, _ = c_q.shape
    pos = jnp.arange(S)
    q = (rms_norm_2(c_q, q_norm) @ w_uq).reshape(B, S, N_HEADS, QK_HEAD_DIM)
    q_nope = q[..., :QK_NOPE_DIM]
    q_pe = rope(q[..., QK_NOPE_DIM:], pos)
    kv = (rms_norm_2(c_kv, kv_norm) @ w_ukv).reshape(B, S, N_HEADS, QK_NOPE_DIM + V_HEAD_DIM)
    k_nope, v = kv[..., :QK_NOPE_DIM], kv[..., QK_NOPE_DIM:]
    k_pe = rope(k_r[:, :, None, :], pos)[:, :, 0, :]
    scale = QK_HEAD_DIM ** -0.5
    n_blk = S // Q_BLOCK

    def to_blocks(t):
        return t.reshape(B, n_blk, Q_BLOCK, *t.shape[2:]).swapaxes(0, 1)

    def attend(args):
        qn, qp, blk = args
        s = (jnp.einsum('bqhd,bkhd->bhqk', qn, k_nope, preferred_element_type=jnp.float32)
             + jnp.einsum('bqhd,bkd->bhqk', qp, k_pe, preferred_element_type=jnp.float32))
        q_pos = blk * Q_BLOCK + jnp.arange(Q_BLOCK)
        s = jnp.where(pos[None, :] <= q_pos[:, None], s * scale, -jnp.inf)
        prob = jax.nn.softmax(s, axis=-1)
        return jnp.einsum('bhqk,bkhd->bqhd', prob.astype(v.dtype), v)

    o = lax.map(attend, (to_blocks(q_nope), to_blocks(q_pe), jnp.arange(n_blk)))
    o = o.swapaxes(0, 1).reshape(B, S, N_HEADS * V_HEAD_DIM)
    return o @ w_attn_o

def rglru_branch(x_r, y_r, conv_w, conv_b, w_rg_a, b_rg_a, w_rg_x, b_rg_x, lru_lambda, w_rnn_o):
    B, S, C = x_r.shape
    xc = lax.conv_general_dilated(x_r, conv_w[:, None, :], window_strides=(1,),
                                  padding=[(CONV_WIDTH - 1, 0)],
                                  dimension_numbers=('NWC', 'WIO', 'NWC'),
                                  feature_group_count=C) + conv_b
    xb = xc.reshape(B, S, RNN_BLOCKS, RNN_BLOCK_DIM)
    r = jax.nn.sigmoid(jnp.einsum('bshi,hij->bshj', xb, w_rg_a) + b_rg_a).reshape(B, S, C)
    i = jax.nn.sigmoid(jnp.einsum('bshi,hij->bshj', xb, w_rg_x) + b_rg_x).reshape(B, S, C)
    log_a = -LRU_C * r.astype(jnp.float32) * jax.nn.softplus(-lru_lambda.astype(jnp.float32))
    a = jnp.exp(log_a)
    mult = jnp.sqrt(-jnp.expm1(2.0 * log_a))
    mult = jnp.where((jnp.arange(S) == 0)[None, :, None], 1.0, mult)
    b = mult * (i * xc).astype(jnp.float32)

    def combine(left, right):
        a1, b1 = left
        a2, b2 = right
        return a1 * a2, a2 * b1 + b2

    _, h = lax.associative_scan(combine, (a, b), axis=1)
    y = h.astype(x_r.dtype) * jax.nn.gelu(y_r)
    return y @ w_rnn_o

def peer_ffn(x, w_peer_q, peer_subkeys, peer_u, peer_v):
    B, S, D = x.shape
    q = (x @ w_peer_q).reshape(B, S, PEER_HEADS, 2, PEER_HALF)
    s = jnp.einsum('bshcd,hcnd->bshcn', q, peer_subkeys, preferred_element_type=jnp.float32)
    top_s, top_i = lax.top_k(s, PEER_TOPK)
    cand = top_s[..., 0, :, None] + top_s[..., 1, None, :]
    cand = cand.reshape(B, S, PEER_HEADS, PEER_TOPK * PEER_TOPK)
    best_s, best_c = lax.top_k(cand, PEER_TOPK)
    i1 = jnp.take_along_axis(top_i[..., 0, :], best_c // PEER_TOPK, axis=-1)
    i2 = jnp.take_along_axis(top_i[..., 1, :], best_c % PEER_TOPK, axis=-1)
    experts = i1 * N_KEYS + i2
    gates = jax.nn.softmax(best_s, axis=-1).astype(x.dtype)
    T = B * S
    HK = PEER_HEADS * PEER_TOPK
    xs = x.reshape(T // PEER_CHUNK, PEER_CHUNK, D)
    es = experts.reshape(T // PEER_CHUNK, PEER_CHUNK, HK)
    gs = gates.reshape(T // PEER_CHUNK, PEER_CHUNK, HK)

    def chunk(args):
        xc, ec, gc = args
        u = peer_u[ec]
        act = jax.nn.gelu(jnp.einsum('tkd,td->tk', u, xc))
        return jnp.einsum('tk,tkd->td', gc * act, peer_v[ec])

    return lax.map(chunk, (xs, es, gs)).reshape(B, S, D)

def second_inputs(seed: int = 0) -> dict:
    key = jax.random.key(seed)
    ks = iter(jax.random.split(key, 40))
    f32 = jnp.float32

    def nrm(shape, scale):
        return jax.random.normal(next(ks), shape, f32) * scale

    def gain(shape):
        return 1.0 + nrm(shape, 0.05)

    L = DEPTH
    u = jax.random.uniform(next(ks), (L, D_RNN), f32, 0.9, 0.999)
    s_root = u ** (1.0 / LRU_C)
    lru_lambda = jnp.log(s_root) - jnp.log1p(-s_root)
    return {
        'x': nrm((BATCH, SEQ, D_MODEL), 1.0),
        'p': nrm((DEPTH, BATCH, SEQ, PLE_DIM), 1.0),
        'attn_norm': gain((L, D_MODEL)),
        'w_in': nrm((L, D_MODEL, IN_WIDTH), D_MODEL ** -0.5),
        'b_gate': nrm((L, 2 * D_MODEL), 0.01),
        'q_norm': gain((L, Q_LORA_RANK)),
        'w_uq': nrm((L, Q_LORA_RANK, N_HEADS * QK_HEAD_DIM), Q_LORA_RANK ** -0.5),
        'kv_norm': gain((L, KV_LORA_RANK)),
        'w_ukv': nrm((L, KV_LORA_RANK, N_HEADS * (QK_NOPE_DIM + V_HEAD_DIM)), KV_LORA_RANK ** -0.5),
        'w_attn_o': nrm((L, N_HEADS * V_HEAD_DIM, D_MODEL), (N_HEADS * V_HEAD_DIM) ** -0.5),
        'conv_w': nrm((L, CONV_WIDTH, D_RNN), CONV_WIDTH ** -0.5),
        'conv_b': nrm((L, D_RNN), 0.01),
        'w_rg_a': nrm((L, RNN_BLOCKS, RNN_BLOCK_DIM, RNN_BLOCK_DIM), RNN_BLOCK_DIM ** -0.5),
        'b_rg_a': nrm((L, RNN_BLOCKS, RNN_BLOCK_DIM), 0.01),
        'w_rg_x': nrm((L, RNN_BLOCKS, RNN_BLOCK_DIM, RNN_BLOCK_DIM), RNN_BLOCK_DIM ** -0.5),
        'b_rg_x': nrm((L, RNN_BLOCKS, RNN_BLOCK_DIM), 0.01),
        'lru_lambda': lru_lambda,
        'w_rnn_o': nrm((L, D_RNN, D_MODEL), D_RNN ** -0.5),
        'w_out': nrm((L, D_MODEL, D_MODEL), D_MODEL ** -0.5),
        'ffn_norm': gain((L, D_MODEL)),
        'w_peer_q': nrm((L, D_MODEL, PEER_HEADS * PEER_QUERY_DIM), D_MODEL ** -0.5),
        'peer_subkeys': nrm((L, PEER_HEADS, 2, N_KEYS, PEER_HALF), PEER_HALF ** -0.5),
        'peer_u': nrm((L, N_EXPERTS, D_MODEL), D_MODEL ** -0.5),
        'peer_v': nrm((L, N_EXPERTS, D_MODEL), PEER_HEADS ** -0.5),
        'ple_norm': gain((L, D_MODEL)),
        'w_ple_gate': nrm((L, D_MODEL, D_MODEL), D_MODEL ** -0.5),
        'w_ple_proj': nrm((L, PLE_DIM, D_MODEL), PLE_DIM ** -0.5),
        'final_norm': gain((D_MODEL,)),
    }

def second_block(x, p, attn_norm, w_in, b_gate, q_norm, w_uq, kv_norm, w_ukv, w_attn_o,
              conv_w, conv_b, w_rg_a, b_rg_a, w_rg_x, b_rg_x, lru_lambda, w_rnn_o, w_out,
              ffn_norm, w_peer_q, peer_subkeys, peer_u, peer_v, ple_norm, w_ple_gate,
              w_ple_proj, final_norm):
    h = x
    for l in range(DEPTH):
        n = rms_norm_2(h, attn_norm[l])
        c_q, c_kv, k_r, x_r, y_r, ga, gr = split_columns(n @ w_in[l])
        g_attn = jax.nn.sigmoid(ga + b_gate[l, :D_MODEL])
        g_rnn = jax.nn.sigmoid(gr + b_gate[l, D_MODEL:])
        y_attn = mla_branch(c_q, c_kv, k_r, q_norm[l], w_uq[l], kv_norm[l], w_ukv[l], w_attn_o[l])
        y_rnn = rglru_branch(x_r, y_r, conv_w[l], conv_b[l], w_rg_a[l], b_rg_a[l],
                             w_rg_x[l], b_rg_x[l], lru_lambda[l], w_rnn_o[l])
        h = h + (g_attn * y_attn + g_rnn * y_rnn) @ w_out[l]
        h = h + peer_ffn(rms_norm_2(h, ffn_norm[l]), w_peer_q[l], peer_subkeys[l], peer_u[l], peer_v[l])
        gate = jax.nn.sigmoid(rms_norm_2(h, ple_norm[l]) @ w_ple_gate[l])
        h = h + gate * (p[l] @ w_ple_proj[l])
    return rms_norm_2(h, final_norm)


def setup_inputs(seed=0):
    out = dict(first_inputs(seed))
    for name, value in second_inputs(seed + 1).items():
        if name != "x":
            out[name + "_2"] = value
    return out


def reference(
    x, mem, positions, g_mix, w_in, g_q, g_k, g_attn_out, conv_w, conv_b, dt_bias, a_log,
    d_skip, g_ssm_out, w_out, g_cross, g_mem, w_cq, w_ckv, g_cq, g_ck, w_co, g_mlp, w_up,
    w_down, p_2, attn_norm_2, w_in_2, b_gate_2, q_norm_2, w_uq_2, kv_norm_2, w_ukv_2,
    w_attn_o_2, conv_w_2, conv_b_2, w_rg_a_2, b_rg_a_2, w_rg_x_2, b_rg_x_2, lru_lambda_2,
    w_rnn_o_2, w_out_2, ffn_norm_2, w_peer_q_2, peer_subkeys_2, peer_u_2, peer_v_2, ple_norm_2,
    w_ple_gate_2, w_ple_proj_2, final_norm_2,
):
    x = first_block(
        x, mem, positions, g_mix, w_in, g_q, g_k, g_attn_out, conv_w, conv_b, dt_bias, a_log,
        d_skip, g_ssm_out, w_out, g_cross, g_mem, w_cq, w_ckv, g_cq, g_ck, w_co, g_mlp, w_up,
        w_down,
    )
    return second_block(
        x, p_2, attn_norm_2, w_in_2, b_gate_2, q_norm_2, w_uq_2, kv_norm_2, w_ukv_2, w_attn_o_2,
        conv_w_2, conv_b_2, w_rg_a_2, b_rg_a_2, w_rg_x_2, b_rg_x_2, lru_lambda_2, w_rnn_o_2,
        w_out_2, ffn_norm_2, w_peer_q_2, peer_subkeys_2, peer_u_2, peer_v_2, ple_norm_2,
        w_ple_gate_2, w_ple_proj_2, final_norm_2,
    )


_drawn_inputs = setup_inputs


def setup_inputs(seed=0):
    import zlib

    import numpy as np

    out = dict(_drawn_inputs(seed))
    spreads = {}
    factors = {'g_q': 4.307,
     'g_k': 3.848,
     'g_attn_out': 3.756,
     'conv_b': 3.072,
     'g_ssm_out': 4.007,
     'g_cross': 8.0,
     'g_mem': 8.0,
     'g_cq': 8.0,
     'g_ck': 8.0,
     'g_mlp': 2.855,
     'b_gate_2': 62.296,
     'q_norm_2': 8.0,
     'kv_norm_2': 5.996,
     'conv_b_2': 41.584,
     'b_rg_a_2': 200.0,
     'b_rg_x_2': 64.0,
     'ple_norm_2': 200.0,
     'w_rg_a_2': 64.0,
     'w_rg_x_2': 7.306,
     'lru_lambda_2': 60.336,
     'ffn_norm_2': 8.0,
     'w_peer_q_2': 4.476,
     'peer_subkeys_2': 4.473,
     'peer_u_2': 4.93,
     'peer_v_2': 4.438,
     'p_2': 6.385,
     'w_ple_gate_2': 8.0,
     'w_ple_proj_2': 6.396}
    for name, (base, spread) in spreads.items():
        noise = np.random.default_rng([zlib.crc32(name.encode()), seed]).standard_normal(out[name].shape)
        drawn = base * np.exp(spread * noise) if base else spread * noise
        out[name] = jnp.asarray(drawn.astype(out[name].dtype))
    for name, factor in factors.items():
        out[name] = (out[name] * factor).astype(out[name].dtype)
    return out
```

```python
from contextlib import ExitStack

import numpy as np
import concourse.bass as bass
from concourse import mybir

F32 = mybir.dt.float32
U32 = mybir.dt.uint32
I32 = mybir.dt.int32
R32 = mybir.dt.float32r
ALU = mybir.AluOpType
ACT = mybir.ActivationFunctionType
AXX = mybir.AxisListType.X

NEG = -1e30
EPS = 1e-6
T = 256
UNIT = 1024
NRAW = 5
NPAIR = 4

CONSTS = [("ident", 128), ("ones", 128), ("rot1", 128), ("rot2", 128), ("triu", 128),
          ("sel2", 62), ("sel1", 7), ("mask", 512),
          ("iota", 16), ("invf", 1), ("eps", 1)]
ORDER = [("w_qk", 32), ("w_v", 16), ("w_z", 16), ("w_xbc", 32), ("w_dt", 2), ("w_ck", 8), ("w_cv", 8), ("w_out", 32),
         ("w_cq", 8), ("w_co", 8), ("w_up0", 64), ("w_down0", 64), ("w_up1", 64), ("w_down1", 64), ("w2_low", 22),
         ("w2_xr", 32), ("w2_yr", 32), ("w2_gr", 32), ("w2_ga", 32), ("w2_rnn_o", 32), ("w2_uq", 24), ("w2_uk", 8),
         ("w2_uv", 8), ("w2_ao", 32), ("w2_out", 32), ("w_pq", 32), ("w2_pp", 4), ("w2_pg", 32)]
VECS = [("g_mix", 16), ("g_cross", 16), ("g_mem", 16), ("g_mlp", 16), ("attn_norm", 16), ("ffn_norm", 16),
        ("ple_norm", 16), ("final_norm", 16), ("g_q", 1), ("g_k", 1), ("g_attn", 8), ("g_ssm", 8),
        ("conv_w", 64), ("conv_b", 16), ("d_skip", 8), ("g_cq", 1), ("g_ck", 1), ("q_norm", 6), ("kv_norm", 4),
        ("b_gate", 32), ("conv_w2", 64), ("conv_b2", 16), ("b_a", 16), ("b_x", 16), ("lam", 16),
        ("dt_bias", 1), ("a_log", 1)]


def offsets(items):
    at, out = 0, {}
    for name, n in items:
        out[name] = (at, n)
        at += n
    return out, at


class Queue:

    def __init__(self, sem, chain):
        self.sem, self.chain, self.n, self.ops, self.seen = sem, chain, 0, [], {}

    def wait(self, toks):
        for t in toks:
            if t is None:
                continue
            if isinstance(t, list):
                self.wait(t)
                continue
            sem, v, key = t
            if self.seen.get(key, 0) < v:
                self.seen[key] = v
                self.ops.append((0, sem, v))

    def __call__(self, fn, *toks, inc=True):
        self.wait(toks)
        if self.chain and self.n:
            self.wait([self.tok()])
        self.ops.append((1, fn, inc))
        if inc:
            self.n += 1
        return self.tok()

    def tok(self):
        return (self.sem, self.n, id(self))

    def play(self, eng):
        for kind, a, b in self.ops:
            if kind == 0:
                eng.wait_ge(a, b)
            elif kind == 1:
                ins = a(eng)
                if b:
                    ins.then_inc(self.sem, 1)
            else:
                a(eng).then_inc(b, 16)


SLOTS = []


class Slot:

    def __init__(self, ap, sem):
        self.ap, self.sem, self.n, self.free = ap, sem, 0, None
        SLOTS.append(self)

    def fill(self, q, fn, *toks):
        q.wait([self.free, *toks])
        self.n += 16
        q.ops.append((2, fn, self.sem))
        return (self.sem, self.n, id(self))


class Bank:
    def __init__(self, ap):
        self.ap, self.free = ap, None


class Ring:
    def __init__(self, items):
        self.items, self.at = items, 0

    def next(self):
        self.at += 1
        return self.items[(self.at - 1) % len(self.items)]


def step(g):
    if g is not None:
        try:
            next(g)
        except StopIteration:
            pass


def drain(g):
    for _ in g:
        pass


def pipeline(gens):
    live = []
    gens = list(gens)
    while gens or live:
        if gens:
            live.append(gens.pop(0))
        for g in list(live):
            try:
                next(g)
            except StopIteration:
                live.remove(g)
        yield


def build(nc, A, out):
    ctx = ExitStack()
    with ctx:
        def sb(name, shape, dt=F32):
            return ctx.enter_context(nc.sbuf_tensor(name, shape, dt))

        def sem(name):
            return ctx.enter_context(nc.semaphore(name))

        co, ncon = offsets(CONSTS)
        vo, nvec = offsets(VECS)
        X = sb("X", [128, 16, T])
        with nc.sbuf_tensor("HF", [128, 2, 16 * T], F32) as HF:
            pass
        HS = sb("HS", [128, 2, 16 * T], R32)
        with nc.sbuf_tensor("BIG", [128, 20480], F32) as BIG:
            pass
        BIGR = sb("BIGR", [128, 20480], R32)
        RAW = sb("RAW", [128, NRAW, UNIT])
        HL = sb("HL", [128, NPAIR, 2, UNIT], R32)
        CON = sb("CON", [128, ncon])
        VEC = sb("VEC", [128, nvec])
        CS1 = sb("CS1", [128, 2, T])
        TMP = sb("TMP", [128, 2, 1024])
        RS = sb("RS", [128, 2, T])
        SM = sb("SM", [128, 512])
        GT = sb("GT", [128, T])
        PS = [ctx.enter_context(nc.psum_tensor(f"ps{i}", [128, 512], F32)) for i in range(8)]

        def con(name):
            o, n = co[name]
            return CON[:, o:o + n]

        def vec(name, i=0, n=1):
            o = vo[name][0] + i
            return VEC[:, o:o + n]

        PE = Queue(sem("s_pe"), False)
        V = Queue(sem("s_v"), True)
        S = Queue(sem("s_a"), True)
        G = Queue(sem("s_g"), True)
        SP = Queue(sem("s_sp"), False)

        raws = Ring([Slot(RAW[:, i, :], sem(f"s_w{i}")) for i in range(NRAW)])
        pairs = Ring([Bank(HL[:, i, :, :]) for i in range(NPAIR)])
        dense_banks = Ring([Bank(PS[i][:, :]) for i in range(3)])
        norm_bank = Bank(PS[3][:, :])
        score_banks = Ring([Bank(PS[4][:, :]), Bank(PS[5][:, :])])
        tr_bank = Bank(PS[6][:, :])
        out_bank = Bank(PS[7][:, :])
        tmp_free = [None, None]
        tmp_at = [0]
        rs_free = [None, None]
        rs_at = [0]

        def big(o, n):
            return BIG[:, o:o + n]

        def chunks(o, n):
            return BIG[:, o:o + n * T].rearrange("p (c t) -> p c t", t=T)

        def mm(o, l, r, start, stop, *toks, inc=False):
            return PE(lambda e: e.matmul(o, l, r, start=start, stop=stop, skip_group_check=True), *toks, inc=inc)

        def tr(o, i, *toks, inc=False):
            k = i.shape[0]
            return PE(lambda e: e.transpose(o, i, con("ident")[0:k, 0:k]), *toks, inc=inc)

        def act(o, i, f, *toks, bias=0.0, scale=1.0, acc=None):
            if acc is not None:
                return S(lambda e: e.activation(o, i, f, bias=bias, scale=scale, accum_out=acc), *toks)
            return S(lambda e: e.activation(o, i, f, bias=bias, scale=scale), *toks)

        def scopy(o, i, *toks):
            return S(lambda e: e.copy(o, i), *toks)

        def ts(o, i, s1, s2, op0, op1, *toks):
            if s2 is None:
                return V(lambda e: e.tensor_scalar(o, i, s1, None, op0), *toks)
            return V(lambda e: e.tensor_scalar(o, i, s1, s2, op0, op1), *toks)

        def tt(o, a, b, op, *toks):
            return V(lambda e: e.tensor_tensor(o, a, b, op), *toks)

        def stt(o, a, s, b, op0, op1, *toks):
            return V(lambda e: e.scalar_tensor_tensor(out=o, in0=a, scalar=s, in1=b, op0=op0, op1=op1), *toks)

        def vcopy(o, i, *toks):
            return V(lambda e: e.tensor_copy(o, i), *toks)

        def recip(o, i, *toks):
            return V(lambda e: e.reciprocal(o, i), *toks)

        def load(dst, src, name, q=None):
            s = Slot(dst, sem(name))
            return s.fill(q or S, lambda e: e.dma_start(dst, src))

        t_con = load(CON[:, :], A["consts"], "s_con")
        t_vec = load(VEC[:, :], A["vecs"], "s_vec")
        t_x = load(X[:, :, :], A["xT"], "s_x")
        MEM = chunks(16384, 16)
        t_mem = load(MEM, A["memT"], "s_mem")
        POSI = big(0, T).bitcast(I32)
        t_pos = load(POSI, A["positions"].partition_broadcast(128), "s_pos")
        for q in (PE, V, S):
            q.wait([t_con, t_vec])

        def split(src, hi, lo, toks, war=None):
            a = scopy(hi, src, toks, war)
            return tt(lo, src, hi.bitcast(F32), ALU.subtract, a)

        class Act:

            def __init__(self, hi, lo):
                self.hi, self.lo, self.tok = hi, lo, [None] * hi.shape[1]

            def cut(self, src, c0, n, toks, war=None):
                t = split(src, self.hi[:, c0:c0 + n, :], self.lo[:, c0:c0 + n, :], toks, war)
                for c in range(c0, c0 + n):
                    self.tok[c] = t
                return t

        def hs_act():
            return Act(*[HS[:, j, :].rearrange("p (c t) -> p c t", t=T) for j in range(2)])

        def bigr(o, n):
            return BIGR[:, o:o + n * T].rearrange("p (c t) -> p c t", t=T)

        loaded, cut_ = [], []

        def load_unit():
            if len(loaded) < len(STREAM):
                u = STREAM[len(loaded)]
                s = raws.next()
                n = u.shape[1]
                loaded.append((s, n, s.fill(SP, lambda e: e.dma_start(s.ap[:, 0:n], u))))

        def cut_unit():
            if len(cut_) < len(loaded):
                s, n, t = loaded[len(cut_)]
                p = pairs.next()
                s.free = split(s.ap[:, 0:n], p.ap[:, 0, 0:n], p.ap[:, 1, 0:n], t, p.free)
                cut_.append((p, n, s.free))

        taken = [0]

        def take(n, held=0):
            while len(cut_) <= min(taken[0] + NPAIR - 1 - held, len(STREAM) - 1):
                if len(loaded) == len(cut_):
                    load_unit()
                cut_unit()
            while len(loaded) < min(len(cut_) + NRAW, len(STREAM)):
                load_unit()
            p, m, t = cut_[taken[0]]
            assert m == n, (taken[0], m, n)
            taken[0] += 1
            return p, t

        def products(o, p, w0, a, k, first, last, *toks, end=False):
            wh, wl = p.ap[:, 0, w0:w0 + 128], p.ap[:, 1, w0:w0 + 128]
            mm(o, wh, a.hi[:, k, :], first, False, a.tok[k], *toks)
            mm(o, wh, a.lo[:, k, :], False, False)
            return mm(o, wl, a.hi[:, k, :], False, last, inc=end)

        def dense(n, K, cw, a, evac, bg=None, parts=1):
            c = 0
            for _ in range(n):
                if parts > 1:
                    assert cw == 128
                b = None
                for u in range(parts):
                    p, t = take(K * cw)
                    for j in range(cw // 128):
                        if u == 0:
                            b = dense_banks.next()
                        for k in range(K):
                            last = products(b.ap[:, 0:T], p, k * cw + j * 128, a, u * K + k, u == 0 and k == 0,
                                            u == parts - 1 and k == K - 1, t, b.free, end=(k == K - 1))
                        p.free = last
                        if u == parts - 1:
                            b.free = evac(c, b.ap[:, 0:T], last)
                            c += 1
                            step(bg)
            return last

        def dense_tok(n, K, cw, a, evac, bg=None, parts=1):
            for c in range(n):
                ps = [take(K * cw, u) for u in range(parts)]
                b = dense_banks.next()
                for i in range(2):
                    o = b.ap[:, i * cw:i * cw + cw]
                    for u, (p, t) in enumerate(ps):
                        for k in range(K):
                            wh, wl = p.ap[:, 0, k * cw:k * cw + cw], p.ap[:, 1, k * cw:k * cw + cw]
                            xh, xl = [x[:, u * K + k, i * 128:i * 128 + 128] for x in (a.hi, a.lo)]
                            end = u == parts - 1 and k == K - 1
                            mm(o, xh, wh, u == 0 and k == 0, False, t, b.free, a.tok[u * K + k])
                            mm(o, xh, wl, False, False)
                            last = mm(o, xl, wh, False, end, inc=end)
                for p, _ in ps:
                    p.free = last
                b.free = evac(c * cw, cw, b.ap[:, 0:2 * cw].rearrange("p (i n) -> p i n", i=2), last)
                step(bg)
            return last

        class Squares:

            def __init__(self, nch):
                self.nch, self.n, self.todo = nch, 0, []

            def add(self, src, m, *toks):
                i = tmp_at[0] % 2
                tmp_at[0] += 1
                sq = TMP[:, i, 0:m * T].rearrange("p (c t) -> p c t", t=T)
                a = act(sq, src, ACT.Square, *toks, tmp_free[i])
                self.todo.append((i, sq, m, a))

            def flush(self):
                for i, sq, m, a in self.todo:
                    for k in range(m):
                        self.last = mm(norm_bank.ap[:, 0:T], con("ones"), sq[:, k, :], self.n == 0,
                                       self.n == self.nch - 1, a, norm_bank.free, inc=(k == m - 1))
                        self.n += 1
                    tmp_free[i] = self.last
                self.todo = []

        def tmp():
            i = tmp_at[0] % 2
            tmp_at[0] += 1
            return i, TMP[:, i, :].rearrange("p (c t) -> p c t", t=T)

        def rms(src, nch, dst, gain, n, toks, war=None, sq=None, keep=None, d0=0):
            if sq is None:
                sq = Squares(nch)
                for c0 in range(0, nch, 4):
                    m = min(4, nch - c0)
                    sq.add(src[:, c0:c0 + m, :], m, toks)
                    sq.flush()
            sq.flush()
            r = rs_at[0] % 2
            rs_at[0] += 1
            a = act(RS[:, r, :], norm_bank.ap[:, 0:T], ACT.Sqrt, sq.last, rs_free[r], bias=con("eps"), scale=1.0 / n)
            norm_bank.free = a
            recip(RS[:, r, :], RS[:, r, :], a)
            groups, c = [], 0
            while c < nch:
                m = min(1 if c == 0 else 3 if c == 1 else 4, nch - c)
                groups.append((c, m))
                c += m
            for c0, m in groups:
                if keep is None:
                    i, buf = tmp()
                else:
                    i, buf = None, keep[:, c0:c0 + m, :]
                for c in range(m):
                    t = stt(buf[:, c, :], src[:, c0 + c, :], gain(c0 + c), RS[:, r, :], ALU.mult, ALU.mult, toks,
                            war if i is None else tmp_free[i])
                t = dst.cut(buf[:, 0:m, :], d0 + c0, m, t, war)
                if i is not None:
                    tmp_free[i] = t
            rs_free[r] = V.tok()
            return V.tok()

        def head_rstd(src, nch, per, n, toks, dst):
            rows = nch * per
            name, w = ("sel2", 30) if per == 2 else ("sel1", 3)
            sel = con(name)
            for c0 in range(0, nch, 4):
                i = tmp_at[0] % 2
                tmp_at[0] += 1
                sq = TMP[:, i, :].rearrange("p (c t) -> p c t", t=T)
                a = act(sq, src[:, c0:c0 + 4, :], ACT.Square, toks, tmp_free[i])
                for k in range(4):
                    c = c0 + k
                    p = mm(norm_bank.ap[0:rows, 0:T], sel[:, w - per * c:w - per * c + rows], sq[:, k, :],
                           c == 0, c == nch - 1, a, norm_bank.free, inc=(k == 3))
                tmp_free[i] = p
            a = act(dst, norm_bank.ap[0:rows, 0:T], ACT.Sqrt, p, bias=con("eps")[0:rows, :], scale=1.0 / n)
            norm_bank.free = a
            return recip(dst, dst, a)

        xsq = [None]

        def residual(c, ps, tok):
            xt[c] = tt(X[:, c, :], X[:, c, :], ps, ALU.add, tok)
            xsq[0].flush()
            xsq[0].add(X[:, c:c + 1, :], 1, xt[c])
            return xt[c]

        def residual_only(c, ps, tok):
            xt[c] = tt(X[:, c, :], X[:, c, :], ps, ALU.add, tok)
            return xt[c]

        xt = [t_x] * 16

        def softmax_head(P, PT, den, score, scale, mask, causal, vl, o, otok):
            b = score_banks.next()
            t = score(b.ap, b.free)
            if mask is not None:
                v = stt(P.ap, b.ap, scale, mask, ALU.mult, ALU.add, t, P.free)
                b.free = v
                V(lambda e: e.tensor_reduce(den[:, 0:2], P.ap.rearrange("p (a k) -> p a k", a=2), AXX, ALU.max,
                                            negate=True))
                m = V.tok()
                for i in range(2):
                    a = act(P.ap[:, i * T:i * T + T], P.ap[:, i * T:i * T + T], ACT.Exp, m,
                            bias=den[:, i:i + 1], acc=den[:, 2 + i:3 + i])
            else:
                V(lambda e: e.tensor_reduce(den[:, 0:2], b.ap.rearrange("p (a k) -> p a k", a=2), AXX, ALU.max,
                                            negate=True), t)
                m = ts(den[:, 0:2], den[:, 0:2], scale, None, ALU.mult, None)
                for i in range(2):
                    a = act(P.ap[:, i * T:i * T + T], b.ap[:, i * T:i * T + T], ACT.Exp, m, P.free,
                            bias=den[:, i:i + 1], scale=scale, acc=den[:, 2 + i:3 + i])
                b.free = a
            recip(den[:, 4:6], den[:, 2:4], a)
            for i in range(2):
                n = 128 if causal and i == 0 else T
                v = ts(P.ap[:, i * T:i * T + n], P.ap[:, i * T:i * T + n], den[:, 4 + i:5 + i], None, ALU.mult, None)
            yield
            blocks = [(0, 0), (1, 0), (1, 1)] if causal else [(0, 0), (1, 0), (0, 1), (1, 1)]
            for n, (i, k) in enumerate(blocks):
                t = tr(tr_bank.ap[:, n * 128:n * 128 + 128], P.ap[:, i * T + k * 128:i * T + k * 128 + 128],
                       v, tr_bank.free, inc=(n == len(blocks) - 1))
            P.free = t
            w = 128 * len(blocks)
            a = scopy(PT.ap[:, 0:w], tr_bank.ap[:, 0:w], t, PT.free)
            tr_bank.free = a
            yield
            lo, hi = o.base_partition() if callable(o.base_partition) else o.base_partition, o.shape[0]
            ob = out_bank.ap[lo:lo + hi, 0:T]
            mm(ob, vl(0), PT.ap[:, 0:T], True, False, a, out_bank.free, otok)
            if causal:
                t = mm(out_bank.ap[lo:lo + hi, 128:T], vl(1), PT.ap[:, T:T + 128], False, True, inc=True)
            else:
                t = mm(ob, vl(1), PT.ap[:, T:2 * T], False, True, inc=True)
            PT.free = t
            out_bank.free = scopy(o, ob, t)
            yield

        class Buf:
            def __init__(self, ap):
                self.ap, self.free = ap, None

        STREAM = [A[n][i] for n, c in ORDER for i in range(c)]
        h1 = hs_act()
        t_h = rms(X, 16, h1, lambda c: vec("g_mix", c), 2048, [t_x])
        QT, KT = chunks(0, 8), chunks(2048, 8)
        QK = chunks(0, 16)
        VT = big(4096, 2048).rearrange("p (i d) -> p i d", i=2)
        Z = chunks(6144, 8)
        XBC = chunks(8192, 16)
        XST = big(12288, 2048).rearrange("p (i d) -> p i d", i=2)
        BT = big(14336, 512)

        ANG = TMP[:, 0, 0:T]
        KK = TMP[:, 0, T:2 * T]
        POS = TMP[:, 0, 2 * T:3 * T]
        t = vcopy(POS, POSI, t_pos, tmp_free[0], tmp_free[1])
        t_posr = t
        for j, ph in enumerate((0.25, 0.0)):
            ts(ANG, POS, con("invf"), None, ALU.mult, None)
            ts(KK, ANG, float(np.float32(1 / (2 * np.pi))), ph, ALU.mult, ALU.add)
            ts(KK, KK, 12582912.0, None, ALU.add, None)
            ts(KK, KK, 12582912.0, None, ALU.subtract, None)
            for cst in (6.28125, 0.0019340515136718750, 1.2556659146e-06):
                stt(ANG, KK, -cst, ANG, ALU.mult, ALU.add)
            t = ts(CS1[:, j, :], ANG, float(np.float32(ph * 2 * np.pi)), float(np.float32(np.pi)), ALU.add, ALU.min)
            t = ts(CS1[:, j, :], CS1[:, j, :], float(-np.float32(np.pi)), None, ALU.max, None)
        t_cs = act(CS1[:, :, :], CS1[:, :, :], ACT.Sin, t)
        tmp_free[0] = t

        qkt = [None] * 16

        def evac_qk(c, ps, tok):
            qkt[c] = (vcopy if c % 2 else scopy)(QK[:, c, :], ps, tok, t_posr)
            return qkt[c]

        dense(16, 8, 128, h1, evac_qk, parts=2)

        qkr = [None] * 16

        def norm_rope():
            rb = SM[0:32, 0:T]
            t_r = head_rstd(QK, 16, 2, 64, [qkt[14], qkt[15]], rb)
            yield
            for c in range(16):
                b = score_banks.next()
                for j in range(2):
                    t = mm(b.ap[64 * j:64 * j + 64, 0:T], con("ident")[0:32, 2 * c + j:2 * c + j + 1].to_broadcast([32, 64]),
                           rb, True, True, t_r, b.free, inc=(j == 1))
                t = stt(QK[:, c, :], QK[:, c, :], vec("g_q" if c < 8 else "g_k"), b.ap[:, 0:T], ALU.mult, ALU.mult, t)
                b.free = t
                if c < 8:
                    t = ts(QK[:, c, :], QK[:, c, :], 0.125, None, ALU.mult, None)
                yield
                b = score_banks.next()
                p = mm(b.ap[:, 0:T], con("rot1"), QK[:, c, :], True, True, t, b.free, inc=True)
                rt = TMP[:, 1, 0:T]
                t = tt(rt, b.ap[:, 0:T], CS1[:, 1, :], ALU.mult, p, t_cs, tmp_free[1])
                b.free = t
                tt(QK[:, c, :], QK[:, c, :], CS1[:, 0, :], ALU.mult, p)
                qkr[c] = tt(QK[:, c, :], QK[:, c, :], rt, ALU.add)
                tmp_free[1] = qkr[c]
                yield

        g_nr = norm_rope()
        t_v = [None]

        def evac_v(c0, n, ps, tok):
            t_v[0] = scopy(VT[:, :, c0:c0 + n], ps, tok)
            return t_v[0]

        dense_tok(8, 8, 128, h1, evac_v, g_nr, parts=2)

        AP_ = [Buf(big(14848 + 512 * i, 512)) for i in range(2)]
        APT = [Buf(big(15872 + 256 * i, 384)) for i in range(1)]
        atok = [None] * 8

        def attn(h):
            c, lo = h // 2, 64 * (h % 2)
            q, k = QK[lo:lo + 64, c, :], QK[lo:lo + 64, 8 + c, :]

            def score(b, free):
                for i in range(2):
                    t = mm(b[:, i * T:i * T + T], q[:, i * 128:i * 128 + 128], k, True, True,
                           qkr[c], qkr[8 + c], free, inc=(i == 1))
                return t

            den = SM[:, 256 + 8 * (h % 4):264 + 8 * (h % 4)]
            yield from softmax_head(AP_[h % 2], APT[0], den, score, 1.0, con("mask"), True,
                                    lambda kt: VT[:, kt, h * 64:h * 64 + 64], q, t_v[0])
            atok[c] = S.tok()

        def all_attn():
            yield from g_nr
            yield from pipeline(attn(h) for h in range(16))

        g_at = all_attn()

        def evac_z(c, ps, tok):
            return vcopy(Z[:, c, :], ps, tok)

        dense(8, 8, 128, h1, evac_z, g_at, parts=2)
        t_z = V.tok()

        ctok = [None] * 16

        def conv(dst, ps, w, b, tok):
            t = ts(dst, ps, w(3), b, ALU.mult, ALU.add, tok)
            for j in (1, 2, 3):
                t = stt(dst[:, j:T], ps[:, 0:T - j], w(3 - j), dst[:, j:T], ALU.mult, ALU.add)
            return t

        def evac_xbc(c, ps, tok):
            ctok[c] = conv(XBC[:, c, :], ps, lambda j: vec("conv_w", 4 * c + j), vec("conv_b", c), tok)
            return ctok[c]

        dense(16, 8, 128, h1, evac_xbc, g_at, parts=2)
        DT = GT[0:16, :]

        def evac_dt(c, ps, tok):
            return ts(DT, ps[0:16, :], vec("dt_bias")[0:16, :], None, ALU.add, None, tok)

        t_hfree = dense(1, 8, 128, h1, evac_dt, g_at, parts=2)
        drain(g_at)
        SILU = ACT.Silu
        t_zs = [act(Z[:, i:i + 4, :], Z[:, i:i + 4, :], SILU, t_z) for i in (0, 4)][-1]
        t_xbc = [act(XBC[:, i:i + 4, :], XBC[:, i:i + 4, :], SILU, ctok[i + 3]) for i in (0, 4, 8, 12)]

        CK = chunks(2048, 4)
        CV = big(3072, 1024).rearrange("p (i d) -> p i d", i=2)

        def log1p_exp(x, m, y, z, p, tok):
            ts(m, x, 0.0, None, ALU.max, None, tok)
            ts(y, x, -1.0, None, ALU.mult, None)
            t = tt(y, x, y, ALU.min)
            t = act(y, y, ACT.Exp, t)
            ts(z, y, 2.0, None, ALU.add, None, t)
            recip(z, z)
            tt(y, y, z, ALU.mult)
            tt(z, y, y, ALU.mult)
            ts(p, z, 1.0 / 17, None, ALU.mult, None)
            for d in (15, 13, 11, 9, 7, 5, 3):
                stt(p, p, 1.0 / d, z, ALU.add, ALU.mult)
            stt(p, p, 1.0, y, ALU.add, ALU.mult)
            return stt(x, p, 2.0, m, ALU.mult, ALU.add)

        DA = SM[0:16, 0:T]
        ACS = RS[0:16, 0, :]
        ACT_ = SM[:, 320:352].rearrange("p (i h) -> p i h", i=2)
        DTT = SM[:, 352:384].rearrange("p (i h) -> p i h", i=2)
        SSB = 14848
        CB = big(SSB, 256).rearrange("p (i l) -> p i l", i=2)
        EE = [big(SSB + 256 + 256 * i, 256) for i in range(2)]
        WW = [Buf(big(SSB + 768 + 256 * i, 256)) for i in range(2)]
        ECS = [Buf(big(SSB + 1280 + 128 * i, 128)) for i in range(2)]
        XW = Buf(big(SSB + 1536 - 0, 64)) if False else Buf(SM[:, 384:448])
        PV = Buf(SM[:, 448:512])
        sst = [None] * 8

        def ssd_pre():
            xx = [TMP[0:16, i, j * T:j * T + T] for i in range(2) for j in range(2)]
            V.wait([tmp_free[0], tmp_free[1]])
            t = log1p_exp(DT, *xx, None)
            tmp_free[0] = tmp_free[1] = t
            al = SM[0:16, 288:289]
            a = act(al, vec("a_log")[0:16, :], ACT.Exp, t)
            ts(DA, DT, al, -1.0, ALU.mult, ALU.mult, a)
            for i in range(2):
                V(lambda e, i=i: e.tensor_tensor_scan(ACS[:, i * 128:i * 128 + 128], con("ones")[0:16, :],
                                                      DA[:, i * 128:i * 128 + 128], 0.0, ALU.mult, ALU.add),
                  rs_free[0])
            t = V.tok()
            yield
            for src, dst in ((ACS, ACT_), (DT, DTT)):
                for i in range(2):
                    p = tr(tr_bank.ap[:, i * 16:i * 16 + 16], src[:, i * 128:i * 128 + 128], t, tr_bank.free,
                           inc=(i == 1))
                u = vcopy(dst, tr_bank.ap[:, 0:32].rearrange("p (i h) -> p i h", i=2), p)
                tr_bank.free = u
                yield
            for c0 in range(0, 8, 4):
                for i in range(2):
                    for c in range(c0, c0 + 4):
                        p = tr(tr_bank.ap[:, (c - c0) * 128:(c - c0) * 128 + 128], XBC[:, c, i * 128:i * 128 + 128],
                               t_xbc, tr_bank.free, inc=(c == c0 + 3))
                    u = vcopy(XST[:, i, c0 * 128:c0 * 128 + 512], tr_bank.ap[:, :], p)
                    tr_bank.free = u
                    yield
            for g in range(4):
                p = tr(tr_bank.ap[:, g * 128:g * 128 + 128], XBC[:, 8 + g, 0:128], t_xbc, tr_bank.free, inc=(g == 3))
            u = vcopy(BT, tr_bank.ap[:, :], p)
            tr_bank.free = u
            pre[0] = u
            yield

        pre = [None]
        cbt = [None]

        def ssd_head(h):
            g, c, lo = h // 4, h // 2, 64 * (h % 2)
            Bg, Cg = XBC[:, 8 + g, :], XBC[:, 12 + g, :]
            if h % 4 == 0:
                sb_ = score_banks.next()
                for i in range(2):
                    p = mm(sb_.ap[:, i * 128:i * 128 + 128], Bg[:, i * 128:i * 128 + 128],
                           Cg[:, i * 128:i * 128 + 128], True, True, sb_.free, t_xbc, pre[0], inc=(i == 1))
                sb_.free = cbt[0] = tt(CB, sb_.ap[:, 0:T].rearrange("p (i l) -> p i l", i=2),
                                       con("triu").unsqueeze(1).to_broadcast([128, 2, 128]), ALU.mult, p)
            k = h % 2
            sb_ = score_banks.next()
            p = mm(sb_.ap[:, 0:T], con("ident")[0:16, h:h + 1].to_broadcast([16, 128]), ACS, True, True,
                   sb_.free, pre[0], inc=True)
            E_ = EE[k]
            for i in range(2):
                t = ts(E_[:, i * 128:i * 128 + 128], sb_.ap[:, i * 128:i * 128 + 128], ACT_[:, i, h:h + 1], 0.0,
                       ALU.subtract, ALU.min, p)
            a = act(ECS[k].ap, sb_.ap[:, 128:T], ACT.Exp, t, ECS[k].free)
            sb_.free = a
            a = act(E_, E_, ACT.Exp, t)
            t_xw = ts(XW.ap, XST[:, 0, h * 64:h * 64 + 64], E_[:, 127:128], DTT[:, 0, h:h + 1], ALU.mult, ALU.mult, a,
                      XW.free)
            for i in range(2):
                t = stt(WW[k].ap[:, i * 128:i * 128 + 128], E_[:, i * 128:i * 128 + 128], DTT[:, i, h:h + 1],
                        CB[:, i, :], ALU.mult, ALU.mult, WW[k].free)
            t = tt(ECS[k].ap, ECS[k].ap, Cg[:, 128:T], ALU.mult, t_xbc)
            yield
            p = mm(tr_bank.ap[:, 0:64], BT[:, g * 128:g * 128 + 128], XW.ap, True, True, t_xw, tr_bank.free, inc=True)
            XW.free = p
            a = scopy(PV.ap, tr_bank.ap[:, 0:64], p, PV.free)
            tr_bank.free = a
            yield
            ob = out_bank.ap[lo:lo + 64, 0:T]
            xs = XST[:, :, h * 64:h * 64 + 64]
            mm(ob[:, 0:128], xs[:, 0, :], WW[k].ap[:, 0:128], True, True, t, out_bank.free)
            mm(ob[:, 128:T], xs[:, 1, :], WW[k].ap[:, 128:T], True, False)
            p = mm(ob[:, 128:T], PV.ap, ECS[k].ap, False, True, a, inc=True)
            WW[k].free = ECS[k].free = PV.free = p
            y = XBC[lo:lo + 64, c, :]
            t = stt(y, y, vec("d_skip", c)[lo:lo + 64, :], ob, ALU.mult, ALU.add, p)
            out_bank.free = t
            sst[c] = tt(Z[lo:lo + 64, c, :], Z[lo:lo + 64, c, :], y, ALU.mult, t_zs)
            yield

        def ssd():
            yield from ssd_pre()
            for h in range(16):
                yield from ssd_head(h)
        g_ss = ssd()
        mh = hs_act()
        rms(MEM, 16, mh, lambda c: vec("g_mem", c), 2048, [t_mem], t_hfree)
        ckt = [None]

        def evac_ck(c, ps, tok):
            ckt[0] = scopy(CK[:, c, :], ps, tok)
            return ckt[0]

        dense(4, 8, 128, mh, evac_ck, g_ss, parts=2)
        t_cv = [None]

        def evac_cv(c0, n, ps, tok):
            t_cv[0] = scopy(CV[:, :, c0:c0 + n], ps, tok)
            return t_cv[0]

        t_hfree = dense_tok(4, 8, 128, mh, evac_cv, g_ss, parts=2)
        drain(g_ss)
        mx = hs_act()
        rms(QT, 8, mx, lambda c: vec("g_attn", c), 1024, [atok[6], atok[7]], t_hfree)
        for g in range(4):
            rms(Z[:, 2 * g:2 * g + 2, :], 2, mx, lambda c, g=g: vec("g_ssm", 2 * g + c), 256,
                [sst[2 * g], sst[2 * g + 1]], t_hfree, d0=8 + 2 * g)

        def head_norm(src, toks, g):
            rb = SM[0:4, 0:T]
            t_r = head_rstd(src, 4, 1, 128, toks, rb)
            for c in range(4):
                b = score_banks.next()
                t = mm(b.ap[:, 0:T], con("ident")[0:4, c:c + 1].to_broadcast([4, 128]), rb, True, True, t_r, b.free,
                       inc=True)
                t = stt(src[:, c, :], src[:, c, :], vec(g), b.ap[:, 0:T], ALU.mult, ALU.mult, t)
                b.free = t
            return t

        t_ckn = head_norm(CK, [ckt[0]], "g_ck")

        xsq[0] = Squares(16)
        t_hfree = dense(16, 8, 128, mx, residual, parts=2)
        hc = hs_act()
        rms(X, 16, hc, lambda c: vec("g_cross", c), 2048, xt, t_hfree, xsq[0])
        CQ = chunks(0, 4)
        cqt = [None]

        def evac_cq(c, ps, tok):
            cqt[0] = scopy(CQ[:, c, :], ps, tok)
            return cqt[0]

        t_hfree = dense(4, 8, 128, hc, evac_cq, parts=2)
        t_cqn = head_norm(CQ, [cqt[0]], "g_cq")
        CP = [Buf(big(4096 + 512 * i, 512)) for i in range(2)]
        CPT = Buf(big(5120, 512))
        cot = [None] * 4

        def cross(h):
            def score(b, free):
                for i in range(2):
                    t = mm(b[:, i * T:i * T + T], CQ[:, h, i * 128:i * 128 + 128], CK[:, h, :], True, True,
                           t_cqn, t_ckn, free, inc=(i == 1))
                return t

            den = SM[:, 256 + 8 * (h % 4):264 + 8 * (h % 4)]
            yield from softmax_head(CP[h % 2], CPT, den, score, 128.0 ** -0.5, None, False,
                                    lambda kt: CV[:, kt, h * 128:h * 128 + 128], CQ[:, h, :], t_cv[0])
            cot[h] = S.tok()

        drain(pipeline(cross(h) for h in range(4)))
        cx = hs_act()
        for c in range(4):
            cx.cut(CQ[:, c:c + 1, :], c, 1, cot[c], t_hfree)
        xsq[0] = Squares(16)
        t_hfree = dense(8, 4, 256, cx, residual)
        hm = hs_act()
        rms(X, 16, hm, lambda c: vec("g_mlp", c), 2048, xt, t_hfree, xsq[0])
        hid = Act(bigr(0, 32), bigr(8192, 32))
        t_cfree = [PE.tok(), V.tok(), S.tok()]

        def evac_up(c, ps, tok):
            i, buf = tmp()
            a = act(buf[:, 0, :], ps, ACT.Relu, tok, tmp_free[i])
            t = tt(buf[:, 1, :], buf[:, 0, :], buf[:, 0, :], ALU.mult, a)
            tmp_free[i] = hid.cut(buf[:, 1:2, :], c, 1, t, t_cfree)
            return a

        for half in range(2):
            dense(32, 8, 128, hm, evac_up, parts=2)
            ev = residual_only
            if half:
                ev = residual
                xsq[0] = Squares(16)
            dense(16, 8, 128, hid, ev, parts=4)

        XR, YR = chunks(0, 16), chunks(4096, 16)
        CKV, KR, C_Q = chunks(8192, 4), chunks(9216, 1), chunks(9472, 6)
        GR, GA_ = chunks(11008, 16), chunks(15104, 16)
        WRG = big(13568, 4096)
        t_bfree = PE.tok()
        t_rg = Slot(WRG, sem("s_rg")).fill(SP, lambda e: e.dma_start(WRG, A["w_rg"]), t_bfree)
        TRIG = Slot(CS1[:, :, :], sem("s_trig"))
        t_trig = TRIG.fill(SP, lambda e: e.dma_start(CS1[:, :, :], A["trig2"]), qkr[15])
        MASK = Slot(con("mask"), sem("s_mask"))
        t_mask = MASK.fill(SP, lambda e: e.dma_start(con("mask"), A["mask2"]), atok[7])
        hn = hs_act()
        rms(X, 16, hn, lambda c: vec("attn_norm", c), 2048, xt, t_bfree, xsq[0])
        NSP = SM[:, 256:272]
        sp = [SM[:, 272 + 16 * i:288 + 16 * i] for i in range(4)]
        t = ts(NSP, vec("lam", 0, 16), -1.0, None, ALU.mult, None)
        log1p_exp(NSP, *sp, t)
        ts(NSP, NSP, -8.0, None, ALU.mult, None)
        c2t = {}
        LOW = BIG[:, 8192:8192 + 11 * T].rearrange("p (c t) -> p c t", t=T)

        def evac_low(c, ps, tok):
            c2t[c] = scopy(LOW[:, c, :], ps, tok, t_bfree)
            return c2t[c]

        dense(11, 8, 128, hn, evac_low, parts=2)
        xrt = [None] * 16
        ytk = [None] * 16

        def evac_xr(c, ps, tok):
            V.wait([t_bfree])
            xrt[c] = conv(XR[:, c, :], ps, lambda j: vec("conv_w2", 4 * c + j), vec("conv_b2", c), tok)
            return xrt[c]

        RA = BIG[:, 17664:18688].rearrange("p (c t) -> p c t", t=T)
        RI = BIG[:, 18688:19712].rearrange("p (c t) -> p c t", t=T)
        RM = TMP[:, 0, :].rearrange("p (c t) -> p c t", t=T)

        def rglru():
            t_prev = None
            for c0 in range(0, 16, 4):
                while xrt[c0 + 3] is None:
                    yield
                for j in range(4):
                    c = c0 + j
                    bk = score_banks.next()
                    mm(bk.ap[:, 0:T], WRG[:, c * 128:c * 128 + 128], XR[:, c, :], True, True, t_rg, xrt[c], bk.free)
                    p = mm(bk.ap[:, T:2 * T], WRG[:, 2048 + c * 128:2048 + c * 128 + 128], XR[:, c, :], True, True,
                           inc=True)
                    a = act(RA[:, j, :], bk.ap[:, 0:T], ACT.Sigmoid, p, t_prev, bias=vec("b_a", c))
                    a = act(RI[:, j, :], bk.ap[:, T:2 * T], ACT.Sigmoid, p, bias=vec("b_x", c))
                    bk.free = a
                    t = ts(RA[:, j, :], RA[:, j, :], NSP[:, c:c + 1], None, ALU.mult, None, a)
                    yield
                t = tt(RI, RI, XR[:, c0:c0 + 4, :], ALU.mult)
                a = act(RM, RA, ACT.Tanh, t, tmp_free[0], scale=-1.0)
                a = act(RA, RA, ACT.Exp, t)
                yield
                sq = TMP[:, 1, :].rearrange("p (c t) -> p c t", t=T)
                tt(sq, RA, RA, ALU.mult, a, tmp_free[1])
                t = tmp_free[1] = stt(RM, sq, 1.0, RM, ALU.add, ALU.mult)
                a = act(RM, RM, ACT.Sqrt, t)
                V(lambda e: e.memset(RM[:, :, 0:1], 1.0), a)
                t = tt(RI, RI, RM, ALU.mult)
                tmp_free[0] = t
                yield
                for j in range(4):
                    V(lambda e, j=j, c=c0 + j: e.tensor_tensor_scan(XR[:, c, :], RA[:, j, :], RI[:, j, :], 0.0,
                                                                   ALU.mult, ALU.add), p)
                    t_prev = ytk[c0 + j] = V.tok()
                yield

        g_rg = rglru()
        dense(16, 8, 128, hn, evac_xr, g_rg, parts=2)
        ym = [None] * 16

        def evac_yr(c, ps, tok):
            v = vcopy(YR[:, c, :], ps, tok)
            if c % 4 == 3:
                while ytk[c] is None:
                    next(g_rg)
                a = act(YR[:, c - 3:c + 1, :], YR[:, c - 3:c + 1, :], ACT.Gelu_apprx_tanh, v)
                t = tt(YR[:, c - 3:c + 1, :], YR[:, c - 3:c + 1, :], XR[:, c - 3:c + 1, :], ALU.mult, a, ytk[c])
                for j in range(c - 3, c + 1):
                    ym[j] = t
            return v

        dense(16, 8, 128, hn, evac_yr, g_rg, parts=2)
        t_wrg = PE.tok()

        def evac_gate(G_, o):
            def evac(c, ps, tok):
                gtok[o + c] = act(G_[:, c, :], ps, ACT.Sigmoid, tok, t_wrg, ym[15], bias=vec("b_gate", o + c))
                return gtok[o + c]
            return evac

        gtok = {}

        dense(16, 8, 128, hn, evac_gate(GR, 16), parts=2)
        t_hfree = dense(16, 8, 128, hn, evac_gate(GA_, 0), parts=2)
        ys = hs_act()
        for c in range(0, 16, 4):
            ys.cut(YR[:, c:c + 4, :], c, 4, ym[c], t_hfree)
        t_yfree = V.tok()

        def rope2(buf, tok):
            bk = score_banks.next()
            p = mm(bk.ap[:, 0:T], con("rot2"), buf, True, True, tok, bk.free, inc=True)
            rt = TMP[:, 1, 0:T]
            t = tt(rt, bk.ap[:, 0:T], CS1[:, 1, :], ALU.mult, p, tmp_free[1], t_trig)
            bk.free = t
            tt(buf, buf, CS1[:, 0, :], ALU.mult, p)
            t = tt(buf, buf, rt, ALU.add)
            tmp_free[1] = t
            return t

        t_kr = rope2(KR[:, 0, :], c2t[10])
        cqs = Act(bigr(4096, 6), bigr(4096 + 6 * T, 6))
        rms(C_Q, 6, cqs, lambda c: vec("q_norm", c), 768, [c2t[10]], t_yfree)
        cks = Act(bigr(4096 + 12 * T, 4), bigr(9472, 4))
        rms(CKV, 4, cks, lambda c: vec("kv_norm", c), 512, [c2t[10]], V.tok())
        xo = [None]

        def evac_yo(c, ps, tok):
            xo[0] = tt(XR[:, c, :], GR[:, c, :], ps, ALU.mult, tok, gtok[16 + c])
            return xo[0]

        t_yo = dense(16, 8, 128, ys, evac_yo, parts=2)
        QN = GR
        QP = HF[:, 0, 0:2048].rearrange("p (c t) -> p c t", t=T)
        K2 = HF[:, :, :].rearrange("p a b -> p (a b)")[:, 2048:6144].rearrange("p (c t) -> p c t", t=T)
        V2 = [HF[:, 1, 2048:4096], big(4096, 2048)]
        qt2 = {}
        qpt = [None] * 8

        def evac_uq(c, ps, tok):
            if c < 16:
                qt2[c] = scopy(QN[:, c, :], ps, tok, xo[0])
                return qt2[c]
            qt2[c] = scopy(QP[:, c - 16, :], ps, tok, t_yo)
            return qt2[c]

        t_uq = dense(24, 6, 128, cqs, evac_uq)
        k2t = {}

        def evac_k2(c, ps, tok):
            if c % 2 == 0:
                qpt[c // 2] = rope2(QP[:, c // 2, :], qt2[16 + c // 2])
            k2t[c] = scopy(K2[:, c, :], ps, tok, t_yo)
            return k2t[c]

        dense(8, 4, 256, cks, evac_k2)
        v2t = [None]

        def evac_v2(c0, n, ps, tok):
            for i in range(2):
                v2t[0] = scopy(V2[i][:, c0:c0 + n], ps[:, i, :], tok, t_yo, t_uq)
            return v2t[0]

        dense_tok(8, 4, 256, cks, evac_v2)
        MP = [Buf(big(6144, 512)), Buf(big(6656, 512))]
        MPT = Buf(TMP[:, 0, 0:384])
        mot = [None] * 16

        def mla(h):
            lo = 64 * (h % 2)

            def score(b, free):
                for i in range(2):
                    mm(b[:, i * T:i * T + T], QN[:, h, i * 128:i * 128 + 128], K2[:, h, :], True, False,
                       qt2[h], k2t[h], free, v2t[0])
                    t = mm(b[:, i * T:i * T + T], QP[lo:lo + 64, h // 2, i * 128:i * 128 + 128],
                           KR[lo:lo + 64, 0, :], False, True, qpt[h // 2], t_kr, inc=(i == 1))
                return t

            if h < 2:
                MP[h].free = t_uq
                V.wait([t_mask])
            if h == 0:
                MPT.free = tmp_free[0]
            den = SM[:, 256 + 8 * (h % 4):264 + 8 * (h % 4)]
            yield from softmax_head(MP[h % 2], MPT, den, score, 192.0 ** -0.5, con("mask"), True,
                                    lambda kt: V2[kt][:, h * 128:h * 128 + 128], QN[:, h, :], v2t[0])
            mot[h] = S.tok()

        g_ml = pipeline(mla(h) for h in range(16))
        drain(g_ml)
        tmp_free[0] = MPT.free
        t_hfree = PE.tok()
        os_ = hs_act()
        for c in range(0, 16, 4):
            os_.cut(QN[:, c:c + 4, :], c, 4, mot[c + 3], t_hfree)
        mix = Act(bigr(4096, 16), bigr(8192, 16))
        gt_free = [None]
        t_qnfree = V.tok()

        def evac_ao(c, ps, tok):
            t = tt(GA_[:, c, :], GA_[:, c, :], ps, ALU.mult, tok, gtok[c])
            tt(XR[:, c, :], XR[:, c, :], GA_[:, c, :], ALU.add)
            mix.cut(XR[:, c:c + 1, :], c, 1, V.tok(), t_qnfree)
            return t

        dense(16, 8, 128, os_, evac_ao, parts=2)
        xsq[0] = Squares(16)
        dense(16, 8, 128, mix, residual, parts=2)
        t_bfree = PE.tok()
        HN = big(0, 4096).rearrange("p (i d) -> p i d", i=2)
        SC = big(4096, 4096).rearrange("p (i c n) -> p i c n", i=2, c=16)
        ACC = big(4096, 4096).rearrange("p (i d) -> p i d", i=2)
        PQ = chunks(8192, 16)
        SK = big(12288, 2048)
        HK = chunks(14336, 16)
        t_sk = Slot(SK, sem("s_sk")).fill(SP, lambda e: e.dma_start(SK, A["subkeys"]), t_bfree, V.tok())
        hp = hs_act()
        t_hk = rms(X, 16, hp, lambda c: vec("ffn_norm", c), 2048, xt, t_bfree, xsq[0], HK)
        t_mixfree = V.tok()
        pqt = [None] * 16

        def evac_pq(c, ps, tok):
            pqt[c] = scopy(PQ[:, c, :], ps, tok, t_mixfree)
            return pqt[c]

        dense(16, 8, 128, hp, evac_pq, parts=2)
        t_pq = PE.tok()
        sct = [None, None]
        for i in range(2):
            for c0 in range(0, 16, 4):
                bk = score_banks.next()
                for c in range(c0, c0 + 4):
                    p = mm(bk.ap[:, (c - c0) * 128:(c - c0) * 128 + 128], PQ[:, c, i * 128:i * 128 + 128],
                           SK[:, c * 128:c * 128 + 128], True, True, pqt[c], t_sk, bk.free, inc=(c == c0 + 3))
                sct[i] = bk.free = scopy(SC[:, i, c0:c0 + 4, :].rearrange("p c n -> p (c n)"), bk.ap, p, t_mixfree)
        t_pqfree = PE.tok()
        for i in range(2):
            for c0 in range(0, 16, 4):
                for c in range(c0, c0 + 4):
                    p = tr(tr_bank.ap[:, (c - c0) * 128:(c - c0) * 128 + 128], HK[:, c, i * 128:i * 128 + 128],
                           tr_bank.free, t_hk, inc=(c == c0 + 3))
                tr_bank.free = t_hn = scopy(HN[:, i, c0 * 128:c0 * 128 + 512], tr_bank.ap, p, t_mixfree)
        t_hfree = PE.tok()

        tflat = TMP[:, :, :].rearrange("p a b -> p (a b)")
        TOPV = tflat[:, 0:256].rearrange("p (c k) -> p c k", k=16)
        TOPI = tflat[:, 256:512].bitcast(U32).rearrange("p (c k) -> p c k", k=16)
        TOPF = tflat[:, 512:768].rearrange("p (c k) -> p c k", k=16)
        BV = tflat[:, 768:896].rearrange("p (c k) -> p c k", k=16)
        BI = tflat[:, 896:1024].bitcast(U32).rearrange("p (c k) -> p c k", k=16)
        PI = tflat[:, 1024:1152].bitcast(U32)
        PF = tflat[:, 1152:1280]
        I1 = tflat[:, 1280:1408]
        I2 = tflat[:, 1408:1536]
        EX = CS1[:, 0, :].bitcast(U32).rearrange("p (i k) -> p i k", i=2)
        GA = sb("GA", [128, 2, 128])
        DOT = CS1[:, 1, :].rearrange("p (i k) -> p i k", i=2)
        CAND = HF[:, 0, 0:2048].rearrange("p (c t) -> p c t", t=T)
        EQ = HF[:, 1, 0:2048].rearrange("p (k j) -> p k j", j=16)

        def top16(vals, v16, i16):
            V(lambda e: e.max(v16[:, 0:8], vals))
            V(lambda e: e.max_index(i16[:, 0:8], v16[:, 0:8], vals))
            yield
            V(lambda e: e.match_replace(vals, v16[:, 0:8], vals, -3e38))
            V(lambda e: e.max(v16[:, 8:16], vals))
            V(lambda e: e.max_index(i16[:, 8:16], v16[:, 8:16], vals))
            yield

        ext = [None, None]

        def route(i):
            V.wait([sct[i], t_hfree])
            for c in range(16):
                yield from top16(SC[:, i, c, :], TOPV[:, c, :], TOPI[:, c, :])
            vcopy(TOPF[:, :, :], TOPI[:, :, :])
            for h in range(8):
                ca = CAND[:, h, :].rearrange("p (a b) -> p a b", a=16)
                tt(ca, TOPV[:, 2 * h, :].unsqueeze(2).to_broadcast([128, 16, 16]),
                   TOPV[:, 2 * h + 1, :].unsqueeze(1).to_broadcast([128, 16, 16]), ALU.add)
                yield from top16(CAND[:, h, :], BV[:, h, :], BI[:, h, :])
            bi = BI[:, :, :].rearrange("p h k -> p (h k)")
            for half, dst in ((0, I1), (1, I2)):
                if half == 0:
                    ts(PI[:, :], bi, 4, None, ALU.logical_shift_right, None)
                else:
                    ts(PI[:, :], bi, 15, None, ALU.bitwise_and, None)
                vcopy(PF[:, :], PI[:, :])
                tt(EQ, con("iota").unsqueeze(1).to_broadcast([128, 128, 16]),
                   PF[:, :].unsqueeze(2).to_broadcast([128, 128, 16]), ALU.is_equal)
                yield
                for h in range(8):
                    tt(EQ[:, 16 * h:16 * h + 16, :], EQ[:, 16 * h:16 * h + 16, :],
                       TOPF[:, 2 * h + half, :].unsqueeze(1).to_broadcast([128, 16, 16]), ALU.mult)
                    yield
                V(lambda e, dst=dst: e.tensor_reduce(dst[:, :], EQ, AXX, ALU.add))
                yield
            stt(I1[:, :], I1[:, :], 128.0, I2[:, :], ALU.mult, ALU.add)
            ext[i] = vcopy(EX[:, i, :], I1[:, :])
            g3 = GA[:, i, :].rearrange("p (h k) -> p h k", h=8)
            t = tt(g3, BV[:, :, :], BV[:, :, 0:1].to_broadcast([128, 8, 16]), ALU.subtract)
            t = act(g3, g3, ACT.Exp, t)
            V(lambda e: e.tensor_reduce(PF[:, 0:8], g3, AXX, ALU.add), t)
            recip(PF[:, 8:16], PF[:, 0:8])
            tt(g3, g3, PF[:, 8:16].unsqueeze(2).to_broadcast([128, 8, 16]), ALU.mult)

        gs = Ring([Slot(big(8192 + 2048 * i, 2048), sem(f"s_r{i}")) for i in range(4)])
        for s in gs.items:
            s.free = [t_pqfree, t_mixfree, t_hfree]

        def gather(table, i, k):
            s = gs.next()
            t = s.fill(G, lambda e, s=s: e.indirect_dma_start(
                out=s.ap, out_offset=None, in_=table,
                in_offset=bass.IndirectOffsetOnAxis(ap=EX[:, i, k:k + 1], axis=0)), ext[i])
            return s, t

        def dot(i, k):
            s, t = gather(A["peer_u"], i, k)
            s.free = V(lambda e: e.tensor_tensor_reduce(
                s.ap, s.ap, HN[:, i, :], 1.0, 0.0, ALU.mult, ALU.add, DOT[:, i, k:k + 1]), t, t_hn)

        def weigh(i):
            a = act(DOT[:, i, :], DOT[:, i, :], ACT.Gelu_apprx_tanh, V.tok())
            tt(GA[:, i, :], GA[:, i, :], DOT[:, i, :], ALU.mult, a)

        def values(i):
            for k in range(128):
                s, t = gather(A["peer_v"], i, k)
                if k == 0:
                    s.free = ts(ACC[:, i, :], s.ap, GA[:, i, 0:1], None, ALU.mult, None, t)
                else:
                    s.free = stt(ACC[:, i, :], s.ap, GA[:, i, k:k + 1], ACC[:, i, :], ALU.mult, ALU.add, t)
            return s.free

        PTF = HF[:, 0, 3072:3584].rearrange("p (c t) -> p c t", t=T)
        PRJ = chunks(16384, 16)
        t_p = Slot(PTF, sem("s_p")).fill(SP, lambda e: e.dma_start(PTF, A["pT"]), t_hfree)

        def evac_pr(c, ps, tok):
            return scopy(PRJ[:, c, :], ps, tok, t_hfree)

        def projection():
            pin = Act(HS[:, 0, 2048:2560].rearrange("p (c t) -> p c t", t=T),
                      HS[:, 0, 2560:3072].rearrange("p (c t) -> p c t", t=T))
            pin.cut(PTF, 0, 2, t_p, t_hfree)
            dense(4, 2, 512, pin, evac_pr)

        drain(route(0))
        r1 = route(1)
        for k in range(128):
            dot(0, k)
            if k == 10:
                projection()
            else:
                step(r1)
        drain(r1)
        weigh(0)
        for k in range(128):
            dot(1, k)
        weigh(1)
        acct = [values(0), values(1)]
        sq = Squares(16)
        for c0 in range(0, 16, 2):
            bk = score_banks.next()
            for c in range(c0, c0 + 2):
                for i in range(2):
                    p = tr(bk.ap[:, (c - c0) * T + i * 128:(c - c0) * T + i * 128 + 128],
                           ACC[:, i, c * 128:c * 128 + 128], bk.free, acct[i], inc=(c == c0 + 1 and i == 1))
            t = tt(X[:, c0:c0 + 2, :], X[:, c0:c0 + 2, :], bk.ap.rearrange("p (c t) -> p c t", t=T), ALU.add, p)
            xt[c0] = xt[c0 + 1] = bk.free = t
            sq.flush()
            sq.add(X[:, c0:c0 + 2, :], 2, t)
        hg = hs_act()
        rms(X, 16, hg, lambda c: vec("ple_norm", c), 2048, xt, V.tok(), sq)

        def evac_pg(c, ps, tok):
            a = act(GT[:, :], ps, ACT.Sigmoid, tok, gt_free[0])
            tt(PRJ[:, c, :], PRJ[:, c, :], GT[:, :], ALU.mult, a)
            gt_free[0] = xt[c] = tt(X[:, c, :], X[:, c, :], PRJ[:, c, :], ALU.add)
            sq.flush()
            sq.add(X[:, c:c + 1, :], 1, xt[c])
            return a

        sq = Squares(16)
        dense(16, 8, 128, hg, evac_pg, parts=2)
        assert taken[0] == len(STREAM)
        sq.flush()
        a = act(RS[:, 0, :], norm_bank.ap[:, 0:T], ACT.Sqrt, sq.last, rs_free[0], bias=con("eps"), scale=1.0 / 2048)
        recip(RS[:, 0, :], RS[:, 0, :], a)
        OUT = chunks(0, 16)
        outs = []
        so = [Slot(None, sem(f"s_out{i}")) for i in range(4)]
        for c in range(16):
            t = stt(OUT[:, c, :], X[:, c, :], vec("final_norm", c), RS[:, 0, :], ALU.mult, ALU.mult, V.tok())
            if c % 4 == 3:
                outs.append(so[c // 4].fill(SP, lambda e, c=c: e.dma_start(out[:, c - 3:c + 1, :],
                                                                          OUT[:, c - 3:c + 1, :]), t))
        SP.wait(outs)

        block = ctx.enter_context(nc.Block())

        @block.sync
        def _(e):
            SP.play(e)

        @block.gpsimd
        def _(e):
            G.play(e)

        @block.scalar
        def _(e):
            S.play(e)

        @block.vector
        def _(e):
            V.play(e)

        @block.tensor
        def _(e):
            PE.play(e)


def constants():
    p = np.arange(128)
    t = np.arange(256)
    c = {}
    c["ident"] = np.eye(128)
    c["ones"] = np.ones((128, 128))
    r1 = np.zeros((128, 128))
    r2 = np.zeros((128, 128))
    for h in range(2):
        for j in range(8):
            r1[64 * h + 8 + j, 64 * h + j] = -1
            r1[64 * h + j, 64 * h + 8 + j] = 1
        for j in range(32):
            r2[64 * h + 32 + j, 64 * h + j] = -1
            r2[64 * h + j, 64 * h + 32 + j] = 1
    c["rot1"], c["rot2"] = r1, r2
    c["triu"] = (p[None, :] >= p[:, None])
    s2 = np.zeros((128, 62))
    s2[p, 30 + p // 64] = 1
    s1 = np.zeros((128, 7))
    s1[:, 3] = 1
    c["sel2"], c["sel1"] = s2, s1
    q = p[:, None, None] + 128 * np.arange(2)[None, :, None]
    d = q - t[None, None, :]
    m = ((d >= 0) & (d <= 128)).astype(int) + ((d >= 0) & (d % 4 == 0)) + ((d >= 0) & (d % 16 == 0))
    c["mask"] = np.where(m > 0, np.log(np.maximum(m, 1)), NEG).reshape(128, 512)
    c["iota"] = np.broadcast_to(np.arange(16), (128, 16))
    f = (np.float32(500000.0) ** (np.float32(-2.0) * np.arange(8, dtype=np.float32) / np.float32(16))).astype(np.float32)
    c["invf"] = np.where(p % 64 < 16, f[p % 8], 0).reshape(128, 1)
    c["eps"] = np.full((128, 1), EPS)
    return np.concatenate([np.asarray(c[n], np.float32).reshape(128, k) for n, k in CONSTS], axis=1)


def constants2():
    p, t = np.arange(128), np.arange(256)
    d = p[:, None, None] + 128 * np.arange(2)[None, :, None] - t[None, None, :]
    inv = (1.0 / (np.float32(10000.0) ** (np.arange(32, dtype=np.float32) / np.float32(32)))).astype(np.float32)
    ang = (t.astype(np.float32)[None, :] * inv[p % 32][:, None]).astype(np.float32).astype(np.float64)
    trig = np.stack([np.cos(ang), np.sin(ang)], axis=1).astype(np.float32)
    return trig, np.where(d >= 0, 0.0, NEG).reshape(128, 512).astype(np.float32)


def kernel(**inp):
    import concourse.bacc as _bacc
    from concourse.bass_utils import run_bass_kernel_spmd as _run

    a = {k: np.asarray(v) for k, v in inp.items()}

    def fm(v):
        return v.reshape(-1, 128).T

    def blocks(w, cw):
        k, n = w.shape
        return np.ascontiguousarray(w.reshape(k // 128, 128, n // cw, cw).transpose(2, 1, 0, 3)
                                    .reshape(n // cw, 128, k // 128 * cw))

    def units(w):
        k, n = w.shape
        return np.ascontiguousarray(w.reshape(k // 1024, 8, 128, n // 128, 128).transpose(3, 0, 2, 1, 4)
                                    .reshape(n // 128 * (k // 1024), 128, 1024))

    def actT(x):
        t, d = x.shape
        return np.ascontiguousarray(x.T.reshape(d // 128, 128, t).transpose(1, 0, 2))

    w = a["w_in"][0]
    w2 = a["w_in_2"][0]
    ar = {
        "xT": actT(a["x"][0]), "memT": actT(a["mem"][0]), "positions": np.ascontiguousarray(a["positions"][0]),
        "pT": actT(a["p_2"][0, 0]), "consts": constants(),
        "w_qk": units(w[:, 0:2048]), "w_v": units(w[:, 2048:3072]), "w_z": units(w[:, 3072:4096]),
        "w_xbc": units(w[:, 4096:6144]),
        "w_dt": units(np.concatenate([w[:, 6144:6160], np.zeros((2048, 112), np.float32)], axis=1)),
        "w_out": units(a["w_out"][0]), "w_cq": units(a["w_cq"][0]),
        "w_ck": units(a["w_ckv"][0][:, 0:512]), "w_cv": units(a["w_ckv"][0][:, 512:1024]),
        "w_co": blocks(a["w_co"][0], 256),
    }
    ar["trig2"], ar["mask2"] = constants2()
    for h in range(2):
        ar[f"w_up{h}"] = units(a["w_up"][0][:, 4096 * h:4096 * h + 4096])
        ar[f"w_down{h}"] = units(a["w_down"][0][4096 * h:4096 * h + 4096])
    low = np.concatenate([w2[:, 768:1280], w2[:, 1280:1344], w2[:, 1280:1344], w2[:, 0:768]], axis=1)
    ar["w2_low"] = units(low)
    for n, o in (("xr", 1344), ("yr", 3392), ("ga", 5440), ("gr", 7488)):
        ar["w2_" + n] = units(w2[:, o:o + 2048])
    uq = a["w_uq_2"][0].reshape(768, 16, 192)
    ar["w2_uq"] = blocks(np.concatenate([uq[:, :, 0:128].reshape(768, 2048), uq[:, :, 128:].reshape(768, 1024)], 1), 128)
    ukv = a["w_ukv_2"][0].reshape(512, 16, 256)
    ar["w2_uk"] = blocks(ukv[:, :, 0:128].reshape(512, 2048), 256)
    ar["w2_uv"] = blocks(ukv[:, :, 128:].reshape(512, 2048), 256)
    ar["w_rg"] = np.ascontiguousarray(np.concatenate(
        [a[n][0].transpose(1, 0, 2).reshape(128, 2048) for n in ("w_rg_a_2", "w_rg_x_2")], axis=1))
    for n, s in (("rnn_o", "w_rnn_o_2"), ("ao", "w_attn_o_2"), ("out", "w_out_2"), ("pg", "w_ple_gate_2")):
        ar["w2_" + n] = units(a[s][0])
    ar["w2_pp"] = blocks(a["w_ple_proj_2"][0], 512)
    ar["w_pq"] = units(a["w_peer_q_2"][0])
    ar["subkeys"] = np.ascontiguousarray(a["peer_subkeys_2"][0].reshape(16, 128, 128).transpose(2, 0, 1).reshape(128, 2048))
    ar["peer_u"] = a["peer_u_2"][0]
    ar["peer_v"] = a["peer_v_2"][0]

    def pad(v):
        o = np.zeros((128, 1), np.float32)
        o[0:16, 0] = v
        return o

    vec = {
        "g_mix": fm(a["g_mix"]), "g_cross": fm(a["g_cross"]), "g_mem": fm(a["g_mem"]), "g_mlp": fm(a["g_mlp"]),
        "attn_norm": fm(a["attn_norm_2"]), "ffn_norm": fm(a["ffn_norm_2"]), "ple_norm": fm(a["ple_norm_2"]),
        "final_norm": fm(a["final_norm_2"]), "g_q": np.tile(a["g_q"][0], 2).reshape(128, 1),
        "g_k": np.tile(a["g_k"][0], 2).reshape(128, 1), "g_attn": fm(a["g_attn_out"]), "g_ssm": fm(a["g_ssm_out"]),
        "conv_w": a["conv_w"][0].reshape(4, 16, 128).transpose(2, 1, 0).reshape(128, 64), "conv_b": fm(a["conv_b"]),
        "d_skip": fm(np.repeat(a["d_skip"][0], 64)), "g_cq": a["g_cq"].T, "g_ck": a["g_ck"].T,
        "q_norm": fm(a["q_norm_2"]), "kv_norm": fm(a["kv_norm_2"]), "b_gate": fm(a["b_gate_2"]),
        "conv_w2": a["conv_w_2"][0].reshape(4, 16, 128).transpose(2, 1, 0).reshape(128, 64), "conv_b2": fm(a["conv_b_2"]),
        "b_a": fm(a["b_rg_a_2"]), "b_x": fm(a["b_rg_x_2"]), "lam": fm(a["lru_lambda_2"]),
        "dt_bias": pad(a["dt_bias"][0]), "a_log": pad(a["a_log"][0]),
    }
    ar["vecs"] = np.ascontiguousarray(np.concatenate([vec[n].reshape(128, k) for n, k in VECS], axis=1))

    nc = _bacc.Bacc("TRN2", target_bir_lowering=False, num_devices=1)
    arrays, ap = {}, {}
    for n, v in ar.items():
        arrays["in_" + n] = v
        ap[n] = nc.dram_tensor("in_" + n, v.shape, mybir.dt.from_np(v.dtype), kind="ExternalInput").ap()
    out = nc.dram_tensor("out_0", (128, 16, 256), F32, kind="ExternalOutput").ap()
    build(nc, ap, out)
    r = _run(nc, [arrays], core_ids=[0])
    got = r.results[0]["out_0"]
    return np.ascontiguousarray(got.transpose(2, 1, 0)).reshape(1, 256, 2048)
```

```python
from contextlib import ExitStack

import numpy as np
import concourse.bass as bass
from concourse import mybir

F32 = mybir.dt.float32
U32 = mybir.dt.uint32
I32 = mybir.dt.int32
R32 = mybir.dt.float32r
ALU = mybir.AluOpType
ACT = mybir.ActivationFunctionType
AXX = mybir.AxisListType.X

NEG = -1e30
EPS = 1e-6
T = 256
UNIT = 1024
NRAW = 5
NPAIR = 4

CONSTS = [("ident", 128), ("ones", 128), ("rot1", 128), ("rot2", 128), ("triu", 128),
          ("sel2", 62), ("sel1", 7), ("mask", 512),
          ("iota", 16), ("invf", 1), ("eps", 1)]
ORDER = [("w_qk", 32), ("w_v", 16), ("w_z", 16), ("w_xbc", 32), ("w_dt", 2), ("w_ck", 8), ("w_cv", 8), ("w_out", 32),
         ("w_cq", 8), ("w_co", 8), ("w_up0", 64), ("w_down0", 64), ("w_up1", 64), ("w_down1", 64), ("w2_low", 22),
         ("w2_xr", 32), ("w2_yr", 32), ("w2_gr", 32), ("w2_ga", 32), ("w2_rnn_o", 32), ("w2_uq", 24), ("w2_uk", 8),
         ("w2_uv", 8), ("w2_ao", 32), ("w2_out", 32), ("w_pq", 32), ("w2_pp", 4), ("w2_pg", 32)]
VECS = [("g_mix", 16), ("g_cross", 16), ("g_mem", 16), ("g_mlp", 16), ("attn_norm", 16), ("ffn_norm", 16),
        ("ple_norm", 16), ("final_norm", 16), ("g_q", 1), ("g_k", 1), ("g_attn", 8), ("g_ssm", 8),
        ("conv_w", 64), ("conv_b", 16), ("d_skip", 8), ("g_cq", 1), ("g_ck", 1), ("q_norm", 6), ("kv_norm", 4),
        ("b_gate", 32), ("conv_w2", 64), ("conv_b2", 16), ("b_a", 16), ("b_x", 16), ("lam", 16),
        ("dt_bias", 1), ("a_log", 1)]


def offsets(items):
    at, out = 0, {}
    for name, n in items:
        out[name] = (at, n)
        at += n
    return out, at


class Queue:

    def __init__(self, sem, chain):
        self.sem, self.chain, self.n, self.ops, self.seen = sem, chain, 0, [], {}

    def wait(self, toks):
        for t in toks:
            if t is None:
                continue
            if isinstance(t, list):
                self.wait(t)
                continue
            sem, v, key = t
            if self.seen.get(key, 0) < v:
                self.seen[key] = v
                self.ops.append((0, sem, v))

    def __call__(self, fn, *toks, inc=True):
        self.wait(toks)
        if self.chain and self.n:
            self.wait([self.tok()])
        self.ops.append((1, fn, inc))
        if inc:
            self.n += 1
        return self.tok()

    def tok(self):
        return (self.sem, self.n, id(self))

    def play(self, eng):
        for kind, a, b in self.ops:
            if kind == 0:
                eng.wait_ge(a, b)
            elif kind == 1:
                ins = a(eng)
                if b:
                    ins.then_inc(self.sem, 1)
            else:
                a(eng).then_inc(b, 16)


SLOTS = []


class Slot:

    def __init__(self, ap, sem):
        self.ap, self.sem, self.n, self.free = ap, sem, 0, None
        SLOTS.append(self)

    def fill(self, q, fn, *toks):
        q.wait([self.free, *toks])
        self.n += 16
        q.ops.append((2, fn, self.sem))
        return (self.sem, self.n, id(self))


class Bank:
    def __init__(self, ap):
        self.ap, self.free = ap, None


class Ring:
    def __init__(self, items):
        self.items, self.at = items, 0

    def next(self):
        self.at += 1
        return self.items[(self.at - 1) % len(self.items)]


def step(g):
    if g is not None:
        try:
            next(g)
        except StopIteration:
            pass


def drain(g):
    for _ in g:
        pass


def pipeline(gens):
    live = []
    gens = list(gens)
    while gens or live:
        if gens:
            live.append(gens.pop(0))
        for g in list(live):
            try:
                next(g)
            except StopIteration:
                live.remove(g)
        yield


def build(nc, A, out):
    ctx = ExitStack()
    with ctx:
        def sb(name, shape, dt=F32):
            return ctx.enter_context(nc.sbuf_tensor(name, shape, dt))

        def sem(name):
            return ctx.enter_context(nc.semaphore(name))

        co, ncon = offsets(CONSTS)
        vo, nvec = offsets(VECS)
        X = sb("X", [128, 16, T])
        with nc.sbuf_tensor("HF", [128, 2, 16 * T], F32) as HF:
            pass
        HS = sb("HS", [128, 2, 16 * T], R32)
        with nc.sbuf_tensor("BIG", [128, 20480], F32) as BIG:
            pass
        BIGR = sb("BIGR", [128, 20480], R32)
        RAW = sb("RAW", [128, NRAW, UNIT])
        HL = sb("HL", [128, NPAIR, 2, UNIT], R32)
        CON = sb("CON", [128, ncon])
        VEC = sb("VEC", [128, nvec])
        CS1 = sb("CS1", [128, 2, T])
        TMP = sb("TMP", [128, 2, 1024])
        RS = sb("RS", [128, 2, T])
        SM = sb("SM", [128, 512])
        GT = sb("GT", [128, T])
        PS = [ctx.enter_context(nc.psum_tensor(f"ps{i}", [128, 512], F32)) for i in range(8)]

        def con(name):
            o, n = co[name]
            return CON[:, o:o + n]

        def vec(name, i=0, n=1):
            o = vo[name][0] + i
            return VEC[:, o:o + n]

        PE = Queue(sem("s_pe"), False)
        V = Queue(sem("s_v"), True)
        S = Queue(sem("s_a"), True)
        G = Queue(sem("s_g"), True)
        SP = Queue(sem("s_sp"), False)

        raws = Ring([Slot(RAW[:, i, :], sem(f"s_w{i}")) for i in range(NRAW)])
        pairs = Ring([Bank(HL[:, i, :, :]) for i in range(NPAIR)])
        dense_banks = Ring([Bank(PS[i][:, :]) for i in range(3)])
        norm_bank = Bank(PS[3][:, :])
        score_banks = Ring([Bank(PS[4][:, :]), Bank(PS[5][:, :])])
        tr_bank = Bank(PS[6][:, :])
        out_bank = Bank(PS[7][:, :])
        tmp_free = [None, None]
        tmp_at = [0]
        rs_free = [None, None]
        rs_at = [0]

        def big(o, n):
            return BIG[:, o:o + n]

        def chunks(o, n):
            return BIG[:, o:o + n * T].rearrange("p (c t) -> p c t", t=T)

        def mm(o, l, r, start, stop, *toks, inc=False):
            return PE(lambda e: e.matmul(o, l, r, start=start, stop=stop, skip_group_check=True), *toks, inc=inc)

        def tr(o, i, *toks, inc=False):
            k = i.shape[0]
            return PE(lambda e: e.transpose(o, i, con("ident")[0:k, 0:k]), *toks, inc=inc)

        def act(o, i, f, *toks, bias=0.0, scale=1.0, acc=None):
            if acc is not None:
                return S(lambda e: e.activation(o, i, f, bias=bias, scale=scale, accum_out=acc), *toks)
            return S(lambda e: e.activation(o, i, f, bias=bias, scale=scale), *toks)

        def scopy(o, i, *toks):
            return S(lambda e: e.copy(o, i), *toks)

        def ts(o, i, s1, s2, op0, op1, *toks):
            if s2 is None:
                return V(lambda e: e.tensor_scalar(o, i, s1, None, op0), *toks)
            return V(lambda e: e.tensor_scalar(o, i, s1, s2, op0, op1), *toks)

        def tt(o, a, b, op, *toks):
            return V(lambda e: e.tensor_tensor(o, a, b, op), *toks)

        def stt(o, a, s, b, op0, op1, *toks):
            return V(lambda e: e.scalar_tensor_tensor(out=o, in0=a, scalar=s, in1=b, op0=op0, op1=op1), *toks)

        def vcopy(o, i, *toks):
            return V(lambda e: e.tensor_copy(o, i), *toks)

        def recip(o, i, *toks):
            return V(lambda e: e.reciprocal(o, i), *toks)

        def load(dst, src, name, q=None):
            s = Slot(dst, sem(name))
            return s.fill(q or S, lambda e: e.dma_start(dst, src))

        XQ = [Slot(X[:, 4 * i:4 * i + 4, :], sem(f"s_x{i}")) for i in range(4)]
        t_x = [q.fill(S, lambda e, i=i, q=q: e.dma_start(q.ap, A["xT"][:, 4 * i:4 * i + 4, :])) for i, q in enumerate(XQ)]
        t_con = load(CON[:, :], A["consts"], "s_con")
        t_vec = load(VEC[:, :], A["vecs"], "s_vec")
        POSI = big(0, T).bitcast(I32)
        t_pos = load(POSI, A["positions"].partition_broadcast(128), "s_pos")
        MEM = chunks(16384, 16)
        t_mem = load(MEM, A["memT"], "s_mem")
        for q in (PE, V, S):
            q.wait([t_con, t_vec])

        def split(src, hi, lo, toks, war=None):
            a = scopy(hi, src, toks, war)
            return tt(lo, src, hi.bitcast(F32), ALU.subtract, a)

        class Act:

            def __init__(self, hi, lo):
                self.hi, self.lo, self.tok = hi, lo, [None] * hi.shape[1]

            def cut(self, src, c0, n, toks, war=None):
                t = split(src, self.hi[:, c0:c0 + n, :], self.lo[:, c0:c0 + n, :], toks, war)
                for c in range(c0, c0 + n):
                    self.tok[c] = t
                return t

        def hs_act():
            return Act(*[HS[:, j, :].rearrange("p (c t) -> p c t", t=T) for j in range(2)])

        def bigr(o, n):
            return BIGR[:, o:o + n * T].rearrange("p (c t) -> p c t", t=T)

        loaded, cut_ = [], []

        def load_unit():
            if len(loaded) < len(STREAM):
                u = STREAM[len(loaded)]
                s = raws.next()
                n = u.shape[1]
                loaded.append((s, n, s.fill(SP, lambda e: e.dma_start(s.ap[:, 0:n], u))))

        def cut_unit():
            if len(cut_) < len(loaded):
                s, n, t = loaded[len(cut_)]
                p = pairs.next()
                s.free = split(s.ap[:, 0:n], p.ap[:, 0, 0:n], p.ap[:, 1, 0:n], t, p.free)
                cut_.append((p, n, s.free))

        taken = [0]

        def take(n):
            while len(cut_) <= min(taken[0] + NPAIR - 1, len(STREAM) - 1):
                if len(loaded) == len(cut_):
                    load_unit()
                cut_unit()
            while len(loaded) < min(len(cut_) + NRAW, len(STREAM)):
                load_unit()
            p, m, t = cut_[taken[0]]
            assert m == n, (taken[0], m, n)
            taken[0] += 1
            return p, t

        def products(o, p, w0, a, k, first, last, *toks, end=False):
            wh, wl = p.ap[:, 0, w0:w0 + 128], p.ap[:, 1, w0:w0 + 128]
            mm(o, wh, a.hi[:, k, :], first, False, a.tok[k], *toks)
            mm(o, wh, a.lo[:, k, :], False, False)
            return mm(o, wl, a.hi[:, k, :], False, last, inc=end)

        def dense(n, K, cw, a, evac, bg=None, parts=1):
            c = 0
            for _ in range(n):
                if parts > 1:
                    assert cw == 128
                b = None
                for u in range(parts):
                    p, t = take(K * cw)
                    for j in range(cw // 128):
                        if u == 0:
                            b = dense_banks.next()
                        for k in range(K):
                            last = products(b.ap[:, 0:T], p, k * cw + j * 128, a, u * K + k, u == 0 and k == 0,
                                            u == parts - 1 and k == K - 1, t, b.free, end=(k == K - 1))
                        p.free = last
                        if u == parts - 1:
                            b.free = evac(c, b.ap[:, 0:T], last)
                            c += 1
                    step(bg)
            return last

        def dense_tok(n, K, cw, a, evac, bg=None, parts=1):
            for c in range(n):
                bs = [dense_banks.next() for _ in range(2)]
                for u in range(parts):
                    p, t = take(K * cw)
                    for i, b in enumerate(bs):
                        o = b.ap[:, 0:cw]
                        for k in range(K):
                            wh, wl = p.ap[:, 0, k * cw:k * cw + cw], p.ap[:, 1, k * cw:k * cw + cw]
                            xh, xl = [x[:, u * K + k, i * 128:i * 128 + 128] for x in (a.hi, a.lo)]
                            end = u == parts - 1 and k == K - 1
                            mm(o, xh, wh, u == 0 and k == 0, False, t, b.free, a.tok[u * K + k])
                            mm(o, xh, wl, False, False)
                            last = mm(o, xl, wh, False, end, inc=(k == K - 1))
                        if u == parts - 1:
                            b.free = evac(i, c * cw, cw, o, last)
                    p.free = last
                    step(bg)
            return last

        class Squares:

            def __init__(self, nch):
                self.nch, self.n, self.todo = nch, 0, []

            def add(self, src, m, *toks):
                i = tmp_at[0] % 2
                tmp_at[0] += 1
                sq = TMP[:, i, 0:m * T].rearrange("p (c t) -> p c t", t=T)
                a = act(sq, src, ACT.Square, *toks, tmp_free[i])
                self.todo.append((i, sq, m, a))

            def flush(self):
                for i, sq, m, a in self.todo:
                    for k in range(m):
                        self.last = mm(norm_bank.ap[:, 0:T], con("ones"), sq[:, k, :], self.n == 0,
                                       self.n == self.nch - 1, a, norm_bank.free, inc=(k == m - 1))
                        self.n += 1
                    tmp_free[i] = self.last
                self.todo = []

        def tmp():
            i = tmp_at[0] % 2
            tmp_at[0] += 1
            return i, TMP[:, i, :].rearrange("p (c t) -> p c t", t=T)

        def rms(src, nch, dst, gain, n, toks, war=None, sq=None, keep=None, d0=0):
            if sq is None:
                sq = Squares(nch)
                for c0 in range(0, nch, 4):
                    m = min(4, nch - c0)
                    sq.add(src[:, c0:c0 + m, :], m, toks if len(toks) < nch else toks[c0:c0 + m])
                    sq.flush()
            sq.flush()
            r = rs_at[0] % 2
            rs_at[0] += 1
            a = act(RS[:, r, :], norm_bank.ap[:, 0:T], ACT.Sqrt, sq.last, rs_free[r], bias=con("eps"), scale=1.0 / n)
            norm_bank.free = a
            recip(RS[:, r, :], RS[:, r, :], a)
            groups, c = [], 0
            while c < nch:
                m = min(1 if c == 0 else 3 if c == 1 else 4, nch - c)
                groups.append((c, m))
                c += m
            for c0, m in groups:
                if keep is None:
                    i, buf = tmp()
                else:
                    i, buf = None, keep[:, c0:c0 + m, :]
                for c in range(m):
                    t = stt(buf[:, c, :], src[:, c0 + c, :], gain(c0 + c), RS[:, r, :], ALU.mult, ALU.mult, toks,
                            war if i is None else tmp_free[i])
                t = dst.cut(buf[:, 0:m, :], d0 + c0, m, t, war)
                if i is not None:
                    tmp_free[i] = t
            rs_free[r] = V.tok()
            return V.tok()

        def head_rstd(src, nch, per, n, toks, dst):
            rows = nch * per
            name, w = ("sel2", 30) if per == 2 else ("sel1", 3)
            sel = con(name)
            for c0 in range(0, nch, 4):
                i = tmp_at[0] % 2
                tmp_at[0] += 1
                sq = TMP[:, i, :].rearrange("p (c t) -> p c t", t=T)
                a = act(sq, src[:, c0:c0 + 4, :], ACT.Square, toks, tmp_free[i])
                for k in range(4):
                    c = c0 + k
                    p = mm(norm_bank.ap[0:rows, 0:T], sel[:, w - per * c:w - per * c + rows], sq[:, k, :],
                           c == 0, c == nch - 1, a, norm_bank.free, inc=(k == 3))
                tmp_free[i] = p
            a = act(dst, norm_bank.ap[0:rows, 0:T], ACT.Sqrt, p, bias=con("eps")[0:rows, :], scale=1.0 / n)
            norm_bank.free = a
            return recip(dst, dst, a)

        xsq = [None]

        def residual(c, ps, tok):
            xt[c] = tt(X[:, c, :], X[:, c, :], ps, ALU.add, tok)
            xsq[0].flush()
            xsq[0].add(X[:, c:c + 1, :], 1, xt[c])
            return xt[c]

        def residual_only(c, ps, tok):
            xt[c] = tt(X[:, c, :], X[:, c, :], ps, ALU.add, tok)
            return xt[c]

        xt = [t_x[c // 4] for c in range(16)]

        def softmax_head(P, PT, den, score, scale, mask, causal, vl, o, otok):
            b = score_banks.next()
            t = score(b.ap, b.free)
            if mask is not None:
                v = stt(P.ap, b.ap, scale, mask, ALU.mult, ALU.add, t, P.free)
                b.free = v
                V(lambda e: e.tensor_reduce(den[:, 0:2], P.ap.rearrange("p (a k) -> p a k", a=2), AXX, ALU.max,
                                            negate=True))
                m = V.tok()
                for i in range(2):
                    a = act(P.ap[:, i * T:i * T + T], P.ap[:, i * T:i * T + T], ACT.Exp, m,
                            bias=den[:, i:i + 1], acc=den[:, 2 + i:3 + i])
            else:
                V(lambda e: e.tensor_reduce(den[:, 0:2], b.ap.rearrange("p (a k) -> p a k", a=2), AXX, ALU.max,
                                            negate=True), t)
                m = ts(den[:, 0:2], den[:, 0:2], scale, None, ALU.mult, None)
                for i in range(2):
                    a = act(P.ap[:, i * T:i * T + T], b.ap[:, i * T:i * T + T], ACT.Exp, m, P.free,
                            bias=den[:, i:i + 1], scale=scale, acc=den[:, 2 + i:3 + i])
                b.free = a
            recip(den[:, 4:6], den[:, 2:4], a)
            for i in range(2):
                n = 128 if causal and i == 0 else T
                v = ts(P.ap[:, i * T:i * T + n], P.ap[:, i * T:i * T + n], den[:, 4 + i:5 + i], None, ALU.mult, None)
            yield
            yield
            blocks = [(0, 0), (1, 0), (1, 1)] if causal else [(0, 0), (1, 0), (0, 1), (1, 1)]
            for n, (i, k) in enumerate(blocks):
                t = tr(tr_bank.ap[:, n * 128:n * 128 + 128], P.ap[:, i * T + k * 128:i * T + k * 128 + 128],
                       v, tr_bank.free, inc=(n == len(blocks) - 1))
            P.free = t
            w = 128 * len(blocks)
            a = scopy(PT.ap[:, 0:w], tr_bank.ap[:, 0:w], t, PT.free)
            tr_bank.free = a
            yield
            lo, hi = o.base_partition() if callable(o.base_partition) else o.base_partition, o.shape[0]
            ob = out_bank.ap[lo:lo + hi, 0:T]
            mm(ob, vl(0), PT.ap[:, 0:T], True, False, a, out_bank.free, otok)
            if causal:
                t = mm(out_bank.ap[lo:lo + hi, 128:T], vl(1), PT.ap[:, T:T + 128], False, True, inc=True)
            else:
                t = mm(ob, vl(1), PT.ap[:, T:2 * T], False, True, inc=True)
            PT.free = t
            out_bank.free = scopy(o, ob, t)
            yield

        class Buf:
            def __init__(self, ap):
                self.ap, self.free = ap, None

        STREAM = [A[n][i] for n, c in ORDER for i in range(c)]
        h1 = hs_act()
        while len(cut_) < NPAIR:
            load_unit()
            cut_unit()
        rms(X, 16, h1, lambda c: vec("g_mix", c), 2048, xt)
        QT, KT = chunks(0, 8), chunks(2048, 8)
        QK = chunks(0, 16)
        VT = big(4096, 2048).rearrange("p (i d) -> p i d", i=2)
        Z = chunks(6144, 8)
        XBC = chunks(8192, 16)
        XST = big(12288, 2048).rearrange("p (i d) -> p i d", i=2)
        BT = big(14336, 512)

        t_posr = [None]
        t_cs = [None]

        def angles():
            POS = GT[:, :]
            t_posr[0] = vcopy(POS, POSI, t_pos)
            for j, ph in enumerate((0.25, 0.0)):
                ANG = CS1[:, j, :]
                KK = RS[:, 1, :]
                ts(ANG, POS, con("invf"), None, ALU.mult, None)
                ts(KK, ANG, float(np.float32(1 / (2 * np.pi))), ph, ALU.mult, ALU.add, rs_free[1])
                ts(KK, KK, 12582912.0, None, ALU.add, None)
                yield
                ts(KK, KK, 12582912.0, None, ALU.subtract, None)
                for cst in (6.28125, 0.0019340515136718750, 1.2556659146e-06):
                    stt(ANG, KK, -cst, ANG, ALU.mult, ALU.add)
                yield
                ts(ANG, ANG, float(np.float32(ph * 2 * np.pi)), float(np.float32(np.pi)), ALU.add, ALU.min)
                t = ts(ANG, ANG, float(-np.float32(np.pi)), None, ALU.max, None)
                rs_free[1] = t
                yield
            t_cs[0] = act(CS1[:, :, :], CS1[:, :, :], ACT.Sin, t)
            yield

        qkt = [None] * 16

        def evac_qk(c, ps, tok):
            qkt[c] = (vcopy if c % 2 else scopy)(QK[:, c, :], ps, tok, t_posr[0])
            return qkt[c]

        g_an = angles()
        next(g_an)
        dense(16, 8, 128, h1, evac_qk, g_an, parts=2)
        drain(g_an)

        qkr = [None] * 16

        def norm_rope():
            rb = SM[0:32, 0:T]
            t_r = head_rstd(QK, 16, 2, 64, [qkt[14], qkt[15]], rb)
            yield
            for c in range(16):
                b = score_banks.next()
                for j in range(2):
                    t = mm(b.ap[64 * j:64 * j + 64, 0:T], con("ident")[0:32, 2 * c + j:2 * c + j + 1].to_broadcast([32, 64]),
                           rb, True, True, t_r, b.free, inc=(j == 1))
                t = stt(QK[:, c, :], QK[:, c, :], vec("g_q" if c < 8 else "g_k"), b.ap[:, 0:T], ALU.mult, ALU.mult, t)
                b.free = t
                if c < 8:
                    t = ts(QK[:, c, :], QK[:, c, :], 0.125, None, ALU.mult, None)
                yield
                b = score_banks.next()
                p = mm(b.ap[:, 0:T], con("rot1"), QK[:, c, :], True, True, t, b.free, inc=True)
                rt = TMP[:, 1, 0:T]
                t = tt(rt, b.ap[:, 0:T], CS1[:, 1, :], ALU.mult, p, t_cs[0], tmp_free[1])
                b.free = t
                tt(QK[:, c, :], QK[:, c, :], CS1[:, 0, :], ALU.mult, p)
                qkr[c] = tt(QK[:, c, :], QK[:, c, :], rt, ALU.add)
                tmp_free[1] = qkr[c]
                yield

        g_nr = norm_rope()
        t_v = [None]

        def evac_v(i, c0, n, ps, tok):
            t_v[0] = scopy(VT[:, i, c0:c0 + n], ps, tok)
            return t_v[0]

        dense_tok(4, 4, 256, h1, evac_v, g_nr, parts=4)

        AP_ = [Buf(big(14848 + 512 * i, 512)) for i in range(3)]
        APT = [Buf(TMP[:, 1, 512:896])]
        APT[0].free = [tmp_free[0], tmp_free[1]]
        atok = [None] * 8

        def attn(h):
            c, lo = h // 2, 64 * (h % 2)
            q, k = QK[lo:lo + 64, c, :], QK[lo:lo + 64, 8 + c, :]

            def score(b, free):
                for i in range(2):
                    t = mm(b[:, i * T:i * T + T], q[:, i * 128:i * 128 + 128], k, True, True,
                           qkr[c], qkr[8 + c], free, inc=(i == 1))
                return t

            den = SM[:, 256 + 8 * (h % 4):264 + 8 * (h % 4)]
            yield from softmax_head(AP_[h % 3], APT[0], den, score, 1.0, con("mask"), True,
                                    lambda kt: VT[:, kt, h * 64:h * 64 + 64], q, t_v[0])
            atok[c] = S.tok()

        def all_attn():
            yield from g_nr
            yield from pipeline(attn(h) for h in range(16))

        g_at = all_attn()

        def evac_z(c, ps, tok):
            return vcopy(Z[:, c, :], ps, tok)

        dense(8, 8, 128, h1, evac_z, g_at, parts=2)
        t_z = V.tok()

        ctok = [None] * 16

        def conv(dst, ps, w, b, tok):
            t = ts(dst, ps, w(3), b, ALU.mult, ALU.add, tok)
            for j in (1, 2, 3):
                t = stt(dst[:, j:T], ps[:, 0:T - j], w(3 - j), dst[:, j:T], ALU.mult, ALU.add)
            return t

        def evac_xbc(c, ps, tok):
            ctok[c] = conv(XBC[:, c, :], ps, lambda j: vec("conv_w", 4 * c + j), vec("conv_b", c), tok)
            return ctok[c]

        dense(16, 8, 128, h1, evac_xbc, g_at, parts=2)
        DT = GT[0:16, :]

        def evac_dt(c, ps, tok):
            return ts(DT, ps[0:16, :], vec("dt_bias")[0:16, :], None, ALU.add, None, tok)

        t_hfree = dense(1, 8, 128, h1, evac_dt, g_at, parts=2)
        drain(g_at)
        SILU = ACT.Silu
        t_zs = [act(Z[:, i:i + 4, :], Z[:, i:i + 4, :], SILU, t_z) for i in (0, 4)][-1]
        t_xbc = [act(XBC[:, i:i + 4, :], XBC[:, i:i + 4, :], SILU, ctok[i + 3]) for i in (0, 4, 8, 12)]

        CK = chunks(2048, 4)
        CV = big(3072, 1024).rearrange("p (i d) -> p i d", i=2)

        def log1p_exp(x, m, y, z, p, tok):
            ts(m, x, 0.0, None, ALU.max, None, tok)
            ts(y, x, -1.0, None, ALU.mult, None)
            t = tt(y, x, y, ALU.min)
            t = act(y, y, ACT.Exp, t)
            ts(z, y, 2.0, None, ALU.add, None, t)
            recip(z, z)
            tt(y, y, z, ALU.mult)
            tt(z, y, y, ALU.mult)
            ts(p, z, 1.0 / 17, None, ALU.mult, None)
            for d in (15, 13, 11, 9, 7, 5, 3):
                stt(p, p, 1.0 / d, z, ALU.add, ALU.mult)
            stt(p, p, 1.0, y, ALU.add, ALU.mult)
            return stt(x, p, 2.0, m, ALU.mult, ALU.add)

        DA = SM[0:16, 0:T]
        ACS = RS[0:16, 0, :]
        ACT_ = SM[:, 320:352].rearrange("p (i h) -> p i h", i=2)
        DTT = SM[:, 352:384].rearrange("p (i h) -> p i h", i=2)
        SSB = 14848
        CB = big(SSB, 256).rearrange("p (i l) -> p i l", i=2)
        EE = [big(SSB + 256 + 256 * i, 256) for i in range(2)]
        WW = [Buf(big(SSB + 768 + 256 * i, 256)) for i in range(2)]
        ECS = [Buf(big(SSB + 1280 + 128 * i, 128)) for i in range(2)]
        XW = Buf(SM[:, 384:448])
        PV = Buf(SM[:, 448:512])
        sst = [None] * 8

        def ssd_pre():
            xx = [TMP[0:16, i, j * T:j * T + T] for i in range(2) for j in range(2)]
            V.wait([tmp_free[0], tmp_free[1]])
            t = log1p_exp(DT, *xx, None)
            tmp_free[0] = tmp_free[1] = t
            al = SM[0:16, 288:289]
            a = act(al, vec("a_log")[0:16, :], ACT.Exp, t)
            ts(DA, DT, al, -1.0, ALU.mult, ALU.mult, a)
            for i in range(2):
                V(lambda e, i=i: e.tensor_tensor_scan(ACS[:, i * 128:i * 128 + 128], con("ones")[0:16, :],
                                                      DA[:, i * 128:i * 128 + 128], 0.0, ALU.mult, ALU.add),
                  rs_free[0])
            t = V.tok()
            yield
            for src, dst in ((ACS, ACT_), (DT, DTT)):
                for i in range(2):
                    p = tr(tr_bank.ap[:, i * 16:i * 16 + 16], src[:, i * 128:i * 128 + 128], t, tr_bank.free,
                           inc=(i == 1))
                u = vcopy(dst, tr_bank.ap[:, 0:32].rearrange("p (i h) -> p i h", i=2), p)
                tr_bank.free = u
                yield
            for c0 in range(0, 8, 4):
                for i in range(2):
                    for c in range(c0, c0 + 4):
                        p = tr(tr_bank.ap[:, (c - c0) * 128:(c - c0) * 128 + 128], XBC[:, c, i * 128:i * 128 + 128],
                               t_xbc, tr_bank.free, inc=(c == c0 + 3))
                    u = vcopy(XST[:, i, c0 * 128:c0 * 128 + 512], tr_bank.ap[:, :], p)
                    tr_bank.free = u
                    yield
            for g in range(4):
                p = tr(tr_bank.ap[:, g * 128:g * 128 + 128], XBC[:, 8 + g, 0:128], t_xbc, tr_bank.free, inc=(g == 3))
            u = vcopy(BT, tr_bank.ap[:, :], p)
            tr_bank.free = u
            pre[0] = u
            yield

        pre = [None]
        cbt = [None]

        def ssd_head(h):
            g, c, lo = h // 4, h // 2, 64 * (h % 2)
            Bg, Cg = XBC[:, 8 + g, :], XBC[:, 12 + g, :]
            if h % 4 == 0:
                sb_ = score_banks.next()
                for i in range(2):
                    p = mm(sb_.ap[:, i * 128:i * 128 + 128], Bg[:, i * 128:i * 128 + 128],
                           Cg[:, i * 128:i * 128 + 128], True, True, sb_.free, t_xbc, pre[0], inc=(i == 1))
                sb_.free = cbt[0] = tt(CB, sb_.ap[:, 0:T].rearrange("p (i l) -> p i l", i=2),
                                       con("triu").unsqueeze(1).to_broadcast([128, 2, 128]), ALU.mult, p)
            k = h % 2
            sb_ = score_banks.next()
            p = mm(sb_.ap[:, 0:T], con("ident")[0:16, h:h + 1].to_broadcast([16, 128]), ACS, True, True,
                   sb_.free, pre[0], inc=True)
            E_ = EE[k]
            for i in range(2):
                t = ts(E_[:, i * 128:i * 128 + 128], sb_.ap[:, i * 128:i * 128 + 128], ACT_[:, i, h:h + 1], 0.0,
                       ALU.subtract, ALU.min, p)
            a = act(ECS[k].ap, sb_.ap[:, 128:T], ACT.Exp, t, ECS[k].free)
            sb_.free = a
            a = act(E_, E_, ACT.Exp, t)
            t_xw = ts(XW.ap, XST[:, 0, h * 64:h * 64 + 64], E_[:, 127:128], DTT[:, 0, h:h + 1], ALU.mult, ALU.mult, a,
                      XW.free)
            for i in range(2):
                t = stt(WW[k].ap[:, i * 128:i * 128 + 128], E_[:, i * 128:i * 128 + 128], DTT[:, i, h:h + 1],
                        CB[:, i, :], ALU.mult, ALU.mult, WW[k].free)
            t = tt(ECS[k].ap, ECS[k].ap, Cg[:, 128:T], ALU.mult, t_xbc)
            yield
            p = mm(tr_bank.ap[:, 0:64], BT[:, g * 128:g * 128 + 128], XW.ap, True, True, t_xw, tr_bank.free, inc=True)
            XW.free = p
            a = scopy(PV.ap, tr_bank.ap[:, 0:64], p, PV.free)
            tr_bank.free = a
            yield
            ob = out_bank.ap[lo:lo + 64, 0:T]
            xs = XST[:, :, h * 64:h * 64 + 64]
            mm(ob[:, 0:128], xs[:, 0, :], WW[k].ap[:, 0:128], True, True, t, out_bank.free)
            mm(ob[:, 128:T], xs[:, 1, :], WW[k].ap[:, 128:T], True, False)
            p = mm(ob[:, 128:T], PV.ap, ECS[k].ap, False, True, a, inc=True)
            WW[k].free = ECS[k].free = PV.free = p
            y = XBC[lo:lo + 64, c, :]
            t = stt(y, y, vec("d_skip", c)[lo:lo + 64, :], ob, ALU.mult, ALU.add, p)
            out_bank.free = t
            sst[c] = tt(Z[lo:lo + 64, c, :], Z[lo:lo + 64, c, :], y, ALU.mult, t_zs)
            yield

        def ssd():
            yield from ssd_pre()
            yield from pipeline(ssd_head(h) for h in range(16))
        g_ss = ssd()
        mh = hs_act()
        rms(MEM, 16, mh, lambda c: vec("g_mem", c), 2048, [t_mem], t_hfree)
        ckt = [None]

        def evac_ck(c, ps, tok):
            ckt[0] = scopy(CK[:, c, :], ps, tok)
            return ckt[0]

        dense(4, 8, 128, mh, evac_ck, g_ss, parts=2)
        t_cv = [None]

        def evac_cv(i, c0, n, ps, tok):
            t_cv[0] = scopy(CV[:, i, c0:c0 + n], ps, tok)
            return t_cv[0]

        t_hfree = dense_tok(2, 4, 256, mh, evac_cv, g_ss, parts=4)
        drain(g_ss)
        mx = hs_act()
        rms(QT, 8, mx, lambda c: vec("g_attn", c), 1024, [atok[6], atok[7]], t_hfree)
        for g in range(4):
            rms(Z[:, 2 * g:2 * g + 2, :], 2, mx, lambda c, g=g: vec("g_ssm", 2 * g + c), 256,
                [sst[2 * g], sst[2 * g + 1]], t_hfree, d0=8 + 2 * g)

        def head_norm(src, toks, g):
            rb = SM[0:4, 0:T]
            t_r = head_rstd(src, 4, 1, 128, toks, rb)
            for c in range(4):
                b = score_banks.next()
                t = mm(b.ap[:, 0:T], con("ident")[0:4, c:c + 1].to_broadcast([4, 128]), rb, True, True, t_r, b.free,
                       inc=True)
                t = stt(src[:, c, :], src[:, c, :], vec(g), b.ap[:, 0:T], ALU.mult, ALU.mult, t)
                b.free = t
            return t

        t_ckn = head_norm(CK, [ckt[0]], "g_ck")

        xsq[0] = Squares(16)
        t_hfree = dense(16, 8, 128, mx, residual, parts=2)
        hc = hs_act()
        rms(X, 16, hc, lambda c: vec("g_cross", c), 2048, xt, t_hfree, xsq[0])
        CQ = chunks(0, 4)
        cqt = [None]

        def evac_cq(c, ps, tok):
            cqt[0] = scopy(CQ[:, c, :], ps, tok)
            return cqt[0]

        t_hfree = dense(4, 8, 128, hc, evac_cq, parts=2)
        t_cqn = head_norm(CQ, [cqt[0]], "g_cq")
        CP = [Buf(big(4096 + 512 * i, 512)) for i in range(3)]
        CPT = Buf(big(5632, 512))
        cot = [None] * 4

        def cross(h):
            def score(b, free):
                for i in range(2):
                    t = mm(b[:, i * T:i * T + T], CQ[:, h, i * 128:i * 128 + 128], CK[:, h, :], True, True,
                           t_cqn, t_ckn, free, inc=(i == 1))
                return t

            den = SM[:, 256 + 8 * (h % 4):264 + 8 * (h % 4)]
            yield from softmax_head(CP[h % 3], CPT, den, score, 128.0 ** -0.5, None, False,
                                    lambda kt: CV[:, kt, h * 128:h * 128 + 128], CQ[:, h, :], t_cv[0])
            cot[h] = S.tok()

        drain(pipeline(cross(h) for h in range(4)))
        cx = hs_act()
        for c in range(4):
            cx.cut(CQ[:, c:c + 1, :], c, 1, cot[c], t_hfree)
        xsq[0] = Squares(16)
        t_hfree = dense(8, 4, 256, cx, residual)
        hm = hs_act()
        rms(X, 16, hm, lambda c: vec("g_mlp", c), 2048, xt, t_hfree, xsq[0])
        hid = Act(bigr(0, 32), bigr(8192, 32))
        t_cfree = [PE.tok(), V.tok(), S.tok()]

        def evac_up(c, ps, tok):
            i, buf = tmp()
            a = act(buf[:, 0, :], ps, ACT.Relu, tok, tmp_free[i])
            t = tt(buf[:, 1, :], buf[:, 0, :], buf[:, 0, :], ALU.mult, a)
            tmp_free[i] = hid.cut(buf[:, 1:2, :], c, 1, t, t_cfree)
            return a

        for half in range(2):
            dense(32, 8, 128, hm, evac_up, parts=2)
            ev = residual_only
            if half:
                ev = residual
                xsq[0] = Squares(16)
            dense(16, 8, 128, hid, ev, parts=4)

        XR, YR = chunks(0, 16), chunks(4096, 16)
        CKV, KR, C_Q = chunks(8192, 4), chunks(9216, 1), chunks(9472, 6)
        GR, GA_ = chunks(11008, 16), chunks(15104, 16)
        WRG = big(13568, 4096)
        t_bfree = PE.tok()
        t_rg = Slot(WRG, sem("s_rg")).fill(SP, lambda e: e.dma_start(WRG, A["w_rg"]), t_bfree)
        TRIG = Slot(CS1[:, :, :], sem("s_trig"))
        t_trig = TRIG.fill(SP, lambda e: e.dma_start(CS1[:, :, :], A["trig2"]), qkr[15])
        MASK = Slot(con("mask"), sem("s_mask"))
        t_mask = MASK.fill(SP, lambda e: e.dma_start(con("mask"), A["mask2"]), atok[7])
        hn = hs_act()
        rms(X, 16, hn, lambda c: vec("attn_norm", c), 2048, xt, t_bfree, xsq[0])
        NSP = SM[:, 256:272]
        sp = [SM[:, 272 + 16 * i:288 + 16 * i] for i in range(4)]
        t = ts(NSP, vec("lam", 0, 16), -1.0, None, ALU.mult, None)
        log1p_exp(NSP, *sp, t)
        ts(NSP, NSP, -8.0, None, ALU.mult, None)
        c2t = {}
        LOW = BIG[:, 8192:8192 + 11 * T].rearrange("p (c t) -> p c t", t=T)

        def evac_low(c, ps, tok):
            c2t[c] = scopy(LOW[:, c, :], ps, tok, t_bfree)
            return c2t[c]

        dense(11, 8, 128, hn, evac_low, parts=2)
        xrt = [None] * 16
        ytk = [None] * 16

        def evac_xr(c, ps, tok):
            V.wait([t_bfree])
            xrt[c] = conv(XR[:, c, :], ps, lambda j: vec("conv_w2", 4 * c + j), vec("conv_b2", c), tok)
            return xrt[c]

        RA = BIG[:, 17664:18688].rearrange("p (c t) -> p c t", t=T)
        RI = BIG[:, 18688:19712].rearrange("p (c t) -> p c t", t=T)
        RM = TMP[:, 0, :].rearrange("p (c t) -> p c t", t=T)

        def rglru():
            t_prev = None
            for c0 in range(0, 16, 4):
                while xrt[c0 + 3] is None:
                    yield
                for j in range(4):
                    c = c0 + j
                    bk = score_banks.next()
                    mm(bk.ap[:, 0:T], WRG[:, c * 128:c * 128 + 128], XR[:, c, :], True, True, t_rg, xrt[c], bk.free)
                    p = mm(bk.ap[:, T:2 * T], WRG[:, 2048 + c * 128:2048 + c * 128 + 128], XR[:, c, :], True, True,
                           inc=True)
                    a = act(RA[:, j, :], bk.ap[:, 0:T], ACT.Sigmoid, p, t_prev, bias=vec("b_a", c))
                    a = act(RI[:, j, :], bk.ap[:, T:2 * T], ACT.Sigmoid, p, bias=vec("b_x", c))
                    bk.free = a
                    t = ts(RA[:, j, :], RA[:, j, :], NSP[:, c:c + 1], None, ALU.mult, None, a)
                    yield
                t = tt(RI, RI, XR[:, c0:c0 + 4, :], ALU.mult)
                a = act(RM, RA, ACT.Tanh, t, tmp_free[0], scale=-1.0)
                a = act(RA, RA, ACT.Exp, t)
                yield
                sq = TMP[:, 1, :].rearrange("p (c t) -> p c t", t=T)
                tt(sq, RA, RA, ALU.mult, a, tmp_free[1])
                t = tmp_free[1] = stt(RM, sq, 1.0, RM, ALU.add, ALU.mult)
                a = act(RM, RM, ACT.Sqrt, t)
                V(lambda e: e.memset(RM[:, :, 0:1], 1.0), a)
                t = tt(RI, RI, RM, ALU.mult)
                tmp_free[0] = t
                yield
                for j in range(4):
                    V(lambda e, j=j, c=c0 + j: e.tensor_tensor_scan(XR[:, c, :], RA[:, j, :], RI[:, j, :], 0.0,
                                                                   ALU.mult, ALU.add), p)
                    t_prev = ytk[c0 + j] = V.tok()
                yield

        g_rg = rglru()
        dense(16, 8, 128, hn, evac_xr, g_rg, parts=2)
        ym = [None] * 16

        def evac_yr(c, ps, tok):
            v = vcopy(YR[:, c, :], ps, tok)
            if c % 4 == 3:
                while ytk[c] is None:
                    next(g_rg)
                a = act(YR[:, c - 3:c + 1, :], YR[:, c - 3:c + 1, :], ACT.Gelu_apprx_tanh, v)
                t = tt(YR[:, c - 3:c + 1, :], YR[:, c - 3:c + 1, :], XR[:, c - 3:c + 1, :], ALU.mult, a, ytk[c])
                for j in range(c - 3, c + 1):
                    ym[j] = t
            return v

        dense(16, 8, 128, hn, evac_yr, g_rg, parts=2)
        t_wrg = PE.tok()

        def evac_gate(G_, o):
            def evac(c, ps, tok):
                gtok[o + c] = act(G_[:, c, :], ps, ACT.Sigmoid, tok, t_wrg, ym[15], bias=vec("b_gate", o + c))
                return gtok[o + c]
            return evac

        gtok = {}

        dense(16, 8, 128, hn, evac_gate(GR, 16), parts=2)
        t_hfree = dense(16, 8, 128, hn, evac_gate(GA_, 0), parts=2)
        ys = hs_act()
        for c in range(0, 16, 4):
            ys.cut(YR[:, c:c + 4, :], c, 4, ym[c], t_hfree)
        t_yfree = V.tok()

        def rope2(buf, tok):
            bk = score_banks.next()
            p = mm(bk.ap[:, 0:T], con("rot2"), buf, True, True, tok, bk.free, inc=True)
            rt = TMP[:, 1, 0:T]
            t = tt(rt, bk.ap[:, 0:T], CS1[:, 1, :], ALU.mult, p, tmp_free[1], t_trig)
            bk.free = t
            tt(buf, buf, CS1[:, 0, :], ALU.mult, p)
            t = tt(buf, buf, rt, ALU.add)
            tmp_free[1] = t
            return t

        t_kr = rope2(KR[:, 0, :], c2t[10])
        cqs = Act(bigr(4096, 6), bigr(4096 + 6 * T, 6))
        rms(C_Q, 6, cqs, lambda c: vec("q_norm", c), 768, [c2t[10]], t_yfree)
        cks = Act(bigr(4096 + 12 * T, 4), bigr(9472, 4))
        rms(CKV, 4, cks, lambda c: vec("kv_norm", c), 512, [c2t[10]], V.tok())
        xo = [None]

        def evac_yo(c, ps, tok):
            xo[0] = tt(XR[:, c, :], GR[:, c, :], ps, ALU.mult, tok, gtok[16 + c])
            return xo[0]

        t_yo = dense(16, 8, 128, ys, evac_yo, parts=2)
        QN = GR
        QP = HF[:, 0, 0:2048].rearrange("p (c t) -> p c t", t=T)
        K2 = HF[:, :, :].rearrange("p a b -> p (a b)")[:, 2048:6144].rearrange("p (c t) -> p c t", t=T)
        V2 = [HF[:, 1, 2048:4096], big(4096, 2048)]
        qt2 = {}
        qpt = [None] * 8

        def evac_uq(c, ps, tok):
            if c < 16:
                qt2[c] = scopy(QN[:, c, :], ps, tok, xo[0])
                return qt2[c]
            qt2[c] = scopy(QP[:, c - 16, :], ps, tok, t_yo)
            return qt2[c]

        t_uq = dense(24, 6, 128, cqs, evac_uq)
        k2t = {}

        def evac_k2(c, ps, tok):
            if c % 2 == 0:
                qpt[c // 2] = rope2(QP[:, c // 2, :], qt2[16 + c // 2])
            k2t[c] = scopy(K2[:, c, :], ps, tok, t_yo)
            return k2t[c]

        dense(8, 4, 256, cks, evac_k2)
        v2t = [None]

        def evac_v2(i, c0, n, ps, tok):
            v2t[0] = scopy(V2[i][:, c0:c0 + n], ps, tok, t_yo, t_uq)
            return v2t[0]

        dense_tok(8, 4, 256, cks, evac_v2)
        MP = [Buf(big(6144, 512)), Buf(big(6656, 512)), Buf(big(7168, 512))]
        t_ckfree = PE.tok()
        MPT = Buf(TMP[:, 0, 0:384])
        mot = [None] * 16

        def mla(h):
            lo = 64 * (h % 2)

            def score(b, free):
                for i in range(2):
                    mm(b[:, i * T:i * T + T], QN[:, h, i * 128:i * 128 + 128], K2[:, h, :], True, False,
                       qt2[h], k2t[h], free, v2t[0])
                    t = mm(b[:, i * T:i * T + T], QP[lo:lo + 64, h // 2, i * 128:i * 128 + 128],
                           KR[lo:lo + 64, 0, :], False, True, qpt[h // 2], t_kr, inc=(i == 1))
                return t

            if h < 3:
                MP[h].free = t_ckfree
                V.wait([t_mask])
            if h == 0:
                MPT.free = tmp_free[0]
            den = SM[:, 256 + 8 * (h % 4):264 + 8 * (h % 4)]
            yield from softmax_head(MP[h % 3], MPT, den, score, 192.0 ** -0.5, con("mask"), True,
                                    lambda kt: V2[kt][:, h * 128:h * 128 + 128], QN[:, h, :], v2t[0])
            mot[h] = S.tok()

        g_ml = pipeline(mla(h) for h in range(16))
        drain(g_ml)
        tmp_free[0] = MPT.free
        t_hfree = PE.tok()
        os_ = hs_act()
        for c in range(0, 16, 4):
            os_.cut(QN[:, c:c + 4, :], c, 4, mot[c + 3], t_hfree)
        mix = Act(bigr(4096, 16), bigr(8192, 16))
        gt_free = [None]
        t_qnfree = V.tok()

        def evac_ao(c, ps, tok):
            t = tt(GA_[:, c, :], GA_[:, c, :], ps, ALU.mult, tok, gtok[c])
            tt(XR[:, c, :], XR[:, c, :], GA_[:, c, :], ALU.add)
            mix.cut(XR[:, c:c + 1, :], c, 1, V.tok(), t_qnfree)
            return t

        dense(16, 8, 128, os_, evac_ao, parts=2)
        xsq[0] = Squares(16)
        dense(16, 8, 128, mix, residual, parts=2)
        t_bfree = PE.tok()
        HN = big(0, 4096).rearrange("p (i d) -> p i d", i=2)
        SC = big(4096, 4096).rearrange("p (i c n) -> p i c n", i=2, c=16)
        ACC = big(4096, 4096).rearrange("p (i d) -> p i d", i=2)
        PQ = chunks(8192, 8)
        SK = big(10240, 2048)
        HK = chunks(14336, 16)
        t_sk = Slot(SK, sem("s_sk")).fill(SP, lambda e: e.dma_start(SK, A["subkeys"]), t_bfree, V.tok())
        hp = hs_act()
        t_hk = rms(X, 16, hp, lambda c: vec("ffn_norm", c), 2048, xt, t_bfree, xsq[0], HK)
        t_mixfree = V.tok()
        pqt = [None] * 16
        sct = [[None] * 4, [None] * 4]
        t_sc = [None] * 4
        t_hn = [None, None]

        def evac_pq(c, ps, tok):
            pqt[c] = scopy(PQ[:, c % 8, :], ps, tok, t_mixfree, t_sc[c // 4 - 2] if c >= 8 else None)
            return pqt[c]

        gs = Ring([Slot(big(12288 + 2048 * i, 2048), sem(f"s_r{i}")) for i in range(4)])

        def scoring():
            for i in range(2):
                for c0 in range(0, 16, 4):
                    for c in range(c0, c0 + 4):
                        p = tr(tr_bank.ap[:, (c - c0) * 128:(c - c0) * 128 + 128], HK[:, c, i * 128:i * 128 + 128],
                               tr_bank.free, t_hk, inc=(c == c0 + 3))
                    tr_bank.free = t_hn[i] = scopy(HN[:, i, c0 * 128:c0 * 128 + 512], tr_bank.ap, p, t_mixfree)
                    if c0 % 8:
                        yield
            for s in gs.items:
                s.free = [p, t_mixfree]
            for g in range(4):
                while pqt[4 * g + 3] is None:
                    yield
                for i in range(2):
                    bk = score_banks.next()
                    for j in range(4):
                        c = 4 * g + j
                        t_sc[g] = mm(bk.ap[:, j * 128:j * 128 + 128], PQ[:, c % 8, i * 128:i * 128 + 128],
                                     SK[:, c * 128:c * 128 + 128], True, True, pqt[c], t_sk, bk.free, inc=(j == 3))
                    sct[i][g] = bk.free = scopy(SC[:, i, 4 * g:4 * g + 4, :].rearrange("p c n -> p (c n)"), bk.ap,
                                                t_sc[g], t_mixfree)
                yield

        RT = TMP[:, 0, :]
        TOPV = RT[:, 0:32].rearrange("p (c k) -> p c k", k=16)
        TOPI = RT[:, 32:64].bitcast(U32).rearrange("p (c k) -> p c k", k=16)
        TOPF = RT[:, 64:96].rearrange("p (c k) -> p c k", k=16)
        BV, BI, PI = RT[:, 96:112], RT[:, 112:128].bitcast(U32), RT[:, 128:144].bitcast(U32)
        PF, I1, I2 = RT[:, 144:160], RT[:, 160:176], RT[:, 176:192]
        CAND, EQ = RT[:, 256:512], RT[:, 512:768].rearrange("p (k j) -> p k j", j=16)
        EX = CS1[:, 0, :].bitcast(U32).rearrange("p (i k) -> p i k", i=2)
        GA = sb("GA", [128, 2, 128])
        DOT = CS1[:, 1, :].rearrange("p (i k) -> p i k", i=2)
        ext = [[None] * 8, [None] * 8]

        def top16(vals, v16, i16):
            V(lambda e: e.max(v16[:, 0:8], vals))
            V(lambda e: e.max_index(i16[:, 0:8], v16[:, 0:8], vals))
            V(lambda e: e.match_replace(vals, v16[:, 0:8], vals, -3e38))
            V(lambda e: e.max(v16[:, 8:16], vals))
            V(lambda e: e.max_index(i16[:, 8:16], v16[:, 8:16], vals))

        def route(i, h):
            while sct[i][h // 2] is None:
                yield
            V.wait([sct[i][h // 2], tmp_free[0]])
            for half in range(2):
                top16(SC[:, i, 2 * h + half, :], TOPV[:, half, :], TOPI[:, half, :])
                yield
            vcopy(TOPF, TOPI)
            tt(CAND.rearrange("p (a b) -> p a b", a=16), TOPV[:, 0, :].unsqueeze(2).to_broadcast([128, 16, 16]),
               TOPV[:, 1, :].unsqueeze(1).to_broadcast([128, 16, 16]), ALU.add)
            top16(CAND, BV, BI)
            yield
            for half, dst in ((0, I1), (1, I2)):
                if half == 0:
                    ts(PI, BI, 4, None, ALU.logical_shift_right, None)
                else:
                    ts(PI, BI, 15, None, ALU.bitwise_and, None)
                vcopy(PF, PI)
                tt(EQ, con("iota").unsqueeze(1).to_broadcast([128, 16, 16]),
                   PF.unsqueeze(2).to_broadcast([128, 16, 16]), ALU.is_equal)
                tt(EQ, EQ, TOPF[:, half, :].unsqueeze(1).to_broadcast([128, 16, 16]), ALU.mult)
                V(lambda e, dst=dst: e.tensor_reduce(dst, EQ, AXX, ALU.add))
                yield
            stt(I1, I1, 128.0, I2, ALU.mult, ALU.add)
            ext[i][h] = vcopy(EX[:, i, 16 * h:16 * h + 16], I1)
            ts(GA[:, i, 16 * h:16 * h + 16], BV, BV[:, 0:1], None, ALU.subtract, None)

        def gather(table, i, k):
            s = gs.next()
            t = s.fill(G, lambda e, s=s: e.indirect_dma_start(
                out=s.ap, out_offset=None, in_=table,
                in_offset=bass.IndirectOffsetOnAxis(ap=EX[:, i, k:k + 1], axis=0)), ext[i][k // 16])
            return s, t

        def dot(i, k):
            s, t = gather(A["peer_u"], i, k)
            s.free = V(lambda e: e.tensor_tensor_reduce(
                s.ap, s.ap, HN[:, i, :], 1.0, 0.0, ALU.mult, ALU.add, DOT[:, i, k:k + 1]), t, t_hn[i])

        def dots():
            work = [(i, h) for h in range(8) for i in range(2)]
            for n, (i, h) in enumerate(work):
                while sct[i][h // 2] is None:
                    yield
                if n == 0:
                    drain(route(i, h))
                nxt = route(*work[n + 1]) if n < 15 else None
                for k in range(16):
                    dot(i, 16 * h + k)
                    step(nxt)
                    yield
                if nxt is not None:
                    while sct[work[n + 1][0]][work[n + 1][1] // 2] is None:
                        yield
                    drain(nxt)

        g_sc, g_do = scoring(), dots()

        def beside():
            while True:
                step(g_sc)
                step(g_do)
                yield

        t_hfree = dense(16, 8, 128, hp, evac_pq, beside(), parts=2)
        drain(g_sc)
        t_pqfree = [PE.tok(), S.tok()]

        def weigh(i):
            g3 = GA[:, i, :].rearrange("p (h k) -> p h k", h=8)
            a = act(g3, g3, ACT.Exp, V.tok())
            V(lambda e: e.tensor_reduce(RT[:, 768:776], g3, AXX, ALU.add), a)
            recip(RT[:, 776:784], RT[:, 768:776])
            tt(g3, g3, RT[:, 776:784].unsqueeze(2).to_broadcast([128, 8, 16]), ALU.mult)
            a = act(DOT[:, i, :], DOT[:, i, :], ACT.Gelu_apprx_tanh, V.tok())
            tmp_free[0] = tt(GA[:, i, :], GA[:, i, :], DOT[:, i, :], ALU.mult, a)

        def values(i):
            for k in range(128):
                s, t = gather(A["peer_v"], i, k)
                if k == 0:
                    s.free = ts(ACC[:, i, :], s.ap, GA[:, i, 0:1], None, ALU.mult, None, t)
                else:
                    s.free = stt(ACC[:, i, :], s.ap, GA[:, i, k:k + 1], ACC[:, i, :], ALU.mult, ALU.add, t)
            return s.free

        PTF = HF[:, 0, 3072:3584].rearrange("p (c t) -> p c t", t=T)
        PRJ = chunks(8192, 16)
        t_p = Slot(PTF, sem("s_p")).fill(SP, lambda e: e.dma_start(PTF, A["pT"]), t_hfree)

        def evac_pr(c, ps, tok):
            return scopy(PRJ[:, c, :], ps, tok, t_pqfree)

        def projection():
            pin = Act(HS[:, 0, 2048:2560].rearrange("p (c t) -> p c t", t=T),
                      HS[:, 0, 2560:3072].rearrange("p (c t) -> p c t", t=T))
            pin.cut(PTF, 0, 2, t_p, t_hfree)
            dense(4, 2, 512, pin, evac_pr)

        for n, _ in enumerate(g_do):
            if n == 10:
                projection()
        weigh(0)
        weigh(1)
        acct = [values(0), values(1)]
        sq = Squares(16)
        for c0 in range(0, 16, 2):
            bk = score_banks.next()
            for c in range(c0, c0 + 2):
                for i in range(2):
                    p = tr(bk.ap[:, (c - c0) * T + i * 128:(c - c0) * T + i * 128 + 128],
                           ACC[:, i, c * 128:c * 128 + 128], bk.free, acct[i], inc=(c == c0 + 1 and i == 1))
            t = tt(X[:, c0:c0 + 2, :], X[:, c0:c0 + 2, :], bk.ap.rearrange("p (c t) -> p c t", t=T), ALU.add, p)
            xt[c0] = xt[c0 + 1] = bk.free = t
            sq.flush()
            sq.add(X[:, c0:c0 + 2, :], 2, t)
        hg = hs_act()
        rms(X, 16, hg, lambda c: vec("ple_norm", c), 2048, xt, V.tok(), sq)

        def evac_pg(c, ps, tok):
            a = act(GT[:, :], ps, ACT.Sigmoid, tok, gt_free[0])
            tt(PRJ[:, c, :], PRJ[:, c, :], GT[:, :], ALU.mult, a)
            gt_free[0] = xt[c] = tt(X[:, c, :], X[:, c, :], PRJ[:, c, :], ALU.add)
            sq.flush()
            sq.add(X[:, c:c + 1, :], 1, xt[c])
            return a

        sq = Squares(16)
        dense(16, 8, 128, hg, evac_pg, parts=2)
        assert taken[0] == len(STREAM)
        sq.flush()
        a = act(RS[:, 0, :], norm_bank.ap[:, 0:T], ACT.Sqrt, sq.last, rs_free[0], bias=con("eps"), scale=1.0 / 2048)
        recip(RS[:, 0, :], RS[:, 0, :], a)
        OUT = chunks(0, 16)
        outs = []
        so = [Slot(None, sem(f"s_out{i}")) for i in range(4)]
        for c in range(16):
            t = stt(OUT[:, c, :], X[:, c, :], vec("final_norm", c), RS[:, 0, :], ALU.mult, ALU.mult, V.tok())
            if c % 4 == 3:
                outs.append(so[c // 4].fill(SP, lambda e, c=c: e.dma_start(out[:, c - 3:c + 1, :],
                                                                          OUT[:, c - 3:c + 1, :]), t))
        SP.wait(outs)

        block = ctx.enter_context(nc.Block())

        @block.sync
        def _(e):
            SP.play(e)

        @block.gpsimd
        def _(e):
            G.play(e)

        @block.scalar
        def _(e):
            S.play(e)

        @block.vector
        def _(e):
            V.play(e)

        @block.tensor
        def _(e):
            PE.play(e)


def constants():
    p = np.arange(128)
    t = np.arange(256)
    c = {}
    c["ident"] = np.eye(128)
    c["ones"] = np.ones((128, 128))
    r1 = np.zeros((128, 128))
    r2 = np.zeros((128, 128))
    for h in range(2):
        for j in range(8):
            r1[64 * h + 8 + j, 64 * h + j] = -1
            r1[64 * h + j, 64 * h + 8 + j] = 1
        for j in range(32):
            r2[64 * h + 32 + j, 64 * h + j] = -1
            r2[64 * h + j, 64 * h + 32 + j] = 1
    c["rot1"], c["rot2"] = r1, r2
    c["triu"] = (p[None, :] >= p[:, None])
    s2 = np.zeros((128, 62))
    s2[p, 30 + p // 64] = 1
    s1 = np.zeros((128, 7))
    s1[:, 3] = 1
    c["sel2"], c["sel1"] = s2, s1
    q = p[:, None, None] + 128 * np.arange(2)[None, :, None]
    d = q - t[None, None, :]
    m = ((d >= 0) & (d <= 128)).astype(int) + ((d >= 0) & (d % 4 == 0)) + ((d >= 0) & (d % 16 == 0))
    c["mask"] = np.where(m > 0, np.log(np.maximum(m, 1)), NEG).reshape(128, 512)
    c["iota"] = np.broadcast_to(np.arange(16), (128, 16))
    f = (np.float32(500000.0) ** (np.float32(-2.0) * np.arange(8, dtype=np.float32) / np.float32(16))).astype(np.float32)
    c["invf"] = np.where(p % 64 < 16, f[p % 8], 0).reshape(128, 1)
    c["eps"] = np.full((128, 1), EPS)
    return np.concatenate([np.asarray(c[n], np.float32).reshape(128, k) for n, k in CONSTS], axis=1)


def constants2():
    p, t = np.arange(128), np.arange(256)
    d = p[:, None, None] + 128 * np.arange(2)[None, :, None] - t[None, None, :]
    inv = (1.0 / (np.float32(10000.0) ** (np.arange(32, dtype=np.float32) / np.float32(32)))).astype(np.float32)
    ang = (t.astype(np.float32)[None, :] * inv[p % 32][:, None]).astype(np.float32).astype(np.float64)
    trig = np.stack([np.cos(ang), np.sin(ang)], axis=1).astype(np.float32)
    return trig, np.where(d >= 0, 0.0, NEG).reshape(128, 512).astype(np.float32)


def kernel(**inp):
    import concourse.bacc as _bacc
    from concourse.bass_utils import run_bass_kernel_spmd as _run

    a = {k: np.asarray(v) for k, v in inp.items()}

    def fm(v):
        return v.reshape(-1, 128).T

    def blocks(w, cw):
        k, n = w.shape
        return np.ascontiguousarray(w.reshape(k // 128, 128, n // cw, cw).transpose(2, 1, 0, 3)
                                    .reshape(n // cw, 128, k // 128 * cw))

    def units(w):
        k, n = w.shape
        return np.ascontiguousarray(w.reshape(k // 1024, 8, 128, n // 128, 128).transpose(3, 0, 2, 1, 4)
                                    .reshape(n // 128 * (k // 1024), 128, 1024))

    def actT(x):
        t, d = x.shape
        return np.ascontiguousarray(x.T.reshape(d // 128, 128, t).transpose(1, 0, 2))

    def units4(w):
        k, n = w.shape
        return np.ascontiguousarray(w.reshape(k // 512, 4, 128, n // 256, 256).transpose(3, 0, 2, 1, 4)
                                    .reshape(n // 256 * (k // 512), 128, 1024))

    w = a["w_in"][0]
    w2 = a["w_in_2"][0]
    ar = {
        "xT": actT(a["x"][0]), "memT": actT(a["mem"][0]), "positions": np.ascontiguousarray(a["positions"][0]),
        "pT": actT(a["p_2"][0, 0]), "consts": constants(),
        "w_qk": units(w[:, 0:2048]), "w_v": units4(w[:, 2048:3072]), "w_z": units(w[:, 3072:4096]),
        "w_xbc": units(w[:, 4096:6144]),
        "w_dt": units(np.concatenate([w[:, 6144:6160], np.zeros((2048, 112), np.float32)], axis=1)),
        "w_out": units(a["w_out"][0]), "w_cq": units(a["w_cq"][0]),
        "w_ck": units(a["w_ckv"][0][:, 0:512]), "w_cv": units4(a["w_ckv"][0][:, 512:1024]),
        "w_co": blocks(a["w_co"][0], 256),
    }
    ar["trig2"], ar["mask2"] = constants2()
    for h in range(2):
        ar[f"w_up{h}"] = units(a["w_up"][0][:, 4096 * h:4096 * h + 4096])
        ar[f"w_down{h}"] = units(a["w_down"][0][4096 * h:4096 * h + 4096])
    low = np.concatenate([w2[:, 768:1280], w2[:, 1280:1344], w2[:, 1280:1344], w2[:, 0:768]], axis=1)
    ar["w2_low"] = units(low)
    for n, o in (("xr", 1344), ("yr", 3392), ("ga", 5440), ("gr", 7488)):
        ar["w2_" + n] = units(w2[:, o:o + 2048])
    uq = a["w_uq_2"][0].reshape(768, 16, 192)
    ar["w2_uq"] = blocks(np.concatenate([uq[:, :, 0:128].reshape(768, 2048), uq[:, :, 128:].reshape(768, 1024)], 1), 128)
    ukv = a["w_ukv_2"][0].reshape(512, 16, 256)
    ar["w2_uk"] = blocks(ukv[:, :, 0:128].reshape(512, 2048), 256)
    ar["w2_uv"] = blocks(ukv[:, :, 128:].reshape(512, 2048), 256)
    ar["w_rg"] = np.ascontiguousarray(np.concatenate(
        [a[n][0].transpose(1, 0, 2).reshape(128, 2048) for n in ("w_rg_a_2", "w_rg_x_2")], axis=1))
    for n, s in (("rnn_o", "w_rnn_o_2"), ("ao", "w_attn_o_2"), ("out", "w_out_2"), ("pg", "w_ple_gate_2")):
        ar["w2_" + n] = units(a[s][0])
    ar["w2_pp"] = blocks(a["w_ple_proj_2"][0], 512)
    ar["w_pq"] = units(a["w_peer_q_2"][0])
    ar["subkeys"] = np.ascontiguousarray(a["peer_subkeys_2"][0].reshape(16, 128, 128).transpose(2, 0, 1).reshape(128, 2048))
    ar["peer_u"] = a["peer_u_2"][0]
    ar["peer_v"] = a["peer_v_2"][0]

    def pad(v):
        o = np.zeros((128, 1), np.float32)
        o[0:16, 0] = v
        return o

    vec = {
        "g_mix": fm(a["g_mix"]), "g_cross": fm(a["g_cross"]), "g_mem": fm(a["g_mem"]), "g_mlp": fm(a["g_mlp"]),
        "attn_norm": fm(a["attn_norm_2"]), "ffn_norm": fm(a["ffn_norm_2"]), "ple_norm": fm(a["ple_norm_2"]),
        "final_norm": fm(a["final_norm_2"]), "g_q": np.tile(a["g_q"][0], 2).reshape(128, 1),
        "g_k": np.tile(a["g_k"][0], 2).reshape(128, 1), "g_attn": fm(a["g_attn_out"]), "g_ssm": fm(a["g_ssm_out"]),
        "conv_w": a["conv_w"][0].reshape(4, 16, 128).transpose(2, 1, 0).reshape(128, 64), "conv_b": fm(a["conv_b"]),
        "d_skip": fm(np.repeat(a["d_skip"][0], 64)), "g_cq": a["g_cq"].T, "g_ck": a["g_ck"].T,
        "q_norm": fm(a["q_norm_2"]), "kv_norm": fm(a["kv_norm_2"]), "b_gate": fm(a["b_gate_2"]),
        "conv_w2": a["conv_w_2"][0].reshape(4, 16, 128).transpose(2, 1, 0).reshape(128, 64), "conv_b2": fm(a["conv_b_2"]),
        "b_a": fm(a["b_rg_a_2"]), "b_x": fm(a["b_rg_x_2"]), "lam": fm(a["lru_lambda_2"]),
        "dt_bias": pad(a["dt_bias"][0]), "a_log": pad(a["a_log"][0]),
    }
    ar["vecs"] = np.ascontiguousarray(np.concatenate([vec[n].reshape(128, k) for n, k in VECS], axis=1))

    nc = _bacc.Bacc("TRN2", target_bir_lowering=False, num_devices=1)
    arrays, ap = {}, {}
    for n, v in ar.items():
        arrays["in_" + n] = v
        ap[n] = nc.dram_tensor("in_" + n, v.shape, mybir.dt.from_np(v.dtype), kind="ExternalInput").ap()
    out = nc.dram_tensor("out_0", (128, 16, 256), F32, kind="ExternalOutput").ap()
    build(nc, ap, out)
    r = _run(nc, [arrays], core_ids=[0])
    got = r.results[0]["out_0"]
    return np.ascontiguousarray(got.transpose(2, 1, 0)).reshape(1, 256, 2048)
```

```python
from contextlib import ExitStack

import numpy as np
import concourse.bass as bass
from concourse import mybir

F32 = mybir.dt.float32
U32 = mybir.dt.uint32
I32 = mybir.dt.int32
R32 = mybir.dt.float32r
ALU = mybir.AluOpType
ACT = mybir.ActivationFunctionType
AXX = mybir.AxisListType.X

NEG = -1e30
EPS = 1e-6
T = 256
UNIT = 1024
NRAW = 5
NPAIR = 4

CONSTS = [("ident", 128), ("ones", 128), ("rot1", 128), ("rot2", 128), ("triu", 128),
          ("sel2", 62), ("sel1", 7), ("mask", 512),
          ("iota", 16), ("invf", 1), ("eps", 1)]
ORDER = [("w_qk", 32), ("w_v", 16), ("w_dt", 2), ("w_z", 16), ("w_xbc", 32), ("w_ck", 8), ("w_cv", 8), ("w_out", 32),
         ("w_cq", 8), ("w_co", 8), ("w_up0", 64), ("w_down0", 64), ("w_up1", 64), ("w_down1", 64), ("w2_low", 22),
         ("w2_xr", 32), ("w2_yr", 32), ("w2_gr", 32), ("w2_ga", 32), ("w2_rnn_o", 32), ("w2_uq", 24), ("w2_uk", 8),
         ("w2_uv", 8), ("w2_ao", 32), ("w2_out", 32), ("w_pq", 32), ("w2_pp", 4), ("w2_pg", 32)]
VECS = [("g_mix", 16), ("g_cross", 16), ("g_mem", 16), ("g_mlp", 16), ("attn_norm", 16), ("ffn_norm", 16),
        ("ple_norm", 16), ("final_norm", 16), ("g_q", 1), ("g_k", 1), ("g_attn", 8), ("g_ssm", 8),
        ("conv_w", 64), ("conv_b", 16), ("d_skip", 8), ("g_cq", 1), ("g_ck", 1), ("q_norm", 6), ("kv_norm", 4),
        ("b_gate", 32), ("conv_w2", 64), ("conv_b2", 16), ("b_a", 16), ("b_x", 16), ("lam", 16),
        ("dt_bias", 1), ("a_log", 1)]


def offsets(items):
    at, out = 0, {}
    for name, n in items:
        out[name] = (at, n)
        at += n
    return out, at


class Queue:

    def __init__(self, sem, chain):
        self.sem, self.chain, self.n, self.ops, self.seen = sem, chain, 0, [], {}

    def wait(self, toks):
        for t in toks:
            if t is None:
                continue
            if isinstance(t, list):
                self.wait(t)
                continue
            sem, v, key = t
            if self.seen.get(key, 0) < v:
                self.seen[key] = v
                self.ops.append((0, sem, v))

    def __call__(self, fn, *toks, inc=True):
        self.wait(toks)
        if self.chain and self.n:
            self.wait([self.tok()])
        self.ops.append((1, fn, inc))
        if inc:
            self.n += 1
        return self.tok()

    def tok(self):
        return (self.sem, self.n, id(self))

    def play(self, eng):
        for kind, a, b in self.ops:
            if kind == 0:
                eng.wait_ge(a, b)
            elif kind == 1:
                ins = a(eng)
                if b:
                    ins.then_inc(self.sem, 1)
            else:
                a(eng).then_inc(b, 16)


SLOTS = []


class Slot:

    def __init__(self, ap, sem):
        self.ap, self.sem, self.n, self.free = ap, sem, 0, None
        SLOTS.append(self)

    def fill(self, q, fn, *toks):
        q.wait([self.free, *toks])
        self.n += 16
        q.ops.append((2, fn, self.sem))
        return (self.sem, self.n, id(self))


class Bank:
    def __init__(self, ap):
        self.ap, self.free = ap, None


class Ring:
    def __init__(self, items):
        self.items, self.at = items, 0

    def next(self):
        self.at += 1
        return self.items[(self.at - 1) % len(self.items)]


def step(g):
    if g is not None:
        try:
            next(g)
        except StopIteration:
            pass


def drain(g):
    for _ in g:
        pass


def pipeline(gens):
    live = []
    gens = list(gens)
    while gens or live:
        if gens:
            live.append(gens.pop(0))
        for g in list(live):
            try:
                next(g)
            except StopIteration:
                live.remove(g)
        yield


def twice(g):
    for _ in g:
        step(g)
        yield


def build(nc, A, out):
    ctx = ExitStack()
    with ctx:
        def sb(name, shape, dt=F32):
            return ctx.enter_context(nc.sbuf_tensor(name, shape, dt))

        def sem(name):
            return ctx.enter_context(nc.semaphore(name))

        co, ncon = offsets(CONSTS)
        vo, nvec = offsets(VECS)
        X = sb("X", [128, 16, T])
        with nc.sbuf_tensor("HF", [128, 2, 16 * T], F32) as HF:
            pass
        HS = sb("HS", [128, 2, 16 * T], R32)
        with nc.sbuf_tensor("BIG", [128, 20480], F32) as BIG:
            pass
        BIGR = sb("BIGR", [128, 20480], R32)
        RAW = sb("RAW", [128, NRAW, UNIT])
        HL = sb("HL", [128, NPAIR, 2, UNIT], R32)
        CON = sb("CON", [128, ncon])
        VEC = sb("VEC", [128, nvec])
        CS1 = sb("CS1", [128, 2, T])
        TMP = sb("TMP", [128, 2, 1024])
        RS = sb("RS", [128, 2, T])
        SM = sb("SM", [128, 512])
        GT = sb("GT", [128, T])
        KEEP = sb("KEEP", [128, 4, T])
        RX, CX = KEEP[:, 2, :], KEEP[:, 3, :]
        PS = [ctx.enter_context(nc.psum_tensor(f"ps{i}", [128, 512], F32)) for i in range(8)]

        def con(name):
            o, n = co[name]
            return CON[:, o:o + n]

        def vec(name, i=0, n=1):
            o = vo[name][0] + i
            return VEC[:, o:o + n]

        PE = Queue(sem("s_pe"), False)
        V = Queue(sem("s_v"), True)
        S = Queue(sem("s_a"), True)
        G = Queue(sem("s_g"), True)
        SP = Queue(sem("s_sp"), False)

        raws = Ring([Slot(RAW[:, i, :], sem(f"s_w{i}")) for i in range(NRAW)])
        pairs = Ring([Bank(HL[:, i, :, :]) for i in range(NPAIR)])
        dense_banks = Ring([Bank(PS[i][:, :]) for i in range(3)])
        norm_bank = Bank(PS[3][:, :])
        score_banks = Ring([Bank(PS[4][:, :]), Bank(PS[5][:, :])])
        tr_bank = Bank(PS[6][:, :])
        out_bank = Bank(PS[7][:, :])
        tmp_free = [None, None]
        tmp_at = [0]
        rs_free = [None, None]
        rs_at = [0]

        def big(o, n):
            return BIG[:, o:o + n]

        def chunks(o, n):
            return BIG[:, o:o + n * T].rearrange("p (c t) -> p c t", t=T)

        def mm(o, l, r, start, stop, *toks, inc=False):
            return PE(lambda e: e.matmul(o, l, r, start=start, stop=stop, skip_group_check=True), *toks, inc=inc)

        def tr(o, i, *toks, inc=False):
            k = i.shape[0]
            return PE(lambda e: e.transpose(o, i, con("ident")[0:k, 0:k]), *toks, inc=inc)

        def act(o, i, f, *toks, bias=0.0, scale=1.0, acc=None):
            if acc is not None:
                return S(lambda e: e.activation(o, i, f, bias=bias, scale=scale, accum_out=acc), *toks)
            return S(lambda e: e.activation(o, i, f, bias=bias, scale=scale), *toks)

        def scopy(o, i, *toks):
            return S(lambda e: e.copy(o, i), *toks)

        def ts(o, i, s1, s2, op0, op1, *toks):
            if s2 is None:
                return V(lambda e: e.tensor_scalar(o, i, s1, None, op0), *toks)
            return V(lambda e: e.tensor_scalar(o, i, s1, s2, op0, op1), *toks)

        def tt(o, a, b, op, *toks):
            return V(lambda e: e.tensor_tensor(o, a, b, op), *toks)

        def stt(o, a, s, b, op0, op1, *toks):
            return V(lambda e: e.scalar_tensor_tensor(out=o, in0=a, scalar=s, in1=b, op0=op0, op1=op1), *toks)

        def vcopy(o, i, *toks):
            return V(lambda e: e.tensor_copy(o, i), *toks)

        def recip(o, i, *toks):
            return V(lambda e: e.reciprocal(o, i), *toks)

        def load(dst, src, name, q=None):
            s = Slot(dst, sem(name))
            return s.fill(q or S, lambda e: e.dma_start(dst, src))

        t_con = load(CON[:, :], A["consts"], "s_con")
        t_vec = load(VEC[:, :], A["vecs"], "s_vec")
        XQ = [Slot(X[:, 4 * i:4 * i + 4, :], sem(f"s_x{i}")) for i in range(4)]
        t_x = [q.fill(S, lambda e, i=i, q=q: e.dma_start(q.ap, A["xT"][:, 4 * i:4 * i + 4, :])) for i, q in enumerate(XQ)]
        POSI = big(0, T).bitcast(I32)
        t_pos = load(POSI, A["positions"].partition_broadcast(128), "s_pos")
        MEM = chunks(16384, 16)
        MEMQ, t_mem = Slot(MEM, sem("s_mem")), [None]
        for q in (PE, V, S):
            q.wait([t_con, t_vec])

        def split(src, hi, lo, toks, war=None):
            a = scopy(hi, src, toks, war)
            return tt(lo, src, hi.bitcast(F32), ALU.subtract, a)

        class Act:

            def __init__(self, hi, lo):
                self.hi, self.lo, self.tok = hi, lo, [None] * hi.shape[1]

            def cut(self, src, c0, n, toks, war=None):
                t = split(src, self.hi[:, c0:c0 + n, :], self.lo[:, c0:c0 + n, :], toks, war)
                for c in range(c0, c0 + n):
                    self.tok[c] = t
                return t

        def hs_act():
            return Act(*[HS[:, j, :].rearrange("p (c t) -> p c t", t=T) for j in range(2)])

        def bigr(o, n):
            return BIGR[:, o:o + n * T].rearrange("p (c t) -> p c t", t=T)

        loaded, high, cut_ = [], [], []

        def load_unit():
            if len(loaded) < len(STREAM):
                u = STREAM[len(loaded)]
                s = raws.next()
                n = u.shape[1]
                loaded.append((s, n, s.fill(SP, lambda e: e.dma_start(s.ap[:, 0:n], u))))

        def high_unit():
            s, n, t = loaded[len(high)]
            p = pairs.next()
            high.append((s, n, p, scopy(p.ap[:, 0, 0:n], s.ap[:, 0:n], t, p.free)))

        def low_unit():
            s, n, p, t = high[len(cut_)]
            s.free = tt(p.ap[:, 1, 0:n], s.ap[:, 0:n], p.ap[:, 0, 0:n].bitcast(F32), ALU.subtract, t)
            cut_.append((p, n, s.free))

        taken = [0]

        def take(n):
            end = len(STREAM)
            while len(high) < min(taken[0] + NPAIR - 1, end):
                high_unit()
            while len(cut_) < min(taken[0] + NPAIR - 1, end):
                low_unit()
                load_unit()
            if len(high) < min(taken[0] + NPAIR, end):
                high_unit()
            p, m, t = cut_[taken[0]]
            assert m == n, (taken[0], m, n)
            taken[0] += 1
            return p, t

        def products(o, p, w0, a, k, first, last, *toks, end=False):
            wh, wl = p.ap[:, 0, w0:w0 + 128], p.ap[:, 1, w0:w0 + 128]
            mm(o, wh, a.hi[:, k, :], first, False, a.tok[k], *toks)
            mm(o, wh, a.lo[:, k, :], False, False)
            return mm(o, wl, a.hi[:, k, :], False, last, inc=end)

        def dense(n, K, cw, a, evac, bg=None, parts=1):
            c = 0
            for block in range(n):
                if parts > 1:
                    assert cw == 128
                b = None
                for u in range(parts):
                    p, t = take(K * cw)
                    for j in range(cw // 128):
                        if u == 0:
                            b = dense_banks.next()
                        x, k0 = (a[u], 0) if isinstance(a, list) else (a, u * K)
                        for k in range(K):
                            last = products(b.ap[:, 0:T], p, k * cw + j * 128, x, k0 + k, u == 0 and k == 0,
                                            u == parts - 1 and k == K - 1, t, b.free, end=(k == K - 1))
                        p.free = last
                        if u == parts - 1:
                            b.free = evac(c, b.ap[:, 0:T], last)
                            c += 1
                    if block < n - 1 or u < parts - 1:
                        step(bg)
            return last

        def dense_tok(n, K, cw, a, evac, bg=None, parts=1):
            for c in range(n):
                bs = [dense_banks.next() for _ in range(2)]
                for u in range(parts):
                    p, t = take(K * cw)
                    for i, b in enumerate(bs):
                        o = b.ap[:, 0:cw]
                        for k in range(K):
                            wh, wl = p.ap[:, 0, k * cw:k * cw + cw], p.ap[:, 1, k * cw:k * cw + cw]
                            xh, xl = [x[:, u * K + k, i * 128:i * 128 + 128] for x in (a.hi, a.lo)]
                            end = u == parts - 1 and k == K - 1
                            mm(o, xh, wh, u == 0 and k == 0, False, t, b.free, a.tok[u * K + k])
                            mm(o, xh, wl, False, False)
                            last = mm(o, xl, wh, False, end, inc=(k == K - 1))
                        if u == parts - 1:
                            b.free = evac(i, c * cw, cw, o, last)
                    p.free = last
                    step(bg)
            return last

        class Squares:

            def __init__(self, nch):
                self.nch, self.n, self.todo = nch, 0, []

            def add(self, src, m, *toks):
                i = tmp_at[0] % 2
                tmp_at[0] += 1
                sq = TMP[:, i, 0:m * T].rearrange("p (c t) -> p c t", t=T)
                a = act(sq, src, ACT.Square, *toks, tmp_free[i])
                self.todo.append((i, sq, m, a))

            def flush(self):
                for i, sq, m, a in self.todo:
                    for k in range(m):
                        self.last = mm(norm_bank.ap[:, 0:T], con("ones"), sq[:, k, :], self.n == 0,
                                       self.n == self.nch - 1, a, norm_bank.free, inc=(k == m - 1))
                        self.n += 1
                    tmp_free[i] = self.last
                self.todo = []

        def tmp():
            i = tmp_at[0] % 2
            tmp_at[0] += 1
            return i, TMP[:, i, :].rearrange("p (c t) -> p c t", t=T)

        def rstd(last, dst, n, *war):
            a = act(dst, norm_bank.ap[:, 0:T], ACT.Sqrt, last, *war, bias=con("eps"), scale=1.0 / n)
            norm_bank.free = a
            recip(dst, dst, a)

        def sums(src, nch, toks):
            sq = Squares(nch)
            for c0 in range(0, nch, 4):
                m = min(4, nch - c0)
                sq.add(src[:, c0:c0 + m, :], m, toks if len(toks) < nch else toks[c0:c0 + m])
                yield
                sq.flush()
            return sq

        def rms_steps(src, nch, dst, gain, n, toks, war=None, d0=0):
            sq = yield from sums(src, nch, toks)
            r = rs_at[0] % 2
            rs_at[0] += 1
            R = RS[:, r, :]
            rstd(sq.last, R, n, rs_free[r])
            c0 = 0
            while c0 < nch:
                m = min(1 if c0 == 0 else 3 if c0 == 1 else 4, nch - c0)
                i, buf = tmp()
                for c in range(m):
                    t = stt(buf[:, c, :], src[:, c0 + c, :], gain(c0 + c), R, ALU.mult, ALU.mult, toks, tmp_free[i])
                rs_free[r] = t
                tmp_free[i] = dst.cut(buf[:, 0:m, :], d0 + c0, m, t, war)
                c0 += m
                yield

        def head_rstd(src, nch, per, n, toks, dst):
            rows = nch * per
            name, w = ("sel2", 30) if per == 2 else ("sel1", 3)
            sel = con(name)
            bk = score_banks.next()
            for c0 in range(0, nch, 4):
                i = tmp_at[0] % 2
                tmp_at[0] += 1
                sq = TMP[:, i, :].rearrange("p (c t) -> p c t", t=T)
                a = act(sq, src[:, c0:c0 + 4, :], ACT.Square, toks, tmp_free[i])
                for k in range(4):
                    c = c0 + k
                    p = mm(bk.ap[0:rows, 0:T], sel[:, w - per * c:w - per * c + rows], sq[:, k, :],
                           c == 0, c == nch - 1, a, bk.free, inc=(k == 3))
                tmp_free[i] = p
            a = act(dst, bk.ap[0:rows, 0:T], ACT.Sqrt, p, bias=con("eps")[0:rows, :], scale=1.0 / n)
            bk.free = a
            return recip(dst, dst, a)

        class Normed:

            def __init__(self, gain, war, a=None):
                self.a, self.gain, self.war = a or hs_act(), gain, war
                self.late, self.n, self.todo, self.free = [], 0, [], [list(tmp_free)] * 8

            def add(self, c, tok, m=1):
                for j in range(c, c + m):
                    hi = act(self.a.hi[:, j, :], X[:, j, :], ACT.Identity, tok, self.war, scale=vec(self.gain, j))
                    self.low()
                    self.late.append((j, hi))
                while len(self.todo) > 2 or sum(q[2] for q in self.todo) + m > 8:
                    self.flush()
                s = c % 8
                sq = TMP[:, s // 4, s % 4 * T:(s % 4 + m) * T].rearrange("p (c t) -> p c t", t=T)
                self.todo.append((s, sq, m, act(sq, X[:, c:c + m, :], ACT.Square, tok, self.free[s:s + m])))

            def flush(self):
                s, sq, m, a = self.todo.pop(0)
                for k in range(m):
                    self.n += 1
                    self.last = mm(norm_bank.ap[:, 0:T], con("ones"), sq[:, k, :], self.n == 1, self.n == 16, a,
                                   norm_bank.free, inc=(k == m - 1))
                for k in range(s, s + m):
                    self.free[k] = self.last

            def low(self):
                for c, hi in self.late:
                    self.a.tok[c] = stt(self.a.lo[:, c, :], X[:, c, :], vec(self.gain, c),
                                        self.a.hi[:, c, :].bitcast(F32), ALU.mult, ALU.subtract, hi, self.war)
                self.late = []

            def done(self):
                self.low()
                while self.todo:
                    self.flush()
                tmp_free[0] = tmp_free[1] = self.last
                rstd(self.last, RX, 2048, V.tok())
                return self.a

        xn = [None]

        def scaled(o, ps, *toks):
            return tt(o, ps, RX, ALU.mult, *toks)

        def columns(row, c0):
            for i in range(2):
                p = tr(tr_bank.ap[:, i * 128:i * 128 + 128], row[:, i * 128:i * 128 + 128], V.tok(), tr_bank.free,
                       inc=(i == 1))
            tr_bank.free = vcopy(SM[:, c0:c0 + 2], tr_bank.ap[:, 0:256:128], p)
            return tr_bank.free

        def residual(c, ps, tok):
            xt[c] = tt(X[:, c, :], X[:, c, :], ps, ALU.add, tok)
            xn[0].add(c, xt[c])
            return xt[c]

        def residual_only(c, ps, tok):
            xt[c] = tt(X[:, c, :], X[:, c, :], ps, ALU.add, tok)
            return xt[c]

        xt = [t_x[c // 4] for c in range(16)]

        def softmax_head(P, PT, den, score, scale, mask, causal, vl, o, otok, ahead=2):
            b = score_banks.next()
            t = score(b.ap, b.free)
            if mask is not None:
                v = stt(P.ap, b.ap, scale, mask, ALU.mult, ALU.add, t, P.free)
                b.free = v
                V(lambda e: e.tensor_reduce(den[:, 0:2], P.ap.rearrange("p (a k) -> p a k", a=2), AXX, ALU.max,
                                            negate=True))
                m = V.tok()
                for i in range(2):
                    a = act(P.ap[:, i * T:i * T + T], P.ap[:, i * T:i * T + T], ACT.Exp, m,
                            bias=den[:, i:i + 1], acc=den[:, 2 + i:3 + i])
            else:
                V(lambda e: e.tensor_reduce(den[:, 0:2], b.ap.rearrange("p (a k) -> p a k", a=2), AXX, ALU.max,
                                            negate=True), t)
                m = ts(den[:, 0:2], den[:, 0:2], scale, None, ALU.mult, None)
                for i in range(2):
                    a = act(P.ap[:, i * T:i * T + T], b.ap[:, i * T:i * T + T], ACT.Exp, m, P.free,
                            bias=den[:, i:i + 1], scale=scale, acc=den[:, 2 + i:3 + i])
                b.free = a
            yield
            recip(den[:, 4:6], den[:, 2:4], a)
            for i in range(2):
                n = 128 if causal and i == 0 else T
                v = ts(P.ap[:, i * T:i * T + n], P.ap[:, i * T:i * T + n], den[:, 4 + i:5 + i], None, ALU.mult, None)
            for _ in range(ahead - 1):
                yield
            blocks = [(0, 0), (1, 0), (1, 1)] if causal else [(0, 0), (1, 0), (0, 1), (1, 1)]
            for n, (i, k) in enumerate(blocks):
                t = tr(tr_bank.ap[:, n * 128:n * 128 + 128], P.ap[:, i * T + k * 128:i * T + k * 128 + 128],
                       v, tr_bank.free, inc=(n == len(blocks) - 1))
            P.free = t
            w = 128 * len(blocks)
            a = scopy(PT.ap[:, 0:w], tr_bank.ap[:, 0:w], t, PT.free)
            tr_bank.free = a
            yield
            lo, hi = o.base_partition() if callable(o.base_partition) else o.base_partition, o.shape[0]
            ob = out_bank.ap[lo:lo + hi, 0:T]
            mm(ob, vl(0), PT.ap[:, 0:T], True, False, a, out_bank.free, otok)
            if causal:
                t = mm(out_bank.ap[lo:lo + hi, 128:T], vl(1), PT.ap[:, T:T + 128], False, True, inc=True)
            else:
                t = mm(ob, vl(1), PT.ap[:, T:2 * T], False, True, inc=True)
            PT.free = t
            out_bank.free = scopy(o, ob, t)
            yield

        class Buf:
            def __init__(self, ap):
                self.ap, self.free = ap, None

        STREAM = [A[n][i] for n, c in ORDER for i in range(c)]
        h1 = Normed("g_mix", None)
        for _ in range(NRAW):
            load_unit()
        for _ in range(2):
            high_unit()
            low_unit()
            load_unit()
        for c in range(0, 16, 4):
            h1.add(c, t_x[c // 4], 4)
        h1 = h1.done()
        QT, KT = chunks(0, 8), chunks(2048, 8)
        QK = chunks(0, 16)
        VT = big(4096, 2048).rearrange("p (i d) -> p i d", i=2)
        Z = chunks(6144, 8)
        XBC = chunks(8192, 16)
        XST = big(12288, 2048).rearrange("p (i d) -> p i d", i=2)
        BT = big(14336, 512)

        t_posr = [None]
        t_cs = [None]

        def angles():
            t_mem[0] = MEMQ.fill(S, lambda e: e.dma_start(MEM, A["memT"]))
            POS = GT[:, :]
            t_posr[0] = vcopy(POS, POSI, t_pos)
            for j, ph in enumerate((0.25, 0.0)):
                ANG = CS1[:, j, :]
                KK = RS[:, 1, :]
                ts(ANG, POS, con("invf"), None, ALU.mult, None)
                ts(KK, ANG, float(np.float32(1 / (2 * np.pi))), ph, ALU.mult, ALU.add, rs_free[1])
                ts(KK, KK, 12582912.0, None, ALU.add, None)
                yield
                ts(KK, KK, 12582912.0, None, ALU.subtract, None)
                for cst in (6.28125, 0.0019340515136718750, 1.2556659146e-06):
                    stt(ANG, KK, -cst, ANG, ALU.mult, ALU.add)
                yield
                ts(ANG, ANG, float(np.float32(ph * 2 * np.pi)), float(np.float32(np.pi)), ALU.add, ALU.min)
                t = ts(ANG, ANG, float(-np.float32(np.pi)), None, ALU.max, None)
                rs_free[1] = t
                yield
            t_cs[0] = act(CS1[:, :, :], CS1[:, :, :], ACT.Sin, t)
            yield
            t_rv[0] = columns(RX, 289)
            yield

        t_rv, t_rm = [None], [None]

        qkt = [None] * 16

        def evac_qk(c, ps, tok):
            qkt[c] = scaled(QK[:, c, :], ps, tok, t_posr[0])
            return qkt[c]

        g_an = angles()
        next(g_an)
        dense(16, 8, 128, h1, evac_qk, g_an, parts=2)
        drain(g_an)

        qkr = [None] * 16

        def norm_rope():
            rb = SM[0:32, 0:T]
            t_r = head_rstd(QK, 16, 2, 64, [qkt[14], qkt[15]], rb)
            yield
            for c in range(16):
                b = score_banks.next()
                for j in range(2):
                    t = mm(b.ap[64 * j:64 * j + 64, 0:T], con("ident")[0:32, 2 * c + j:2 * c + j + 1].to_broadcast([32, 64]),
                           rb, True, True, t_r, b.free, inc=(j == 1))
                t = stt(QK[:, c, :], QK[:, c, :], vec("g_q" if c < 8 else "g_k"), b.ap[:, 0:T], ALU.mult, ALU.mult, t)
                b.free = t
                if c < 8:
                    t = ts(QK[:, c, :], QK[:, c, :], 0.125, None, ALU.mult, None)
                yield
                b = score_banks.next()
                p = mm(b.ap[:, 0:T], con("rot1"), QK[:, c, :], True, True, t, b.free, inc=True)
                rt = TMP[:, 1, 0:T]
                t = tt(rt, b.ap[:, 0:T], CS1[:, 1, :], ALU.mult, p, t_cs[0], tmp_free[1])
                b.free = t
                tt(QK[:, c, :], QK[:, c, :], CS1[:, 0, :], ALU.mult, p)
                qkr[c] = tt(QK[:, c, :], QK[:, c, :], rt, ALU.add)
                tmp_free[1] = qkr[c]
                yield

        def mem_sums():
            sq = yield from sums(MEM, 16, t_mem)
            rstd(sq.last, KEEP[:, 0, :], 2048)
            yield
            yield
            t_rm[0] = columns(KEEP[:, 0, :], 291)
            yield

        def before():
            yield from norm_rope()
            yield from mem_sums()

        g_nr = before()
        t_v = [None]

        def evac_v(i, c0, n, ps, tok):
            t_v[0] = act(VT[:, i, c0:c0 + n], ps, ACT.Identity, tok, t_rv[0], scale=SM[:, 289 + i:290 + i])
            return t_v[0]

        dense_tok(4, 4, 256, h1, evac_v, twice(g_nr), parts=4)

        AP_ = [Buf(big(o, 512)) for o in (12288, 14848, 15360, 15872)]
        APT = [Buf(TMP[:, 1, 512:896])]
        atok = [None] * 8

        def attn(h):
            c, lo = h // 2, 64 * (h % 2)
            q, k = QK[lo:lo + 64, c, :], QK[lo:lo + 64, 8 + c, :]

            def score(b, free):
                for i in range(2):
                    t = mm(b[:, i * T:i * T + T], q[:, i * 128:i * 128 + 128], k, True, True,
                           qkr[c], qkr[8 + c], free, inc=(i == 1))
                return t

            den = SM[:, 256 + 8 * (h % 4):264 + 8 * (h % 4)]
            yield from softmax_head(AP_[h % 4], APT[0], den, score, 1.0, con("mask"), True,
                                    lambda kt: VT[:, kt, h * 64:h * 64 + 64], q, t_v[0], 3)
            atok[c] = S.tok()

        DT = GT[0:16, :]
        t_dt = [None]

        def evac_dt(c, ps, tok):
            t = tt(DT, ps[0:16, :], RX[0:16, :], ALU.mult, tok)
            t_dt[0] = ts(DT, DT, vec("dt_bias")[0:16, :], None, ALU.add, None)
            return t

        dense(1, 8, 128, h1, evac_dt, g_nr, parts=2)
        t_zs = [None] * 8
        t_xbc = [None] * 16

        CK = chunks(2048, 4)
        CV = big(3072, 1024).rearrange("p (i d) -> p i d", i=2)

        def log1p_exp(x, m, y, z, p, tok):
            ts(m, x, 0.0, None, ALU.max, None, tok)
            ts(y, x, -1.0, None, ALU.mult, None)
            t = tt(y, x, y, ALU.min)
            t = act(y, y, ACT.Exp, t)
            ts(z, y, 2.0, None, ALU.add, None, t)
            recip(z, z)
            tt(y, y, z, ALU.mult)
            tt(z, y, y, ALU.mult)
            ts(p, z, 1.0 / 17, None, ALU.mult, None)
            for d in (15, 13, 11, 9, 7, 5, 3):
                stt(p, p, 1.0 / d, z, ALU.add, ALU.mult)
            stt(p, p, 1.0, y, ALU.add, ALU.mult)
            return stt(x, p, 2.0, m, ALU.mult, ALU.add)

        DA = SM[0:16, 0:T]
        ACS = KEEP[0:16, 1, :]
        ACT_ = SM[:, 320:352].rearrange("p (i h) -> p i h", i=2)
        DTT = SM[:, 352:384].rearrange("p (i h) -> p i h", i=2)
        SSB = 14848
        CB = big(SSB, 256).rearrange("p (i l) -> p i l", i=2)
        EE = [big(SSB + 256 + 256 * i, 256) for i in range(2)]
        WW = [Buf(big(SSB + 768 + 256 * i, 256)) for i in range(2)]
        ECS = [Buf(big(SSB + 1280, 128)), Buf(big(SSB + 1408, 128)), Buf(SM[:, 0:128])]
        XW = Buf(SM[:, 384:448])
        PV = Buf(SM[:, 448:512])
        sst = [None] * 8

        def ssd_pre():
            xx = [TMP[0:16, i, j * T:j * T + T] for i in range(2) for j in range(2)]
            V.wait([tmp_free[0], tmp_free[1]])
            t = tmp_free[0] = tmp_free[1] = log1p_exp(DT, *xx, t_dt[0])
            yield
            yield
            al = SM[0:16, 288:289]
            a = act(al, vec("a_log")[0:16, :], ACT.Exp, t)
            ts(DA, DT, al, -1.0, ALU.mult, ALU.mult, a)
            for i in range(2):
                V(lambda e, i=i: e.tensor_tensor_scan(ACS[:, i * 128:i * 128 + 128], con("ones")[0:16, :],
                                                      DA[:, i * 128:i * 128 + 128], 0.0, ALU.mult, ALU.add))
            t = V.tok()
            yield
            yield
            for src, dst in ((ACS, ACT_), (DT, DTT)):
                for i in range(2):
                    p = tr(tr_bank.ap[:, i * 16:i * 16 + 16], src[:, i * 128:i * 128 + 128], t, tr_bank.free,
                           inc=(i == 1))
                u = vcopy(dst, tr_bank.ap[:, 0:32].rearrange("p (i h) -> p i h", i=2), p)
                tr_bank.free = u
                yield
            t_acs[0] = t

        def ssd_b():
            while t_xbc[11] is None:
                yield
            yield
            for g in range(4):
                p = tr(tr_bank.ap[:, g * 128:g * 128 + 128], XBC[:, 8 + g, 0:128], t_xbc[11], tr_bank.free, inc=(g == 3))
            tr_bank.free = t_bt[0] = vcopy(BT, tr_bank.ap[:, :], p)
            yield

        def ssd_x(c0):
            while t_xbc[c0] is None or t_xbc[15] is None:
                yield
            yield
            for i in range(2):
                for c in range(c0, c0 + 4):
                    p = tr(tr_bank.ap[:, (c - c0) * 128:(c - c0) * 128 + 128], XBC[:, c, i * 128:i * 128 + 128],
                           t_xbc[c], tr_bank.free, inc=(c == c0 + 3))
                tr_bank.free = t_xst[0] = vcopy(XST[:, i, c0 * 128:c0 * 128 + 512], tr_bank.ap[:, :], p)
                yield

        t_acs, t_bt, t_xst = [None], [None], [None]
        cbt = [None]

        def ssd_head(h):
            g, c, lo = h // 4, h // 2, 64 * (h % 2)
            Bg, Cg = XBC[:, 8 + g, :], XBC[:, 12 + g, :]
            if h % 4 == 0:
                sb_ = score_banks.next()
                for i in range(2):
                    p = mm(sb_.ap[:, i * 128:i * 128 + 128], Bg[:, i * 128:i * 128 + 128],
                           Cg[:, i * 128:i * 128 + 128], True, True, sb_.free, t_xbc[8 + g], t_xbc[12 + g], inc=(i == 1))
                sb_.free = cbt[0] = tt(CB, sb_.ap[:, 0:T].rearrange("p (i l) -> p i l", i=2),
                                       con("triu").unsqueeze(1).to_broadcast([128, 2, 128]), ALU.mult, p)
            k, ecs = h % 2, ECS[h % 3]
            sb_ = score_banks.next()
            p = mm(sb_.ap[:, 0:T], con("ident")[0:16, h:h + 1].to_broadcast([16, 128]), ACS, True, True,
                   sb_.free, t_acs[0], inc=True)
            E_ = EE[k]
            for i in range(2):
                t = ts(E_[:, i * 128:i * 128 + 128], sb_.ap[:, i * 128:i * 128 + 128], ACT_[:, i, h:h + 1], 0.0,
                       ALU.subtract, ALU.min, p)
            a = act(ecs.ap, sb_.ap[:, 128:T], ACT.Exp, t, ecs.free)
            sb_.free = a
            a = act(E_, E_, ACT.Exp, t)
            yield
            t_xw = ts(XW.ap, XST[:, 0, h * 64:h * 64 + 64], E_[:, 127:128], DTT[:, 0, h:h + 1], ALU.mult, ALU.mult, a,
                      XW.free, t_xst[0])
            for i in range(2):
                t = stt(WW[k].ap[:, i * 128:i * 128 + 128], E_[:, i * 128:i * 128 + 128], DTT[:, i, h:h + 1],
                        CB[:, i, :], ALU.mult, ALU.mult, WW[k].free)
            t = tt(ecs.ap, ecs.ap, Cg[:, 128:T], ALU.mult, t_xbc[12 + g])
            yield
            p = mm(tr_bank.ap[:, 0:64], BT[:, g * 128:g * 128 + 128], XW.ap, True, True, t_xw, t_bt[0], tr_bank.free, inc=True)
            XW.free = p
            a = scopy(PV.ap, tr_bank.ap[:, 0:64], p, PV.free)
            tr_bank.free = a
            yield
            ob = out_bank.ap[lo:lo + 64, 0:T]
            xs = XST[:, :, h * 64:h * 64 + 64]
            mm(ob[:, 0:128], xs[:, 0, :], WW[k].ap[:, 0:128], True, True, t, t_xst[0], out_bank.free)
            mm(ob[:, 128:T], xs[:, 1, :], WW[k].ap[:, 128:T], True, False)
            p = mm(ob[:, 128:T], PV.ap, ecs.ap, False, True, a, inc=True)
            WW[k].free = ecs.free = PV.free = p
            y = XBC[lo:lo + 64, c, :]
            t = stt(y, y, vec("d_skip", c)[lo:lo + 64, :], ob, ALU.mult, ALU.add, p)
            out_bank.free = t
            sst[c] = tt(Z[lo:lo + 64, c, :], Z[lo:lo + 64, c, :], y, ALU.mult, t_zs[c])
            yield

        def head_norm(src, toks, g):
            rb = SM[0:4, 0:T]
            t_r = head_rstd(src, 4, 1, 128, toks, rb)
            yield
            for c in range(4):
                b = score_banks.next()
                t = mm(b.ap[:, 0:T], con("ident")[0:4, c:c + 1].to_broadcast([4, 128]), rb, True, True, t_r, b.free,
                       inc=True)
                b.free = stt(src[:, c, :], src[:, c, :], vec(g), b.ap[:, 0:T], ALU.mult, ALU.mult, t)
                yield

        t_attn, t_memcut, ckt = [None], [None], [None] * 4
        mxa = Act(bigr(4096, 8), bigr(0, 8))
        mxs = Act(bigr(16384, 8), bigr(18432, 8))

        def mixers():
            yield from g_nr
            yield from ssd_pre()
            APT[0].free = [tmp_free[0], tmp_free[1]]
            yield from pipeline(attn(h) for h in range(16))
            tmp_free[1] = [tmp_free[1], APT[0].free]
            t_attn[0] = [PE.tok(), S.tok()]
            yield from rms_steps(QT, 8, mxa, lambda c: vec("g_attn", c), 1024, t_attn, t_attn)
            yield from ssd_b()
            yield from ssd_x(0)
            yield from pipeline(ssd_head(h) for h in range(8))
            yield from ssd_x(4)
            while t_memcut[0] is None:
                yield
            yield from pipeline([ssm_norm(0), *(ssd_head(h) for h in range(8, 12)), ssm_norm(1),
                                 *(ssd_head(h) for h in range(12, 16)), ssm_norm(2)])
            yield from ssm_norm(3)

        t_ckn = [None]

        def ssm_norm(g):
            yield from rms_steps(Z[:, 2 * g:2 * g + 2, :], 2, mxs, lambda c: vec("g_ssm", 2 * g + c), 256,
                                 [sst[2 * g + 1]], t_memcut, d0=2 * g)

        g_bg = mixers()

        def evac_z(c, ps, tok):
            t = scaled(Z[:, c, :], ps, tok)
            if c % 4 == 3:
                z = act(Z[:, c - 3:c + 1, :], Z[:, c - 3:c + 1, :], ACT.Silu, t)
                for j in range(c - 3, c + 1):
                    t_zs[j] = z
            return t

        dense(8, 8, 128, h1, evac_z, g_bg, parts=2)


        def conv(dst, ps, w, b, tok):
            t_ps = scaled(CX, ps, tok)
            t = ts(dst, CX, w(3), b, ALU.mult, ALU.add)
            for j in (1, 2, 3):
                t = stt(dst[:, j:T], CX[:, 0:T - j], w(3 - j), dst[:, j:T], ALU.mult, ALU.add)
            return t_ps, t

        def evac_xbc(n, ps, tok):
            c = (n + 8) % 16
            t_ps, t = conv(XBC[:, c, :], ps, lambda j: vec("conv_w", 4 * c + j), vec("conv_b", c), tok)
            if c % 4 == 3 and c != 7:
                silu(c - 3, t)
            elif c == 7:
                t_conv[0] = t
            return t_ps

        t_conv = [None]

        def silu(c, t):
            a = act(XBC[:, c:c + 4, :], XBC[:, c:c + 4, :], ACT.Silu, t)
            for j in range(c, c + 4):
                t_xbc[j] = a

        t_hfree = dense(16, 8, 128, h1, evac_xbc, g_bg, parts=2)

        mh = hs_act()
        late = []
        for c in range(17):
            if c < 16:
                late.append(act(mh.hi[:, c, :], MEM[:, c, :], ACT.Identity, t_mem, t_hfree, scale=vec("g_mem", c)))
            if c:
                mh.tok[c - 1] = stt(mh.lo[:, c - 1, :], MEM[:, c - 1, :], vec("g_mem", c - 1),
                                    mh.hi[:, c - 1, :].bitcast(F32), ALU.mult, ALU.subtract, late[c - 1], t_hfree)
        silu(4, t_conv[0])
        t_memcut[0] = V.tok()
        assert t_attn[0] is not None

        def evac_ck(c, ps, tok):
            ckt[c] = tt(CK[:, c, :], ps, KEEP[:, 0, :], ALU.mult, tok, t_attn[0])
            return ckt[c]

        dense(4, 8, 128, mh, evac_ck, twice(g_bg), parts=2)
        t_cv = [None]

        def evac_cv(i, c0, n, ps, tok):
            t_cv[0] = act(CV[:, i, c0:c0 + n], ps, ACT.Identity, tok, t_rm[0], scale=SM[:, 291 + i:292 + i])
            return t_cv[0]

        t_hfree = dense_tok(2, 4, 256, mh, evac_cv, twice(g_bg), parts=4)
        drain(g_bg)

        xn[0] = Normed("g_cross", t_hfree)
        g_ck = head_norm(CK, ckt, "g_ck")
        t_mx = dense(16, 8, 128, [mxa, mxs], residual, g_ck, parts=2)
        drain(g_ck)
        t_ckn[0] = V.tok()
        hc = xn[0].done()
        CQ = chunks(0, 4)
        cqt = [None]

        def evac_cq(c, ps, tok):
            cqt[0] = scaled(CQ[:, c, :], ps, tok)
            return cqt[0]

        t_hfree = dense(4, 8, 128, hc, evac_cq, parts=2)
        drain(head_norm(CQ, [cqt[0]], "g_cq"))
        t_cqn = V.tok()
        CP = [Buf(big(4096 + 512 * i, 512)) for i in range(3)]
        CPT = Buf(big(5632, 512))
        cot = [None] * 4

        def cross(h):
            def score(b, free):
                for i in range(2):
                    t = mm(b[:, i * T:i * T + T], CQ[:, h, i * 128:i * 128 + 128], CK[:, h, :], True, True,
                           t_cqn, t_ckn[0], free, inc=(i == 1))
                return t

            den = SM[:, 256 + 8 * (h % 4):264 + 8 * (h % 4)]
            yield from softmax_head(CP[h % 3], CPT, den, score, 128.0 ** -0.5, None, False,
                                    lambda kt: CV[:, kt, h * 128:h * 128 + 128], CQ[:, h, :], t_cv[0])
            cot[h] = S.tok()

        drain(pipeline(cross(h) for h in range(4)))
        cx = Act(bigr(8192, 4), bigr(9216, 4))
        for c in range(4):
            cx.cut(CQ[:, c:c + 1, :], c, 1, cot[c], t_mx)
        xn[0] = Normed("g_mlp", t_hfree)
        dense(8, 4, 256, cx, residual)
        hm = xn[0].done()
        hid = Act(bigr(0, 32), bigr(8192, 32))
        t_cfree = [PE.tok(), V.tok(), S.tok()]

        def evac_up(c, ps, tok):
            i, buf = tmp()
            t = stt(buf[:, 0, :], ps, 0.0, RX, ALU.max, ALU.mult, tok, tmp_free[i])
            a = act(buf[:, 1, :], buf[:, 0, :], ACT.Square, t)
            tmp_free[i] = hid.cut(buf[:, 1:2, :], c, 1, a, t_cfree)
            return t

        for half in range(2):
            t_hfree = dense(32, 8, 128, hm, evac_up, parts=2)
            ev = residual_only
            if half:
                ev = residual
                xn[0] = Normed("attn_norm", t_hfree)
            dense(16, 8, 128, hid, ev, parts=4)

        XR, YR = chunks(0, 16), chunks(4096, 16)
        CKV, KR, C_Q = chunks(8192, 4), chunks(9216, 1), chunks(9472, 6)
        GR, GA_ = chunks(11008, 16), chunks(15104, 16)
        WRG = big(13568, 4096)
        t_bfree = PE.tok()
        t_rg = Slot(WRG, sem("s_rg")).fill(SP, lambda e: e.dma_start(WRG, A["w_rg"]), t_bfree)
        TRIG = Slot(CS1[:, :, :], sem("s_trig"))
        t_trig = TRIG.fill(SP, lambda e: e.dma_start(CS1[:, :, :], A["trig2"]), qkr[15])
        MASK = Slot(con("mask"), sem("s_mask"))
        t_mask = MASK.fill(SP, lambda e: e.dma_start(con("mask"), A["mask2"]), atok[7])
        hn = xn[0].done()
        NSP = SM[:, 256:272]
        sp = [SM[:, 272 + 16 * i:288 + 16 * i] for i in range(4)]
        t = ts(NSP, vec("lam", 0, 16), -1.0, None, ALU.mult, None)
        log1p_exp(NSP, *sp, t)
        ts(NSP, NSP, -8.0, None, ALU.mult, None)
        c2t = {}
        LOW = BIG[:, 8192:8192 + 11 * T].rearrange("p (c t) -> p c t", t=T)

        def evac_low(c, ps, tok):
            c2t[c] = scaled(LOW[:, c, :], ps, tok, t_bfree)
            return c2t[c]

        dense(11, 8, 128, hn, evac_low, parts=2)
        xrt = [None] * 16
        ytk = [None] * 16

        def evac_xr(c, ps, tok):
            V.wait([t_bfree])
            t_ps, xrt[c] = conv(XR[:, c, :], ps, lambda j: vec("conv_w2", 4 * c + j), vec("conv_b2", c), tok)
            return t_ps

        RA = BIG[:, 17664:18688].rearrange("p (c t) -> p c t", t=T)
        RI = BIG[:, 18688:19712].rearrange("p (c t) -> p c t", t=T)
        RM = TMP[:, 0, :].rearrange("p (c t) -> p c t", t=T)

        def rglru():
            t_prev = None
            for c0 in range(0, 16, 4):
                while xrt[c0 + 3] is None:
                    yield
                yield
                for j in range(4):
                    c = c0 + j
                    bk = score_banks.next()
                    mm(bk.ap[:, 0:T], WRG[:, c * 128:c * 128 + 128], XR[:, c, :], True, True, t_rg, xrt[c], bk.free)
                    p = mm(bk.ap[:, T:2 * T], WRG[:, 2048 + c * 128:2048 + c * 128 + 128], XR[:, c, :], True, True,
                           inc=True)
                    a = act(RA[:, j, :], bk.ap[:, 0:T], ACT.Sigmoid, p, t_prev, bias=vec("b_a", c))
                    a = act(RI[:, j, :], bk.ap[:, T:2 * T], ACT.Sigmoid, p, bias=vec("b_x", c))
                    bk.free = a
                    yield
                    t = ts(RA[:, j, :], RA[:, j, :], NSP[:, c:c + 1], None, ALU.mult, None, a)
                t = tt(RI, RI, XR[:, c0:c0 + 4, :], ALU.mult)
                a = act(RM, RA, ACT.Tanh, t, tmp_free[0], scale=-1.0)
                a = act(RA, RA, ACT.Exp, t)
                yield
                sq = TMP[:, 1, :].rearrange("p (c t) -> p c t", t=T)
                tt(sq, RA, RA, ALU.mult, a, tmp_free[1])
                t = tmp_free[1] = stt(RM, sq, 1.0, RM, ALU.add, ALU.mult)
                a = act(RM, RM, ACT.Sqrt, t)
                yield
                V(lambda e: e.memset(RM[:, :, 0:1], 1.0), a)
                t = tt(RI, RI, RM, ALU.mult)
                tmp_free[0] = t
                for j in range(4):
                    V(lambda e, j=j, c=c0 + j: e.tensor_tensor_scan(XR[:, c, :], RA[:, j, :], RI[:, j, :], 0.0,
                                                                   ALU.mult, ALU.add), p)
                    t_prev = ytk[c0 + j] = V.tok()
                yield

        g_rg = rglru()
        dense(16, 8, 128, hn, evac_xr, g_rg, parts=2)
        ym = [None] * 16

        def evac_yr(c, ps, tok):
            v = scaled(YR[:, c, :], ps, tok, t_bfree)
            if c % 4 == 3:
                while ytk[c] is None:
                    next(g_rg)
                a = act(YR[:, c - 3:c + 1, :], YR[:, c - 3:c + 1, :], ACT.Gelu_apprx_tanh, v)
                t = tt(YR[:, c - 3:c + 1, :], YR[:, c - 3:c + 1, :], XR[:, c - 3:c + 1, :], ALU.mult, a, ytk[c])
                for j in range(c - 3, c + 1):
                    ym[j] = t
            return v

        dense(16, 8, 128, hn, evac_yr, g_rg, parts=2)
        t_wrg = PE.tok()

        def evac_gate(G_, o):
            def evac(c, ps, tok):
                t = scaled(G_[:, c, :], ps, tok, t_wrg, ym[15])
                gtok[o + c] = act(G_[:, c, :], G_[:, c, :], ACT.Sigmoid, t, bias=vec("b_gate", o + c))
                return t
            return evac

        gtok = {}

        dense(16, 8, 128, hn, evac_gate(GR, 16), parts=2)
        t_hfree = dense(16, 8, 128, hn, evac_gate(GA_, 0), parts=2)
        ys = hs_act()
        for c in range(0, 16, 4):
            ys.cut(YR[:, c:c + 4, :], c, 4, ym[c], t_hfree)
        t_yfree = V.tok()

        def rope2(buf, tok):
            bk = score_banks.next()
            p = mm(bk.ap[:, 0:T], con("rot2"), buf, True, True, tok, bk.free, inc=True)
            rt = TMP[:, 1, 0:T]
            t = tt(rt, bk.ap[:, 0:T], CS1[:, 1, :], ALU.mult, p, tmp_free[1], t_trig)
            bk.free = t
            tt(buf, buf, CS1[:, 0, :], ALU.mult, p)
            t = tt(buf, buf, rt, ALU.add)
            tmp_free[1] = t
            return t

        cqs = Act(bigr(4096, 6), bigr(4096 + 6 * T, 6))
        cks = Act(bigr(4096 + 12 * T, 4), bigr(9472, 4))
        t_kr = [None]

        def low_norms():
            yield from rms_steps(C_Q, 6, cqs, lambda c: vec("q_norm", c), 768, [c2t[10]], t_yfree)
            yield from rms_steps(CKV, 4, cks, lambda c: vec("kv_norm", c), 512, [c2t[10]], V.tok())
            t_kr[0] = rope2(KR[:, 0, :], c2t[10])

        xo = [None]

        def evac_yo(c, ps, tok):
            xo[0] = tt(XR[:, c, :], GR[:, c, :], ps, ALU.mult, tok, gtok[16 + c])
            return xo[0]

        g_low = low_norms()
        t_yo = dense(16, 8, 128, ys, evac_yo, g_low, parts=2)
        drain(g_low)
        QN = GR
        QP = HF[:, 0, 0:2048].rearrange("p (c t) -> p c t", t=T)
        K2 = HF[:, :, :].rearrange("p a b -> p (a b)")[:, 2048:6144].rearrange("p (c t) -> p c t", t=T)
        V2 = [HF[:, 1, 2048:4096], big(4096, 2048)]
        qt2 = {}
        qpt = [None] * 8

        def evac_uq(c, ps, tok):
            if c < 16:
                qt2[c] = scopy(QN[:, c, :], ps, tok, xo[0])
                return qt2[c]
            qt2[c] = scopy(QP[:, c - 16, :], ps, tok, t_yo)
            return qt2[c]

        t_uq = dense(24, 6, 128, cqs, evac_uq)
        k2t = {}

        def evac_k2(c, ps, tok):
            if c % 2 == 0:
                qpt[c // 2] = rope2(QP[:, c // 2, :], qt2[16 + c // 2])
            k2t[c] = scopy(K2[:, c, :], ps, tok, t_yo)
            return k2t[c]

        dense(8, 4, 256, cks, evac_k2)
        v2t = [None]

        def evac_v2(i, c0, n, ps, tok):
            v2t[0] = scopy(V2[i][:, c0:c0 + n], ps, tok, t_yo, t_uq)
            return v2t[0]

        dense_tok(8, 4, 256, cks, evac_v2)
        MP = [Buf(big(6144, 512)), Buf(big(6656, 512)), Buf(big(7168, 512))]
        t_ckfree = PE.tok()
        MPT = Buf(TMP[:, 0, 0:384])
        mot = [None] * 16

        def mla(h):
            lo = 64 * (h % 2)

            def score(b, free):
                for i in range(2):
                    mm(b[:, i * T:i * T + T], QN[:, h, i * 128:i * 128 + 128], K2[:, h, :], True, False,
                       qt2[h], k2t[h], free, v2t[0])
                    t = mm(b[:, i * T:i * T + T], QP[lo:lo + 64, h // 2, i * 128:i * 128 + 128],
                           KR[lo:lo + 64, 0, :], False, True, qpt[h // 2], t_kr[0], inc=(i == 1))
                return t

            if h < 3:
                MP[h].free = t_ckfree
                V.wait([t_mask])
            if h == 0:
                MPT.free = tmp_free[0]
            den = SM[:, 256 + 8 * (h % 4):264 + 8 * (h % 4)]
            yield from softmax_head(MP[h % 3], MPT, den, score, 192.0 ** -0.5, con("mask"), True,
                                    lambda kt: V2[kt][:, h * 128:h * 128 + 128], QN[:, h, :], v2t[0])
            mot[h] = S.tok()

        g_ml = pipeline(mla(h) for h in range(16))
        drain(g_ml)
        tmp_free[0] = MPT.free
        t_hfree = PE.tok()
        os_ = hs_act()
        for c in range(0, 16, 4):
            os_.cut(QN[:, c:c + 4, :], c, 4, mot[c + 3], t_hfree)
        mix = Act(bigr(4096, 16), bigr(8192, 16))
        t_qnfree = V.tok()

        def evac_ao(c, ps, tok):
            t = tt(GA_[:, c, :], GA_[:, c, :], ps, ALU.mult, tok, gtok[c])
            tt(XR[:, c, :], XR[:, c, :], GA_[:, c, :], ALU.add)
            mix.cut(XR[:, c:c + 1, :], c, 1, V.tok(), t_qnfree)
            return t

        dense(16, 8, 128, os_, evac_ao, parts=2)
        xn[0] = Normed("ffn_norm", PE.tok())
        dense(16, 8, 128, mix, residual, parts=2)
        t_bfree = PE.tok()
        HN = big(0, 4096).rearrange("p (i d) -> p i d", i=2)
        SC = big(4096, 4096).rearrange("p (i c n) -> p i c n", i=2, c=16)
        ACC = HF[:, 1, :].rearrange("p (i d) -> p i d", i=2)
        PQ = chunks(8192, 8)
        SK = big(10240, 2048)
        HK = chunks(14336, 16)
        t_sk = Slot(SK, sem("s_sk")).fill(SP, lambda e: e.dma_start(SK, A["subkeys"]), t_bfree, V.tok())
        hp = xn[0].done()
        t_mixfree = V.tok()
        pqt = [None] * 16
        sct = [[None] * 8, [None] * 8]
        t_sc = [None] * 8
        t_hn = [None, None]

        def evac_pq(c, ps, tok):
            pqt[c] = scaled(PQ[:, c % 8, :], ps, tok, t_bfree, t_sc[c // 2 - 4] if c >= 8 else None)
            return pqt[c]

        gs = Ring([Slot(big(12288 + 2048 * i, 2048), sem(f"s_r{i}")) for i in range(4)])

        def rows():
            for c in range(16):
                t_hk = stt(HK[:, c, :], X[:, c, :], vec("ffn_norm", c), RX, ALU.mult, ALU.mult, t_bfree)
                if c % 4 == 3:
                    yield
            for i in range(2):
                for c0 in range(0, 16, 4):
                    for c in range(c0, c0 + 4):
                        p = tr(tr_bank.ap[:, (c - c0) * 128:(c - c0) * 128 + 128], HK[:, c, i * 128:i * 128 + 128],
                               tr_bank.free, t_hk, inc=(c == c0 + 3))
                    tr_bank.free = t_hn[i] = scopy(HN[:, i, c0 * 128:c0 * 128 + 512], tr_bank.ap, p, t_mixfree)
                    if c0 % 8:
                        yield
            for s in gs.items:
                s.free = [p, t_mixfree]
            rowed[0] = True

        def scoring():
            for h in range(8):
                while pqt[2 * h + 1] is None:
                    yield
                bk = score_banks.next()
                for i in range(2):
                    for c in (2 * h, 2 * h + 1):
                        o = i * 256 + c % 2 * 128
                        t_sc[h] = mm(bk.ap[:, o:o + 128], PQ[:, c % 8, i * 128:i * 128 + 128],
                                     SK[:, c * 128:c * 128 + 128], True, True, pqt[c], t_sk, bk.free,
                                     inc=(i == 1 and c % 2 == 1))
                bk.free = scopy(SC[:, :, 2 * h:2 * h + 2, :], bk.ap.rearrange("p (i c n) -> p i c n", i=2, c=2),
                                t_sc[h], t_mixfree)
                sct[0][h] = sct[1][h] = bk.free
                yield

        RT = TMP[:, 0, :]
        TOPV = RT[:, 0:32].rearrange("p (c k) -> p c k", k=16)
        TOPI = RT[:, 32:64].bitcast(U32).rearrange("p (c k) -> p c k", k=16)
        TOPF = RT[:, 64:96].rearrange("p (c k) -> p c k", k=16)
        BV, BI = RT[:, 96:112], RT[:, 112:128].bitcast(U32)
        PI, PF, I12 = RT[:, 128:160].bitcast(U32), RT[:, 160:192], RT[:, 192:224]
        CAND, EQ = RT[:, 256:512], RT[:, 512:1024].rearrange("p (k j) -> p k j", j=16)
        EX = CS1[:, 0, :].bitcast(U32).rearrange("p (i k) -> p i k", i=2)
        GA = sb("GA", [128, 2, 128])
        DOT = CS1[:, 1, :].rearrange("p (i k) -> p i k", i=2)
        ext = [[None] * 8, [None] * 8]

        def top16(vals, v16, i16):
            V(lambda e: e.max(v16[:, 0:8], vals))
            V(lambda e: e.max_index(i16[:, 0:8], v16[:, 0:8], vals))
            yield
            V(lambda e: e.match_replace(vals, v16[:, 0:8], vals, -3e38))
            V(lambda e: e.max(v16[:, 8:16], vals))
            V(lambda e: e.max_index(i16[:, 8:16], v16[:, 8:16], vals))
            yield

        def route(i, h):
            while sct[i][h] is None:
                yield
            V.wait([sct[i][h], tmp_free[0]])
            for half in range(2):
                yield from top16(SC[:, i, 2 * h + half, :], TOPV[:, half, :], TOPI[:, half, :])
            vcopy(TOPF, TOPI)
            tt(CAND.rearrange("p (a b) -> p a b", a=16), TOPV[:, 0, :].unsqueeze(2).to_broadcast([128, 16, 16]),
               TOPV[:, 1, :].unsqueeze(1).to_broadcast([128, 16, 16]), ALU.add)
            yield
            yield from top16(CAND, BV, BI)
            ts(PI[:, 0:16], BI, 4, None, ALU.logical_shift_right, None)
            ts(PI[:, 16:32], BI, 15, None, ALU.bitwise_and, None)
            vcopy(PF, PI)
            yield
            tt(EQ, con("iota").unsqueeze(1).to_broadcast([128, 32, 16]), PF.unsqueeze(2).to_broadcast([128, 32, 16]),
               ALU.is_equal)
            yield
            tt(EQ.rearrange("p (a k) j -> p a k j", a=2), EQ.rearrange("p (a k) j -> p a k j", a=2),
               TOPF.unsqueeze(2).to_broadcast([128, 2, 16, 16]), ALU.mult)
            yield
            V(lambda e: e.tensor_reduce(I12, EQ, AXX, ALU.add))
            yield
            stt(I12[:, 0:16], I12[:, 0:16], 128.0, I12[:, 16:32], ALU.mult, ALU.add)
            ts(GA[:, i, 16 * h:16 * h + 16], BV, BV[:, 0:1], None, ALU.subtract, None)
            ext[i][h] = vcopy(EX[:, i, 16 * h:16 * h + 16], I12[:, 0:16])

        def gather(table, i, k):
            s = gs.next()
            t = s.fill(G, lambda e, s=s: e.indirect_dma_start(
                out=s.ap, out_offset=None, in_=table,
                in_offset=bass.IndirectOffsetOnAxis(ap=EX[:, i, k:k + 1], axis=0)), ext[i][k // 16])
            return s, t

        def dot(i, k):
            s, t = gather(A["peer_u"], i, k)
            s.free = V(lambda e: e.tensor_tensor_reduce(
                s.ap, s.ap, HN[:, i, :], 1.0, 0.0, ALU.mult, ALU.add, DOT[:, i, k:k + 1]), t, t_hn[i])

        acct = [None, None]
        late, rowed = [False], [False]

        def values(i, h, t):
            g, d, den = part(i, h)
            stt(g, g, den[:, 1:2], d, ALU.mult, ALU.mult, t)
            for k in range(16 * h, 16 * h + 16):
                s, t = gather(A["peer_v"], i, k)
                if k == 0:
                    t = ts(ACC[:, i, :], s.ap, GA[:, i, 0:1], None, ALU.mult, None, t, t_hfree)
                else:
                    t = stt(ACC[:, i, :], s.ap, GA[:, i, k:k + 1], ACC[:, i, :], ALU.mult, ALU.add, t)
                s.free = acct[i] = t
                yield

        def part(i, h):
            n = 384 + 2 * (8 * i + h)
            return GA[:, i, 16 * h:16 * h + 16], DOT[:, i, 16 * h:16 * h + 16], SM[:, n:n + 2]

        def experts():
            work = [(i, h) for h in range(8) for i in range(2)]
            routes, ready = chain(work), []
            while not rowed[0]:
                yield
            for i, h in work:
                while ext[i][h] is None:
                    if sct[i][h] is None:
                        yield
                    else:
                        step(routes)
                g, d, den = part(i, h)
                a = act(g, g, ACT.Exp, ext[i][h], acc=den[:, 0:1])
                for k in range(16):
                    dot(i, 16 * h + k)
                    if not late[0] or k % 2 or k == 0:
                        step(routes)
                    yield
                t = act(d, d, ACT.Gelu_apprx_tanh, V.tok())
                while late[0] and ready:
                    for n, _ in enumerate(values(*ready.pop(0))):
                        if n % 2:
                            step(routes)
                        yield
                recip(den[:, 1:2], den[:, 0:1], a)
                ready.append((i, h, t))
            for head in ready:
                yield from values(*head)

        def chain(work):
            for i, h in work:
                yield from route(i, h)

        g_row, g_sc, g_ex = rows(), scoring(), experts()

        def beside():
            while True:
                step(g_row)
                step(g_row)
                step(g_sc)
                step(g_ex)
                yield

        t_hfree = dense(16, 8, 128, hp, evac_pq, beside(), parts=2)
        drain(g_sc)
        t_pqfree = [PE.tok(), S.tok()]
        late[0] = True
        gs.items.append(Slot(HF[:, 0, 0:2048], sem("s_r4")))
        gs.items[-1].free = t_hfree

        PTF = HF[:, 0, 3072:3584].rearrange("p (c t) -> p c t", t=T)
        PRJ = chunks(8192, 16)
        t_p = Slot(PTF, sem("s_p")).fill(SP, lambda e: e.dma_start(PTF, A["pT"]), t_hfree)

        def evac_pr(c, ps, tok):
            return scopy(PRJ[:, c, :], ps, tok, t_pqfree)

        def projection():
            pin = Act(HS[:, 0, 2048:2560].rearrange("p (c t) -> p c t", t=T),
                      HS[:, 0, 2560:3072].rearrange("p (c t) -> p c t", t=T))
            pin.cut(PTF, 0, 2, t_p, t_hfree)
            dense(4, 2, 512, pin, evac_pr)

        for n, _ in enumerate(g_ex):
            if n == 10:
                projection()
        xn[0] = Normed("ple_norm", [PE.tok(), V.tok()], Act(HS[:, 0, :].rearrange("p (c t) -> p c t", t=T), bigr(4096, 16)))
        for c0 in range(0, 16, 2):
            bk = score_banks.next()
            for c in range(c0, c0 + 2):
                for i in range(2):
                    p = tr(bk.ap[:, (c - c0) * T + i * 128:(c - c0) * T + i * 128 + 128],
                           ACC[:, i, c * 128:c * 128 + 128], bk.free, acct[i], inc=(c == c0 + 1 and i == 1))
            t = tt(X[:, c0:c0 + 2, :], X[:, c0:c0 + 2, :], bk.ap.rearrange("p (c t) -> p c t", t=T), ALU.add, p)
            xt[c0] = xt[c0 + 1] = bk.free = t
            xn[0].add(c0, t, 2)
        hg = xn[0].done()

        def evac_pg(c, ps, tok):
            t = scaled(GT[:, :], ps, tok)
            a = act(GT[:, :], GT[:, :], ACT.Sigmoid, t)
            tt(PRJ[:, c, :], PRJ[:, c, :], GT[:, :], ALU.mult, a)
            xt[c] = tt(X[:, c, :], X[:, c, :], PRJ[:, c, :], ALU.add)
            sq.flush()
            sq.add(X[:, c:c + 1, :], 1, xt[c])
            return t

        sq = Squares(16)
        dense(16, 8, 128, hg, evac_pg, parts=2)
        assert taken[0] == len(STREAM)
        sq.flush()
        a = act(RS[:, 0, :], norm_bank.ap[:, 0:T], ACT.Sqrt, sq.last, rs_free[0], bias=con("eps"), scale=1.0 / 2048)
        recip(RS[:, 0, :], RS[:, 0, :], a)
        OUT = chunks(0, 16)
        outs = []
        so = [Slot(None, sem(f"s_out{i}")) for i in range(4)]
        for c in range(16):
            t = stt(OUT[:, c, :], X[:, c, :], vec("final_norm", c), RS[:, 0, :], ALU.mult, ALU.mult, V.tok())
            if c % 4 == 3:
                outs.append(so[c // 4].fill(SP, lambda e, c=c: e.dma_start(out[:, c - 3:c + 1, :],
                                                                          OUT[:, c - 3:c + 1, :]), t))
        SP.wait(outs)

        block = ctx.enter_context(nc.Block())

        @block.sync
        def _(e):
            SP.play(e)

        @block.gpsimd
        def _(e):
            G.play(e)

        @block.scalar
        def _(e):
            S.play(e)

        @block.vector
        def _(e):
            V.play(e)

        @block.tensor
        def _(e):
            PE.play(e)


def constants():
    p = np.arange(128)
    t = np.arange(256)
    c = {}
    c["ident"] = np.eye(128)
    c["ones"] = np.ones((128, 128))
    r1 = np.zeros((128, 128))
    r2 = np.zeros((128, 128))
    for h in range(2):
        for j in range(8):
            r1[64 * h + 8 + j, 64 * h + j] = -1
            r1[64 * h + j, 64 * h + 8 + j] = 1
        for j in range(32):
            r2[64 * h + 32 + j, 64 * h + j] = -1
            r2[64 * h + j, 64 * h + 32 + j] = 1
    c["rot1"], c["rot2"] = r1, r2
    c["triu"] = (p[None, :] >= p[:, None])
    s2 = np.zeros((128, 62))
    s2[p, 30 + p // 64] = 1
    s1 = np.zeros((128, 7))
    s1[:, 3] = 1
    c["sel2"], c["sel1"] = s2, s1
    q = p[:, None, None] + 128 * np.arange(2)[None, :, None]
    d = q - t[None, None, :]
    m = ((d >= 0) & (d <= 128)).astype(int) + ((d >= 0) & (d % 4 == 0)) + ((d >= 0) & (d % 16 == 0))
    c["mask"] = np.where(m > 0, np.log(np.maximum(m, 1)), NEG).reshape(128, 512)
    c["iota"] = np.broadcast_to(np.arange(16), (128, 16))
    f = (np.float32(500000.0) ** (np.float32(-2.0) * np.arange(8, dtype=np.float32) / np.float32(16))).astype(np.float32)
    c["invf"] = np.where(p % 64 < 16, f[p % 8], 0).reshape(128, 1)
    c["eps"] = np.full((128, 1), EPS)
    return np.concatenate([np.asarray(c[n], np.float32).reshape(128, k) for n, k in CONSTS], axis=1)


def constants2():
    p, t = np.arange(128), np.arange(256)
    d = p[:, None, None] + 128 * np.arange(2)[None, :, None] - t[None, None, :]
    inv = (1.0 / (np.float32(10000.0) ** (np.arange(32, dtype=np.float32) / np.float32(32)))).astype(np.float32)
    ang = (t.astype(np.float32)[None, :] * inv[p % 32][:, None]).astype(np.float32).astype(np.float64)
    trig = np.stack([np.cos(ang), np.sin(ang)], axis=1).astype(np.float32)
    return trig, np.where(d >= 0, 0.0, NEG).reshape(128, 512).astype(np.float32)


def kernel(**inp):
    import concourse.bacc as _bacc
    from concourse.bass_utils import run_bass_kernel_spmd as _run

    a = {k: np.asarray(v) for k, v in inp.items()}

    def fm(v):
        return v.reshape(-1, 128).T

    def blocks(w, cw):
        k, n = w.shape
        return np.ascontiguousarray(w.reshape(k // 128, 128, n // cw, cw).transpose(2, 1, 0, 3)
                                    .reshape(n // cw, 128, k // 128 * cw))

    def units(w):
        k, n = w.shape
        return np.ascontiguousarray(w.reshape(k // 1024, 8, 128, n // 128, 128).transpose(3, 0, 2, 1, 4)
                                    .reshape(n // 128 * (k // 1024), 128, 1024))

    def actT(x):
        t, d = x.shape
        return np.ascontiguousarray(x.T.reshape(d // 128, 128, t).transpose(1, 0, 2))

    def units4(w):
        k, n = w.shape
        return np.ascontiguousarray(w.reshape(k // 512, 4, 128, n // 256, 256).transpose(3, 0, 2, 1, 4)
                                    .reshape(n // 256 * (k // 512), 128, 1024))

    w = a["w_in"][0]
    w2 = a["w_in_2"][0]
    ar = {
        "xT": actT(a["x"][0]), "memT": actT(a["mem"][0]), "positions": np.ascontiguousarray(a["positions"][0]),
        "pT": actT(a["p_2"][0, 0]), "consts": constants(),
        "w_qk": units(w[:, 0:2048]), "w_v": units4(w[:, 2048:3072]), "w_z": units(w[:, 3072:4096]),
        "w_xbc": units(np.concatenate([w[:, 5120:6144], w[:, 4096:5120]], axis=1)),
        "w_dt": units(np.concatenate([w[:, 6144:6160], np.zeros((2048, 112), np.float32)], axis=1)),
        "w_out": units(a["w_out"][0]), "w_cq": units(a["w_cq"][0]),
        "w_ck": units(a["w_ckv"][0][:, 0:512]), "w_cv": units4(a["w_ckv"][0][:, 512:1024]),
        "w_co": blocks(a["w_co"][0], 256),
    }
    ar["trig2"], ar["mask2"] = constants2()
    for h in range(2):
        ar[f"w_up{h}"] = units(a["w_up"][0][:, 4096 * h:4096 * h + 4096])
        ar[f"w_down{h}"] = units(a["w_down"][0][4096 * h:4096 * h + 4096])
    low = np.concatenate([w2[:, 768:1280], w2[:, 1280:1344], w2[:, 1280:1344], w2[:, 0:768]], axis=1)
    ar["w2_low"] = units(low)
    for n, o in (("xr", 1344), ("yr", 3392), ("ga", 5440), ("gr", 7488)):
        ar["w2_" + n] = units(w2[:, o:o + 2048])
    uq = a["w_uq_2"][0].reshape(768, 16, 192)
    ar["w2_uq"] = blocks(np.concatenate([uq[:, :, 0:128].reshape(768, 2048), uq[:, :, 128:].reshape(768, 1024)], 1), 128)
    ukv = a["w_ukv_2"][0].reshape(512, 16, 256)
    ar["w2_uk"] = blocks(ukv[:, :, 0:128].reshape(512, 2048), 256)
    ar["w2_uv"] = blocks(ukv[:, :, 128:].reshape(512, 2048), 256)
    ar["w_rg"] = np.ascontiguousarray(np.concatenate(
        [a[n][0].transpose(1, 0, 2).reshape(128, 2048) for n in ("w_rg_a_2", "w_rg_x_2")], axis=1))
    for n, s in (("rnn_o", "w_rnn_o_2"), ("ao", "w_attn_o_2"), ("out", "w_out_2"), ("pg", "w_ple_gate_2")):
        ar["w2_" + n] = units(a[s][0])
    ar["w2_pp"] = blocks(a["w_ple_proj_2"][0], 512)
    ar["w_pq"] = units(a["w_peer_q_2"][0])
    ar["subkeys"] = np.ascontiguousarray(a["peer_subkeys_2"][0].reshape(16, 128, 128).transpose(2, 0, 1).reshape(128, 2048))
    ar["peer_u"] = a["peer_u_2"][0]
    ar["peer_v"] = a["peer_v_2"][0]

    def pad(v):
        o = np.zeros((128, 1), np.float32)
        o[0:16, 0] = v
        return o

    vec = {
        "g_mix": fm(a["g_mix"]), "g_cross": fm(a["g_cross"]), "g_mem": fm(a["g_mem"]), "g_mlp": fm(a["g_mlp"]),
        "attn_norm": fm(a["attn_norm_2"]), "ffn_norm": fm(a["ffn_norm_2"]), "ple_norm": fm(a["ple_norm_2"]),
        "final_norm": fm(a["final_norm_2"]), "g_q": np.tile(a["g_q"][0], 2).reshape(128, 1),
        "g_k": np.tile(a["g_k"][0], 2).reshape(128, 1), "g_attn": fm(a["g_attn_out"]), "g_ssm": fm(a["g_ssm_out"]),
        "conv_w": a["conv_w"][0].reshape(4, 16, 128).transpose(2, 1, 0).reshape(128, 64), "conv_b": fm(a["conv_b"]),
        "d_skip": fm(np.repeat(a["d_skip"][0], 64)), "g_cq": a["g_cq"].T, "g_ck": a["g_ck"].T,
        "q_norm": fm(a["q_norm_2"]), "kv_norm": fm(a["kv_norm_2"]), "b_gate": fm(a["b_gate_2"]),
        "conv_w2": a["conv_w_2"][0].reshape(4, 16, 128).transpose(2, 1, 0).reshape(128, 64), "conv_b2": fm(a["conv_b_2"]),
        "b_a": fm(a["b_rg_a_2"]), "b_x": fm(a["b_rg_x_2"]), "lam": fm(a["lru_lambda_2"]),
        "dt_bias": pad(a["dt_bias"][0]), "a_log": pad(a["a_log"][0]),
    }
    ar["vecs"] = np.ascontiguousarray(np.concatenate([vec[n].reshape(128, k) for n, k in VECS], axis=1))

    nc = _bacc.Bacc("TRN2", target_bir_lowering=False, num_devices=1)
    arrays, ap = {}, {}
    for n, v in ar.items():
        arrays["in_" + n] = v
        ap[n] = nc.dram_tensor("in_" + n, v.shape, mybir.dt.from_np(v.dtype), kind="ExternalInput").ap()
    out = nc.dram_tensor("out_0", (128, 16, 256), F32, kind="ExternalOutput").ap()
    build(nc, ap, out)
    r = _run(nc, [arrays], core_ids=[0])
    got = r.results[0]["out_0"]
    return np.ascontiguousarray(got.transpose(2, 1, 0)).reshape(1, 256, 2048)
```
